# Optimizing a Trainium2 kernel written in Bass

```python
import math
import jax, jax.numpy as jnp
from jax import lax
import numpy as np

D_MODEL = 1024
BATCH = 1
SEQ = 1024
DEPTH = 1
DEC_BATCH = 8
DEC_SEQ = 4
PAST_LEN = 512
PAGE_SIZE = 128

N_META = 16
MIX_WIDTH = D_MODEL
POOL_WIDTH = MIX_WIDTH // 2
POOL_WINDOWS = (2, 4, 8, 16)
POOL_GROUP = POOL_WIDTH // len(POOL_WINDOWS)
POOL_HIST = max(POOL_WINDOWS) - 1
ATTN_WIDTH = MIX_WIDTH - POOL_WIDTH
HEAD_DIM = 64
N_HEADS = ATTN_WIDTH // HEAD_DIM
SB_BLOCK = 128
SB_BIAS_HI = -2.0
SB_BIAS_LO = -9.0
N_GROUPS = 4
EXPERTS_PER_GROUP = 8
N_EXPERTS = N_GROUPS * EXPERTS_PER_GROUP
TOP_K = 2
D_EXPERT = D_MODEL // 2
MOE_BLOCK = 64
EPS = 1e-6

kernel_name = 'hymba_pool_stickbreak_hmoe_step'

def rms_norm(x, g):
    xf = x.astype(jnp.float32)
    y = xf * lax.rsqrt(jnp.mean(xf * xf, axis=-1, keepdims=True) + EPS)
    return (y * g.astype(jnp.float32)).astype(x.dtype)

def mixer_projections(x, norm_g, w_in, g_q, g_k):
    B, T = x.shape[:2]
    n = rms_norm(x, norm_g)
    proj = jnp.einsum('btd,de->bte', n, w_in)
    u, q, k, v = jnp.split(proj, [POOL_WIDTH, POOL_WIDTH + ATTN_WIDTH, POOL_WIDTH + 2 * ATTN_WIDTH], axis=-1)
    heads = lambda a: a.reshape(B, T, N_HEADS, HEAD_DIM)
    q = rms_norm(heads(q), g_q)
    k = rms_norm(heads(k), g_k)
    return u, q, k, heads(v)

def pool_mixer(u, hist, p0, w_pool, pool_scale):
    T = u.shape[1]
    ext = jnp.concatenate([hist.astype(u.dtype), u], axis=1).astype(jnp.float32)
    cs = jnp.concatenate([jnp.zeros_like(ext[:, :1]), jnp.cumsum(ext, axis=1)], axis=1)
    pos = p0 + jnp.arange(T)
    outs = []
    for g, w in enumerate(POOL_WINDOWS):
        sl = slice(g * POOL_GROUP, (g + 1) * POOL_GROUP)
        win_sum = cs[:, POOL_HIST + 1:POOL_HIST + 1 + T, sl] - cs[:, POOL_HIST + 1 - w:POOL_HIST + 1 - w + T, sl]
        count = jnp.minimum(w, pos + 1).astype(jnp.float32)
        d = win_sum / count[None, :, None] - ext[:, POOL_HIST:, sl]
        outs.append(jnp.einsum('btc,ce->bte', d, w_pool[g].astype(jnp.float32)))
    y = jnp.concatenate(outs, axis=-1) * pool_scale.astype(jnp.float32)
    return y.astype(u.dtype), ext[:, -POOL_HIST:].astype(u.dtype)

def stick_breaking(q, k, v, q_pos, k_pos, sb_bias):
    z = jnp.einsum('bqhd,bkhd->bhqk', q, k).astype(jnp.float32) * (HEAD_DIM ** -0.5)
    z = z + sb_bias.astype(jnp.float32)[None, :, None, None]
    visible = k_pos[None, :] < q_pos[:, None]
    log_beta = jax.nn.log_sigmoid(z)
    log_keep = jnp.where(visible, jax.nn.log_sigmoid(-z), 0.0)
    later = lax.cumsum(log_keep, axis=3, reverse=True) - log_keep
    a = jnp.where(visible, jnp.exp(log_beta + later), 0.0)
    return jnp.einsum('bhqk,bkhd->bqhd', a.astype(v.dtype), v)

def stick_breaking_prompt(q, k, v, sb_bias):
    B, L = q.shape[:2]
    lead = (-N_META) % SB_BLOCK
    nb = -(-(L + lead) // SB_BLOCK)
    tail = nb * SB_BLOCK - L - lead
    qp = jnp.pad(q, ((0, 0), (lead, tail), (0, 0), (0, 0)))
    k_pos = jnp.arange(L)

    def block(b):
        qb = lax.dynamic_slice_in_dim(qp, b * SB_BLOCK, SB_BLOCK, axis=1)
        q_pos = b * SB_BLOCK - lead + jnp.arange(SB_BLOCK)
        return stick_breaking(qb, k, v, q_pos, k_pos, sb_bias)

    o = lax.map(block, jnp.arange(nb))
    o = jnp.moveaxis(o, 0, 1).reshape(B, nb * SB_BLOCK, N_HEADS, HEAD_DIM)
    return o[:, lead:lead + L]

def merge_heads(pool_o, attn, w_out):
    B, T = pool_o.shape[:2]
    cat = jnp.concatenate([pool_o, attn.reshape(B, T, ATTN_WIDTH)], axis=-1)
    return jnp.einsum('bte,ed->btd', cat, w_out)

def hier_moe(h, w_group, w_expert, w_gate, w_up, w_down):
    T, D = h.shape
    hf = h.astype(jnp.float32)
    p_group = jax.nn.softmax(hf @ w_group.astype(jnp.float32), axis=-1)
    g_sel = jnp.argmax(p_group, axis=-1)
    g_w = jnp.take_along_axis(p_group, g_sel[:, None], axis=-1)[:, 0]
    logits_e = (hf @ w_expert.astype(jnp.float32)).reshape(T, N_GROUPS, EXPERTS_PER_GROUP)
    le = jnp.take_along_axis(logits_e, g_sel[:, None, None], axis=1)[:, 0]
    top_v, top_i = lax.top_k(le, TOP_K)
    gate = g_w[:, None] * jax.nn.softmax(top_v, axis=-1)
    expert_id = (g_sel[:, None] * EXPERTS_PER_GROUP + top_i).astype(jnp.int32)
    M = T * TOP_K
    e_flat = expert_id.reshape(M)
    tok = jnp.repeat(jnp.arange(T, dtype=jnp.int32), TOP_K)
    wt = gate.reshape(M)
    order = jnp.argsort(e_flat)
    e_s = e_flat[order]
    counts = jnp.bincount(e_flat, length=N_EXPERTS)
    padded = (counts + MOE_BLOCK - 1) // MOE_BLOCK * MOE_BLOCK
    pad_end = jnp.cumsum(padded)
    pad_start = pad_end - padded
    start = jnp.cumsum(counts) - counts
    dest = pad_start[e_s] + jnp.arange(M) - start[e_s]
    P = (-(-M // MOE_BLOCK) + N_EXPERTS) * MOE_BLOCK
    nblk = P // MOE_BLOCK
    row_tok = jnp.full((P,), T, jnp.int32).at[dest].set(tok[order])
    row_w = jnp.zeros((P,), h.dtype).at[dest].set(wt[order].astype(h.dtype))
    blk_exp = jnp.clip(jnp.searchsorted(pad_end, jnp.arange(nblk) * MOE_BLOCK, side='right'), 0, N_EXPERTS - 1)
    h_pad = jnp.concatenate([h, jnp.zeros((1, D), h.dtype)], axis=0)
    xs = h_pad[row_tok].reshape(nblk, MOE_BLOCK, D)

    def expert_block(args):
        xb, e = args
        return (jax.nn.silu(xb @ w_gate[e]) * (xb @ w_up[e])) @ w_down[e]

    ys = lax.map(expert_block, (xs, blk_exp)).reshape(P, D)
    out = jax.ops.segment_sum(ys * row_w[:, None], row_tok, num_segments=T + 1)[:T]
    return out.astype(h.dtype)

def channel_mixer(x, norm_g, w_group, w_expert, w_gate, w_up, w_down):
    B, T, D = x.shape
    n = rms_norm(x, norm_g).reshape(B * T, D)
    return x + hier_moe(n, w_group, w_expert, w_gate, w_up, w_down).reshape(B, T, D)

def setup_inputs(seed: int = 0) -> dict:
    key = jax.random.key(seed)
    ks = jax.random.split(key, 24)
    f32 = jnp.float32
    n_pages = PAST_LEN // PAGE_SIZE
    n_used = DEC_BATCH * n_pages
    n_phys = n_used + n_used // 4
    nrm = lambda k, shape, s: jax.random.normal(k, shape, f32) * s
    page_table = jax.random.permutation(ks[5], n_phys)[:n_used].reshape(DEC_BATCH, n_pages).astype(jnp.int32)
    sb_bias = jnp.broadcast_to(jnp.linspace(SB_BIAS_HI, SB_BIAS_LO, N_HEADS, dtype=f32), (DEPTH, N_HEADS)) + nrm(ks[20], (DEPTH, N_HEADS), 0.05)
    return {
        'x_prompt': nrm(ks[0], (BATCH, SEQ, D_MODEL), 1.0),
        'x_sample': nrm(ks[1], (DEC_BATCH, DEC_SEQ, D_MODEL), 1.0),
        'cache_k': nrm(ks[2], (DEPTH, n_phys, PAGE_SIZE, N_HEADS, HEAD_DIM), 1.0),
        'cache_v': nrm(ks[3], (DEPTH, n_phys, PAGE_SIZE, N_HEADS, HEAD_DIM), 1.0),
        'state_pool': nrm(ks[4], (DEPTH, DEC_BATCH, POOL_HIST, POOL_WIDTH), 1.0),
        'page_table': page_table,
        'meta_tokens': nrm(ks[6], (N_META, D_MODEL), 1.0),
        'norm_mix': 1.0 + nrm(ks[7], (DEPTH, D_MODEL), 0.02),
        'w_in': nrm(ks[8], (DEPTH, D_MODEL, POOL_WIDTH + 3 * ATTN_WIDTH), D_MODEL ** -0.5),
        'g_q': 1.0 + nrm(ks[9], (DEPTH, HEAD_DIM), 0.02),
        'g_k': 1.0 + nrm(ks[10], (DEPTH, HEAD_DIM), 0.02),
        'sb_bias': sb_bias,
        'w_pool': nrm(ks[11], (DEPTH, len(POOL_WINDOWS), POOL_GROUP, POOL_GROUP), POOL_GROUP ** -0.5),
        'pool_scale': 1.0 + nrm(ks[12], (DEPTH, POOL_WIDTH), 0.02),
        'w_out': nrm(ks[13], (DEPTH, MIX_WIDTH, D_MODEL), MIX_WIDTH ** -0.5),
        'norm_ffn': 1.0 + nrm(ks[14], (DEPTH, D_MODEL), 0.02),
        'w_group': nrm(ks[15], (DEPTH, D_MODEL, N_GROUPS), D_MODEL ** -0.5),
        'w_expert': nrm(ks[16], (DEPTH, D_MODEL, N_EXPERTS), D_MODEL ** -0.5),
        'w_gate': nrm(ks[17], (DEPTH, N_EXPERTS, D_MODEL, D_EXPERT), D_MODEL ** -0.5),
        'w_up': nrm(ks[18], (DEPTH, N_EXPERTS, D_MODEL, D_EXPERT), D_MODEL ** -0.5),
        'w_down': nrm(ks[19], (DEPTH, N_EXPERTS, D_EXPERT, D_MODEL), D_EXPERT ** -0.5),
    }

def reference(x_prompt, x_sample, cache_k, cache_v, state_pool, page_table, meta_tokens,
              norm_mix, w_in, g_q, g_k, sb_bias, w_pool, pool_scale, w_out, norm_ffn,
              w_group, w_expert, w_gate, w_up, w_down):
    B = x_prompt.shape[0]
    DB, Ts = x_sample.shape[:2]
    past = page_table.shape[1] * PAGE_SIZE
    meta = jnp.broadcast_to(meta_tokens[None].astype(x_prompt.dtype), (B, N_META, D_MODEL))
    xp = jnp.concatenate([meta, x_prompt], axis=1)
    xs = x_sample
    kp_l, vp_l, pp_l, ks_l, vs_l, ps_l = [], [], [], [], [], []
    for l in range(DEPTH):
        u, q, k, v = mixer_projections(xp, norm_mix[l], w_in[l], g_q[l], g_k[l])
        pool_o, pool_tail = pool_mixer(u, jnp.zeros((B, POOL_HIST, POOL_WIDTH), u.dtype), 0, w_pool[l], pool_scale[l])
        attn = stick_breaking_prompt(q, k, v, sb_bias[l])
        xp = xp + merge_heads(pool_o, attn, w_out[l])
        xp = channel_mixer(xp, norm_ffn[l], w_group[l], w_expert[l], w_gate[l], w_up[l], w_down[l])
        kp_l.append(k)
        vp_l.append(v)
        pp_l.append(pool_tail)
        u, q, k, v = mixer_projections(xs, norm_mix[l], w_in[l], g_q[l], g_k[l])
        pool_o, pool_tail = pool_mixer(u, state_pool[l], PAST_LEN, w_pool[l], pool_scale[l])
        past_k = cache_k[l][page_table].reshape(DB, past, N_HEADS, HEAD_DIM).astype(k.dtype)
        past_v = cache_v[l][page_table].reshape(DB, past, N_HEADS, HEAD_DIM).astype(v.dtype)
        k_all = jnp.concatenate([past_k, k], axis=1)
        v_all = jnp.concatenate([past_v, v], axis=1)
        attn = stick_breaking(q, k_all, v_all, past + jnp.arange(Ts), jnp.arange(past + Ts), sb_bias[l])
        xs = xs + merge_heads(pool_o, attn, w_out[l])
        xs = channel_mixer(xs, norm_ffn[l], w_group[l], w_expert[l], w_gate[l], w_up[l], w_down[l])
        ks_l.append(k)
        vs_l.append(v)
        ps_l.append(pool_tail)
    y_prompt = xp[:, N_META:]
    y_sample = xs
    k_prompt = jnp.stack(kp_l)
    v_prompt = jnp.stack(vp_l)
    pool_prompt = jnp.stack(pp_l)
    k_sample = jnp.stack(ks_l)
    v_sample = jnp.stack(vs_l)
    pool_sample = jnp.stack(ps_l)
    return (y_prompt, y_sample, k_prompt, v_prompt, pool_prompt, k_sample, v_sample, pool_sample)


_drawn_inputs = setup_inputs


def setup_inputs(seed=0):
    import zlib

    import numpy as np

    out = dict(_drawn_inputs(seed))
    spreads = {}
    factors = {'g_q': 23.775, 'pool_scale': 2.938, 'norm_ffn': 3.341}
    for name, (base, spread) in spreads.items():
        noise = np.random.default_rng([zlib.crc32(name.encode()), seed]).standard_normal(out[name].shape)
        drawn = base * np.exp(spread * noise) if base else spread * noise
        out[name] = __import__('jax').numpy.asarray(drawn.astype(out[name].dtype))
    for name, factor in factors.items():
        out[name] = (out[name] * factor).astype(out[name].dtype)
    return out
```

```python
import math

import concourse.bass as bass
from concourse import mybir

F32 = mybir.dt.float32
F32R = mybir.dt.float32r
I32 = mybir.dt.int32
U32 = mybir.dt.uint32
ACT = mybir.ActivationFunctionType
ALU = mybir.AluOpType
AXX = mybir.AxisListType.X

P = 128
D = 1024
KT = D // P
SEQ, META = 1024, 16
TP = SEQ + META
DB, DS = 8, 4
TS = DB * DS
T = TP + TS
NT = -(-T // P)
ROWS = [min(P, T - P * t) for t in range(NT)]
LAST = NT - 1
TAILP = TP - P * LAST
H, HD = 8, 64
HP = H // 2
PW = 512
AW = H * HD
WINDOWS = (2, 4, 8, 16)
NG = len(WINDOWS)
HIST = 15
PAST, PAGE = 512, 128
NPG = PAST // PAGE
EPS = 1e-6
CG = 256
NK = TP
TAIL_Q = 32
NKS = PAST + ROWS[-1]
PIECES = [(0, 512), (512, 512), (1024, T - 1024)]
NE, NGRP, EPG = 32, 4, 8
F = D // 2
FT = F // P
CAP = 96
OVB = 2 * T // CAP
NBLK = NE + OVB
NCOL = NBLK + 2
OVMAX = -(-T // CAP) - 1
NY = T + CAP
NCONST = 4


def row0(t):
    return P * t


class Chain:

    def __init__(self, eng, sem):
        self.eng, self.sem, self.n = eng, sem, 0

    def done(self, ins):
        self.n += 1
        ins.then_inc(self.sem, 1)
        return self.n

    def settle(self):
        self.eng.wait_ge(self.sem, self.n)

    def link(self, ins):
        self.done(ins)
        self.settle()


def hybrid_step(nc, x_prompt, x_sample, cache_k, cache_v, state_pool, page_table, meta_tokens,
                norm_mix, w_in, g_q, g_k, sb_bias, w_pool, pool_scale, w_out, norm_ffn,
                w_group, w_expert, w_gate, w_up, w_down,
                y_all, k_all, v_all, pool_p, pool_s):
    base = 16512
    end = 229344

    def place(name, shape, dtype, at):
        size = 4
        for n in shape[1:]:
            size *= n
        size = -(-size // 32) * 32
        assert base <= at and at + size <= end, (name, at, size, end)
        return nc.alloc_sbuf_tensor_at(name, shape, dtype, offset=at), at + size

    at_x = base
    xh, at = place("xh", [P, KT, T], F32R, at_x)
    xl, at_w = place("xl", [P, KT, T], F32R, at)
    w_raw, w_hi, w_lo = [], [], []
    at = at_w
    for i in range(2):
        for lst, nm, dt in ((w_raw, "w_raw", F32), (w_hi, "w_hi", F32R), (w_lo, "w_lo", F32R)):
            tns, at = place(f"{nm}{i}", [P, KT, CG], dt, at)
            lst.append(tns)
    at_q = at
    qT, at = place("qT", [P, HP, T], F32, at_q)
    kT, at = place("kT", [P, HP, T], F32, at)
    junk, _ = place("junk", [P, D], F32, at)
    vv, at_m = place("vv", [P, NT, AW], F32, at)
    xt = []
    at = at_m
    for i in range(3):
        tns, at = place(f"xt{i}", [P, D], F32, at)
        xt.append(tns)
    gmix, at = place("gmix", [P, D], F32, at)
    NKN = 3
    sq, kn = [], []
    for i in range(2):
        tns, at = place(f"sq{i}", [P, CG], F32, at)
        sq.append(tns)
    for i in range(NKN):
        tns, at = place(f"kn{i}", [P, CG], F32, at)
        kn.append(tns)
    ss, at = place("ss", [P, 2], F32, at)
    rs, at = place("rs", [P, 2], F32, at)
    hs, at = place("hs", [P, 2, 4], F32, at)
    hr, at = place("hr", [P, 2, 4], F32, at)
    at_c = at
    ident, at = place("ident", [P, P], F32, at_c)
    gq_bc, at = place("gq_bc", [P, HD], F32, at)
    gk_bc, at = place("gk_bc", [P, HD], F32, at)
    bias_bc, at = place("bias_bc", [P, H], F32, at)
    bias_tail, at = place("bias_tail", [P, 2], F32, at)
    bias_smp, at = place("bias_smp", [P, 1], F32, at)
    diag_mask, at = place("diag_mask", [P, P], F32, at)
    tail_mask, at = place("tail_mask", [P, TAILP], F32, at)
    smp_mask, at = place("smp_mask", [P, 2, ROWS[-1]], F32, at)
    wp_sb, at = place("wp_sb", [P, NG, P], F32, at)
    pscale, at = place("pscale", [P, NG], F32, at)
    rcnt, at = place("rcnt", [P, 16], F32, at)
    pint, at = place("pint", [P, 4], I32, at)
    pflt, at = place("pflt", [P, 8], F32, at)
    col48, at = place("col48", [P, ROWS[-1]], F32, at)
    hist, at = place("hist", [P, PW], F32, at)
    up_rows, at = place("up_rows", [TAILP, PW], F32, at)
    us_rows, at = place("us_rows", [TS, PW], F32, at)
    us_cols, at = place("us_cols", [P, NG, TS], F32, at)
    pt_sb, at = place("pt_sb", [1, DB * NPG], I32, at)
    at_u = at
    u_ext, at = place("u_ext", [P, NG, 16 + TP], F32, at_m)
    es, at = place("es", [P, NG, DB, 20], F32, at)
    assert at <= at_c
    dT, at = place("dT", [P, T], F32, at_w)
    wsum = []
    for i in range(2):
        tns, at = place(f"wsum{i}", [P, 16 + TP], F32, at)
        wsum.append(tns)
    wsmall0, at = place("wsmall0", [P, DB, 20], F32, at)
    wsmall1, at = place("wsmall1", [P, DB, 20], F32, at)
    sg, am, pb, aT = [], [], [], []
    at = at_w
    kp, at = place("kp", [P, NK], F32, at)
    for i in range(2):
        for lst, nm, shape in ((sg, "sg", [P, NK]), (am, "am", [P, NK]), (pb, "pb", [P, NK + 1]),
                               (aT, "aT", [P, NT, P])):
            tns, at = place(f"{nm}{i}", shape, F32, at)
            lst.append(tns)
    o_sb, at = place("o_sb", [P, AW], F32, at)
    assert at <= at_q, (at, at_q)
    pg = []
    at = at_m
    for i in range(2):
        tns, at = place(f"pg{i}", [PAGE, NPG, AW], F32, at)
        pg.append(tns)
    qz, at = place("qz", [P, DB, HP, 32], F32, at)
    assert at <= at_c
    kTs, at_end = place("kTs", [P, HP, PAST], F32, at_u)
    xmid, at_e = place("xmid", [P, NT, D], F32, at_q)
    wg, wu, wd = [], [], []
    for i, at in enumerate((at_w, at_x)):
        for lst, nm, shape in ((wg, "wg", [P, KT, F]), (wu, "wu", [P, KT, F]), (wd, "wd", [P, FT, D])):
            tns, at = place(f"{nm}{i}", shape, F32, at)
            lst.append(tns)
    at_r = at
    xg, xTe, hT, sgl, yo, gidx, sidx, gcol = [], [], [], [], [], [], [], []
    at, starts = at_e, {}
    for i in range(2):
        for lst, nm, shape, dt in ((xg, "xg", [P, D], F32), (xTe, "xTe", [P, KT, CAP], F32), (hT, "hT", [P, FT, CAP], F32),
                                   (sgl, "sgl", [P, FT, CAP], F32), (yo, "yo", [CAP, D], F32), (gidx, "gidx", [CAP, 1], I32),
                                   (sidx, "sidx", [CAP, 1], I32), (gcol, "gcol", [CAP, 1], F32)):
            starts[f"{nm}{i}"] = at
            tns, at = place(f"{nm}{i}", shape, dt, at)
            lst.append(tns)
    zrow, at = place("zrow", [CAP, D], F32, at)
    assert at <= at_c, (at, at_c)
    gffn, at = place("gffn", [P, D], F32, at_u)
    nT = [place(f"nT{i}", [P, KT, P], F32, starts[f"yo{i}"])[0] for i in range(2)]
    junk2, at = place("junk2", [P, D], F32, starts["xTe0"])
    assert at <= starts["yo0"]
    row_oh, at = place("row_oh", [P, NT, 2, CAP], F32, at_u)
    col_oh, at = place("col_oh", [P, NT, 2, 2 * NCOL], F32, starts["xTe0"])
    assert at <= starts["xg1"]
    small = {}
    at = at_r
    for nm, shape, dt in (("w_r", [P, KT, NGRP + NE], F32), ("lg", [P, NT, NGRP + NE], F32),
                          ("gmx", [P, NT], F32), ("goh", [P, NT, NGRP], F32), ("gex", [P, NT, NGRP], F32),
                          ("gw", [P, NT], F32), ("le", [P, NT, EPG], F32), ("tmp8", [P, NT, EPG], F32),
                          ("oh", [P, 2, NT, EPG], F32), ("mx", [P, 2, NT], F32), ("gt", [P, 2, NT], F32),
                          ("ek", [P, 2, NT, NE], F32), ("eb", [P, NT, NE], F32), ("cum", [P, NT, NE], F32),
                          ("rk", [P, 2, NT], F32), ("eid", [P, 2, NT], F32), ("ovs", [P, 2, NT], F32),
                          ("bk", [P, 2, NT], F32), ("rw", [P, 2, NT], F32), ("cl", [P, 2, NT], F32),
                          ("cnt", [P, NE], F32), ("nov", [P, NE], F32), ("ovend", [P, NE], F32), ("ovst", [P, NE], F32),
                          ("tab", [CAP, NCOL], I32), ("tabf", [CAP, NCOL], F32), ("vld", [CAP, NCOL], F32),
                          ("gtab", [CAP, NCOL], F32), ("valid", [P, NT], F32), ("tok", [P, NT], F32),
                          ("io4", [P, NGRP], F32), ("io8", [P, EPG], F32), ("io128", [P, P], F32), ("jt", [P, OVMAX], F32),
                          ("prow", [P, 1], F32), ("nprow", [P, 1], F32), ("before", [P, P], F32), ("ones", [P, P], F32),
                          ("cmp", [P, NE, OVMAX], F32), ("ovm", [1, 32], F32), ("ovmi", [1, 32], I32), ("rsum", [P, NT], F32)):
        small[nm], at = place(nm, shape, dt, at)
    assert at <= at_w, (at, at_w)
    (w_r, lg, gmx, goh, gex, gw, le, tmp8, oh, mx, gt, ek, eb, cum, rk, eid, ovs, bk, rw, cl, cnt, nov, ovend, ovst,
     tab, tabf, vld, gtab, valid, tok, io4, io8, io128, jt, prow, nprow, before, ones, cmp_, ovm, ovmi, rsum) = small.values()

    bank = nc.alloc_psum_tensor("bank", [P, 8, 512], F32)
    xT_ps = bank[:, 0:2, :].rearrange("p b (c n) -> p (b c) n", n=P)

    def proj_ps(s):
        return bank[:, 2 + s % 4, 0:CG]

    def head_ps(s):
        return bank[:, 6 + s % 2, 0:2 * P].rearrange("p (c n) -> p c n", n=P)


    def z_ps(u):
        kind = units[u][0]
        b0 = 0 if kind == "tail" else 2 * (u % 2)
        return bank[:, b0:b0 + (3 if kind == "tail" else 2), :].rearrange("p b n -> p (b n)")

    def t_ps(n):
        return bank[:, 4 + n % 2, :].rearrange("p (c n) -> p c n", n=P)

    def o_ps(i):
        return bank[:, 6 + i % 2, :]

    units = [("full", t, h) for t in range(LAST) for h in range(H)]
    units += [("tail", 0), ("tail", 1), ("smp", 0), ("smp", 1)]
    NU, NFULL = len(units), LAST * H

    def width(u):
        kind = units[u][0]
        return P * (units[u][1] + 1) if kind == "full" else TP if kind == "tail" else NKS

    def chunks(u):
        return [(c, min(P, width(u) - P * c)) for c in range(-(-width(u) // P))]

    def groups(u):
        ch = chunks(u)
        return [ch[i:i + 4] for i in range(0, len(ch), 4)]

    first_of_weights, first_of_keys, count = {}, {}, 0
    for i in range(NU + 2):
        if i < NU and units[i][0] == "smp":
            first_of_keys[units[i][1]] = count
            count += 4 * HP
        if i >= 2:
            first_of_weights[i - 2] = count
            count += len(groups(i - 2))

    def first_group(u):
        return first_of_weights[u]

    def key_group(b, hp):
        return first_of_keys[b // 4] + (b % 4) * HP + hp

    def summed_at(u):
        return u + 1 if units[u][0] != "smp" else NFULL + 2 + 4 * (units[u][1] + 1)

    def smp_out(x, g, rows):
        lo = TP + 4 * DS * g
        return x[rows, HP:KT, lo:lo + 4 * DS].rearrange("p c (b j) -> p b c j", j=DS)

    def smp_in(i, half, rows):
        v = o_ps(i)[rows, 0:4 * HP * 8].rearrange("p (b c e) -> p b c e", b=4, c=HP)
        return v[:, :, :, DS * half:DS * half + DS]

    NOUT = NT + 2

    def out_of(u):
        kind = units[u][0]
        if kind == "full":
            return units[u][1], units[u][2] == H - 1
        if kind == "tail":
            return LAST, units[u][1] == 1
        return NT + units[u][1], True

    def sem(name):
        return nc.alloc_semaphore(name)

    s_const = sem("const_loaded")
    s_ident = sem("ident_ready")
    s_xld = [sem(f"x_loaded{i}") for i in range(3)]
    s_wld = [sem(f"w_loaded{i}") for i in range(2)]
    s_whi = sem("w_hi_ready")
    s_wlo = sem("w_lo_ready")
    s_ssq = sem("sumsq_ready")
    s_ms = sem("meansq_ready")
    s_rms = sem("rms_ready")
    s_xs = sem("x_normed")
    s_xT = sem("x_transposed")
    s_xh = sem("x_hi_ready")
    s_xl = sem("x_lo_ready")
    s_pr = sem("projected")
    s_sq = sem("head_squares")
    s_hms = sem("head_meansq")
    s_hrms = sem("head_rms")
    s_kn = sem("qk_normed")
    s_kt = sem("qk_transposed")
    s_ke = sem("qk_copied")
    s_v = sem("v_copied")
    s_kst = [sem(f"k_stored{i}") for i in range(NKN)]
    s_vst = sem("v_stored")
    s_cst2 = sem("more_const_loaded")
    s_mask = sem("masks_ready")
    s_hld = sem("history_loaded")
    s_ht = sem("history_transposed")
    s_uc = sem("u_copied")
    s_ut = sem("u_rows_transposed")
    s_ur = sem("u_rows_copied")
    s_ust = sem("u_rows_stored")
    s_uscr = sem("u_rows_in_scratch")
    s_d = sem("pool_diff_ready")
    s_pm = sem("pool_product")
    s_ph = sem("pool_hi_ready")
    s_pl = sem("pool_lo_ready")
    s_pad = sem("zero_history")
    s_z = sem("scores")
    s_sg = sem("sigmoid_ready")
    s_am = sem("weights_ready")
    s_t = sem("banks_transposed")
    s_te = sem("banks_copied")
    s_av = sem("values_summed")
    s_os = sem("o_copied")
    s_oT = sem("o_transposed")
    s_oh = sem("o_hi_ready")
    s_ol = sem("o_lo_ready")
    s_kld = [sem(f"k_page_loaded{i}") for i in range(2)]
    s_kTs = sem("past_k_copied")
    s_qz = sem("q_spread")
    s_xr = [sem(f"residual_loaded{t}") for t in range(NT)]
    s_wo = sem("w_out_product")
    s_xm = sem("residual_added")
    s_wr = sem("router_weights_loaded")
    s_tbl = sem("router_tables_ready")
    s_zr = sem("zero_rows_ready")
    s_ssq2 = sem("sumsq2_ready")
    s_ms2 = sem("meansq2_ready")
    s_rms2 = sem("rms2_ready")
    s_n2 = sem("ffn_normed")
    s_n2T = sem("ffn_transposed")
    s_n2c = sem("ffn_copied")
    s_lgp = sem("logits_product")
    s_lg = sem("logits_ready")
    s_nst = [sem(f"rows_stored{i}") for i in range(2)]
    s_yst = sem("residual_stored")
    s_gx = sem("group_shifted")
    s_ge = sem("group_exp")
    s_ex = sem("pair_exp")
    s_eb = sem("experts_marked")
    s_rkp = sem("ranks_product")
    s_ohr = sem("slot_one_hots")
    s_tbp = sem("tables_product")
    s_tab = sem("tables_ready")
    s_wl = [[sem(f"{nm}_loaded{i}") for nm in ("gate", "up", "down")] for i in range(2)]
    s_ix = sem("gather_rows_named")
    s_sx = sem("block_gates_ready")
    s_sx2 = sem("scatter_rows_named")
    s_gl = [sem(f"gathered{i}") for i in range(2)]
    s_xt = sem("block_transposed")
    s_xc = sem("block_copied")
    s_gp = sem("gate_product")
    s_up = sem("up_product")
    s_si = sem("silu_ready")
    s_h = sem("hidden_ready")
    s_dp = sem("down_product")
    s_ya = sem("left_half_gated")
    s_yd = sem("right_half_gated")
    s_sc = sem("block_scattered")
    s_dve = sem("dve_chain")
    s_act = sem("act_chain")
    s_pool = sem("pool_chain")

    order = [("k", 0), ("k", 1), ("q", 0), ("q", 1), ("v", 0), ("v", 1), ("u", 0), ("u", 1)]
    first_col = {"u": 0, "q": PW, "k": PW + AW, "v": PW + 2 * AW}
    steps = [(kind, half, t) for kind, half in order[:6] for t in range(NT)]
    NS = len(steps)
    qk_steps = [s for s in range(NS) if steps[s][0] in "qk"]
    NQK = len(qk_steps)
    assert qk_steps == list(range(NQK))

    usteps = [(g, piece) for g in range(NG) for piece in range(3)]
    NUS = len(usteps)
    wsteps = [(n, t) for n in range(D // CG) for t in range(NT)]

    def wide_ps(s):
        return bank[:, 2 + s % 4, :]

    def u_copies(i):
        return 1 + i + 1 + 2 * ((i + 1) // 3)

    u_scr = nc.dram_tensor("u_scr", [TS, PW], F32).ap()
    w_in_v = w_in.rearrange("(kt p) e -> p kt e", p=P)
    n_scr = nc.dram_tensor("n_scr", [NY, D], F32).ap()
    gate_v = w_gate.rearrange("e (kt p) f -> e p kt f", p=P)
    up_v = w_up.rearrange("e (kt p) f -> e p kt f", p=P)
    down_v = w_down.rearrange("e (ft p) d -> e p ft d", p=P)
    w_out_v = w_out.rearrange("(kt p) e -> p kt e", p=P)

    def gate_ps(i):
        return bank[:, 2 + i, 0:FT * CAP].rearrange("p (f n) -> p f n", f=FT)

    def up_ps(i):
        return bank[:, 4 + i, 0:FT * CAP].rearrange("p (f n) -> p f n", f=FT)

    def blocks(eng, body):
        for b in range(2):
            body(b, b)
        with eng.Fori(1, NE // 2) as i:
            for k in range(2):
                body(k, 2 * i + k)
        eng.wait_ge(s_tab, 1)
        n_over = eng.value_load(ovmi[0:1, OVB:OVB + 1], min_val=0, max_val=OVB)
        with eng.Fori(0, OVB // 2) as i:
            for k in range(2):
                with eng.If(n_over > 2 * i + k):
                    body(k, 2 * i + k + NE)

    blk = nc.Block()

    with nc.allow_non_contiguous_dma(reason="small vectors and broadcasts"), blk as block:

        @block.sync
        def _(sp):
            def load_x(t):
                if t >= 3:
                    sp.wait_ge(s_xT, t - 2)
                lo = P * t - META
                if t == 0:
                    sp.dma_start(xt[0][0:META, :], meta_tokens).then_inc(s_xld[0], 16)
                    sp.dma_start(xt[0][META:P, :], x_prompt[0, 0:P - META, :]).then_inc(s_xld[0], 16)
                elif t < LAST:
                    sp.dma_start(xt[t % 3][:, :], x_prompt[0, lo:lo + P, :]).then_inc(s_xld[t % 3], 32)
                else:
                    sp.dma_start(xt[t % 3][0:TAILP, :], x_prompt[0, lo:SEQ, :]).then_inc(s_xld[t % 3], 16)
                    sp.dma_start(xt[t % 3][TAILP:TAILP + TS, :],
                                 x_sample.rearrange("b s d -> (b s) d")).then_inc(s_xld[t % 3], 16)

            def load_w(n):
                kind, half = order[n]
                c = first_col[kind] + half * CG
                if n >= 2:
                    sp.wait_ge(s_whi, n - 1)
                    sp.wait_ge(s_wlo, n - 1)
                sp.dma_start(w_raw[n % 2][:, :, :], w_in_v[:, :, c:c + CG]).then_inc(s_wld[n % 2], 16)

            load_x(0)
            sp.dma_start(gmix[:, :], norm_mix.to_broadcast([P, D])).then_inc(s_const, 16)
            load_w(0)
            sp.dma_start(gq_bc[:, :], g_q.to_broadcast([P, HD])).then_inc(s_const, 16)
            sp.dma_start(gk_bc[:, :], g_k.to_broadcast([P, HD])).then_inc(s_const, 16)
            load_x(1)
            load_x(2)
            load_w(1)
            sp.dma_start(hist[0:DB * HIST, :], state_pool.rearrange("b h w -> (b h) w")).then_inc(s_hld, 16)
            consts = [(bias_bc[:, :], sb_bias.to_broadcast([P, H])),
                      (wp_sb[:, :, :], w_pool.rearrange("g c e -> c g e")),
                      (pscale[:, :], pool_scale.rearrange("a (g c) -> c (a g)", c=P)),
                      (pt_sb[:, :], page_table.rearrange("(a b) j -> a (b j)", a=1))]
            assert len(consts) == NCONST
            for out, src in consts:
                sp.dma_start(out, src).then_inc(s_cst2, 16)
            for s in range(NS):
                kind, half, t = steps[s]
                if s + 3 < NT:
                    load_x(s + 3)
                if t == 5 and s // NT + 2 < 8:
                    load_w(s // NT + 2)
                r = ROWS[t]
                if kind == "k":
                    sp.wait_ge(s_kn, s + 1)
                    sp.dma_start(k_all[row0(t):row0(t) + r, half * CG:half * CG + CG],
                                 kn[s % NKN][0:r, :]).then_inc(s_kst[s % NKN], 16)
                if kind == "v":
                    sp.wait_ge(s_v, s - NQK + 1)
                    sp.dma_start(v_all[row0(t):row0(t) + r, half * CG:half * CG + CG],
                                 vv[0:r, t, half * CG:half * CG + CG]).then_inc(s_vst, 16)
            sp.wait_ge(s_ur, 2)
            sp.dma_start(pool_p, up_rows[TAILP - HIST:TAILP, :]).then_inc(s_ust, 16)
            sp.dma_start(u_scr, us_rows[:, :]).then_inc(s_uscr, 16)
            sp.dma_start(pool_s[:, 0:HIST - DS, :], state_pool[:, DS:HIST, :]).then_inc(s_ust, 16)
            sp.wait_ge(s_uscr, 16)
            sp.dma_start(pool_s[:, HIST - DS:HIST, :],
                         u_scr.rearrange("(b s) w -> b s w", s=DS)).then_inc(s_ust, 16)
            sp.wait_ge(s_cst2, 16 * NCONST)
            loads = [(k, b) for k in ("k", "v") for b in range(DB)]
            for i, (k, b) in enumerate(loads):
                if i == 0:
                    sp.wait_ge(s_d, NG)
                    sp.wait_ge(s_pl, NUS)
                    sp.wait_ge(s_ut, 1)
                if i >= 2:
                    kk, bb = loads[i - 2]
                    if kk == "k":
                        sp.wait_ge(s_t, key_group(bb, HP - 1) + 1)
                    else:
                        sp.wait_ge(s_av, NFULL + 2 + bb + 1)
                for j in range(NPG):
                    page = sp.value_load(pt_sb[0:1, b * NPG + j:b * NPG + j + 1], min_val=0,
                                         max_val=cache_k.shape[0] - 1)
                    src = (cache_k if k == "k" else cache_v)[bass.ds(page, 1), :, :, :]
                    sp.dma_start(pg[i % 2][:, j, :],
                                 src.rearrange("a p h d -> (a p) (h d)")).then_inc(s_kld[i % 2], 16)
            sp.wait_ge(s_av, NFULL + 2 + DB)
            def load_w_out(n):
                if n >= 2:
                    sp.wait_ge(s_whi, 8 + n - 1)
                    sp.wait_ge(s_wlo, 8 + n - 1)
                sp.dma_start(w_raw[n % 2][:, :, :], w_out_v[:, :, n * CG:n * CG + CG]).then_inc(s_wld[n % 2], 16)

            load_w_out(0)
            load_w_out(1)
            for t in range(NT):
                lo = P * t - META
                if t == 0:
                    sp.dma_start(xmid[0:META, 0, :], meta_tokens).then_inc(s_xr[t], 16)
                    sp.dma_start(xmid[META:P, 0, :], x_prompt[0, 0:P - META, :]).then_inc(s_xr[t], 16)
                elif t < LAST:
                    sp.dma_start(xmid[:, t, :], x_prompt[0, lo:lo + P, :]).then_inc(s_xr[t], 32)
                else:
                    sp.dma_start(xmid[0:TAILP, t, :], x_prompt[0, lo:SEQ, :]).then_inc(s_xr[t], 16)
                    sp.dma_start(xmid[TAILP:TAILP + TS, t, :],
                                 x_sample.rearrange("b s d -> (b s) d")).then_inc(s_xr[t], 16)
            load_w_out(2)
            load_w_out(3)

            def load_expert(i, e, gate_free, down_free):
                for j, (buf, src, done, value) in enumerate(((wg, gate_v, s_gp, gate_free), (wu, up_v, s_up, gate_free),
                                                             (wd, down_v, s_dp, down_free))):
                    if gate_free is not None:
                        sp.wait_ge(done, value)
                    part = src[bass.ds(e, 1)].rearrange("a p k f -> (a p) k f")
                    sp.dma_start(buf[i][:, :, :], part).then_inc(s_wl[i][j], 16)

            sp.wait_ge(s_wo, len(wsteps))
            sp.dma_start(w_r[:, :, 0:NGRP], w_group.rearrange("(kt p) e -> p kt e", p=P)).then_inc(s_wr, 16)
            sp.dma_start(w_r[:, :, NGRP:NGRP + NE], w_expert.rearrange("(kt p) e -> p kt e", p=P)).then_inc(s_wr, 16)
            sp.dma_start(gffn[:, :], norm_ffn.to_broadcast([P, D])).then_inc(s_wr, 16)
            for i in range(2):
                load_expert(i, i, None, None)
            sp.wait_ge(s_zr, 1)
            sp.dma_start(n_scr[T:NY, :], zrow[:, :]).then_inc(s_yst, 16)
            sp.dma_start(y_all[T:NY, :], zrow[:, :]).then_inc(s_yst, 16)
            for t in range(NT):
                r = ROWS[t]
                sp.wait_ge(s_n2, t + 1)
                sp.dma_start(y_all[row0(t):row0(t) + r, :], xmid[0:r, t, :]).then_inc(s_yst, 16)
                sp.dma_start(n_scr[row0(t):row0(t) + r, :], xg[t % 2][0:r, :]).then_inc(s_nst[t % 2], 16)
            with sp.Fori(1, NE // 2) as i:
                for k in range(2):
                    b = 2 * i + k
                    load_expert(k, b, b - 1, 2 * b - 2)
            sp.wait_ge(s_tab, 1)
            n_over = sp.value_load(ovmi[0:1, OVB:OVB + 1], min_val=0, max_val=OVB)
            with sp.Fori(0, OVB // 2) as i:
                for k in range(2):
                    o = 2 * i + k
                    with sp.If(n_over > o):
                        e = sp.value_load(ovmi[0:1, bass.ds(o, 1)], min_val=0, max_val=NE - 1)
                        load_expert(k, e, o + NE - 1, 2 * o + 2 * NE - 2)
            sp.wait_ge(s_ust, 48)
            for i in range(NKN):
                sp.wait_ge(s_kst[i], 16 * len([s for s in range(2 * NT) if s % NKN == i]))
            sp.wait_ge(s_vst, 16 * 2 * NT)

        @block.gpsimd
        def _(pool):
            chain = Chain(pool, s_pool)
            chain.link(pool.memset(ident[:, :], 1.0))
            pool.affine_select(out=ident[:, :], in_=ident[:, :], compare_op=ALU.is_equal, fill=0.0, base=0,
                               pattern=[[-1, P]], channel_multiplier=1).then_inc(s_ident, 1)
            chain.link(pool.memset(diag_mask[:, :], 1.0))
            chain.link(pool.affine_select(out=diag_mask[:, :], in_=diag_mask[:, :], compare_op=ALU.is_gt, fill=0.0,
                                          base=0, pattern=[[-1, P]], channel_multiplier=1))
            chain.link(pool.memset(tail_mask[:, :], 1.0))
            for j in range(4):
                part = tail_mask[32 * j:32 * j + 32, :]
                chain.link(pool.affine_select(out=part, in_=part, compare_op=ALU.is_gt, fill=0.0, base=0,
                                              pattern=[[-1, TAILP]], channel_multiplier=1))
            chain.link(pool.iota(pint[:, 0:1], [[0, 1]], base=0, channel_multiplier=1))
            chain.link(pool.iota(col48[:, :], [[1, ROWS[-1]]], base=0, channel_multiplier=0,
                                 allow_small_or_imprecise_dtypes=True))
            pool.iota(rcnt[:, :], [[1, 16]], base=1, channel_multiplier=0,
                      allow_small_or_imprecise_dtypes=True).then_inc(s_mask, 1)
            pool.wait_ge(s_kn, NQK)
            pool.wait_ge(s_kt, NQK)
            pool.wait_ge(s_xT, NT)
            for i in range(NKN):
                pool.wait_ge(s_kst[i], 16 * len([s for s in range(2 * NT) if s % NKN == i]))
            chain.link(pool.memset(u_ext[:, :, 0:16], 0.0))
            pool.memset(es[:, :, :, 0:1], 0.0).then_inc(s_pad, 1)
            pool.wait_ge(s_pl, NUS)
            pool.wait_ge(s_ut, 1)
            pool.memset(qz[:, :, :, :], 0.0).then_inc(s_pad, 1)
            pool.wait_ge(s_wo, len(wsteps))
            chain.link(pool.memset(zrow[:, :], 0.0))
            pool.memset(ones[:, :], 1.0).then_inc(s_zr, 1)
            pool.wait_ge(s_zr, 1)
            chain.link(pool.memset(before[:, :], 1.0))
            chain.link(pool.affine_select(out=before[:, :], in_=before[:, :], compare_op=ALU.is_gt, fill=0.0,
                                          base=0, pattern=[[1, P]], channel_multiplier=-1))
            for out, pattern, first, mult in ((tok[:, :], [[P, NT]], -T, 1), (io4[:, :], [[1, NGRP]], -NGRP, 0),
                                              (io8[:, :], [[1, EPG]], -EPG, 0), (io128[:, :], [[1, P]], 0, 0),
                                              (jt[:, :], [[CAP, OVMAX]], CAP, 0), (nprow[:, :], [[0, 1]], 0, -1),
                                              (prow[:, :], [[0, 1]], T, 1)):
                chain.link(pool.iota(out, pattern, base=first, channel_multiplier=mult,
                                     allow_small_or_imprecise_dtypes=True))
            pool.memset(lg[:, LAST, :], 0.0).then_inc(s_tbl, 1)

            def gather(b):
                i = b % 2
                pool.wait_ge(s_ix, b + 1)
                if b >= 2:
                    pool.wait_ge(s_xt, b - 1)
                pool.indirect_dma_start(out=xg[i][0:CAP, :], out_offset=None, in_=n_scr,
                                        in_offset=bass.IndirectOffsetOnAxis(ap=gidx[i][:, 0:1].bitcast(U32), axis=0)
                                        ).then_inc(s_gl[i], 16)

            def block_io(b):
                gather(b + 2)
                pool.wait_ge(s_ya, b + 1)
                pool.wait_ge(s_yd, b + 1)
                pool.wait_ge(s_sx2, b + 1)
                pool.indirect_dma_start(out=y_all,
                                        out_offset=bass.IndirectOffsetOnAxis(ap=sidx[b % 2][:, 0:1].bitcast(U32), axis=0),
                                        in_=yo[b % 2][:, :], in_offset=None, compute_op=ALU.add,
                                        bounds_check=NY - 1).then_inc(s_sc, 16)
                pool.wait_ge(s_gl[b % 2], 16 * (b // 2 + 2))
                pool.wait_ge(s_sc, 16 * (b + 1))

            for i in range(2):
                pool.wait_ge(s_nst[i], 16 * len(range(i, NT, 2)))
            pool.wait_ge(s_yst, 16 * (NT + 2))
            gather(0)
            gather(1)
            for b in range(NE):
                block_io(b)
            pool.wait_ge(s_tab, 1)
            n_over = pool.value_load(ovmi[0:1, OVB:OVB + 1], min_val=0, max_val=OVB)
            for o in range(OVB):
                with pool.If(n_over > o):
                    block_io(NE + o)

        @block.scalar
        def _(act):
            chain = Chain(act, s_act)

            def norm_tile(t):
                r = ROWS[t]
                act.wait_ge(s_xld[t % 3], 32 * (t // 3 + 1))
                if t >= 1:
                    act.wait_ge(s_ssq, t)
                if t >= 2:
                    act.wait_ge(s_ms, t - 1)
                act.activation(junk[0:r, :], xt[t % 3][0:r, :], ACT.Square,
                               accum_out=ss[0:r, t % 2:t % 2 + 1]).then_inc(s_ssq, 1)
                act.wait_ge(s_ms, t + 1)
                act.activation(rs[0:r, t % 2:t % 2 + 1], ss[0:r, t % 2:t % 2 + 1], ACT.Sqrt).then_inc(s_rms, 1)
                act.wait_ge(s_xT, t + 1)
                act.activation(xh[:, :, row0(t):row0(t) + r], xT_ps[:, :, 0:r], ACT.Copy).then_inc(s_xh, 1)

            def split_hi(n):
                act.wait_ge(s_wld[n % 2], 16 * (n // 2 + 1))
                if n >= 2:
                    act.wait_ge(s_pr, NT * (n - 1))
                act.activation(w_hi[n % 2][:, :, :], w_raw[n % 2][:, :, :], ACT.Copy).then_inc(s_whi, 1)

            split_hi(0)
            norm_tile(0)
            for s in range(NS + 3):
                if s + 1 < NT:
                    norm_tile(s + 1)
                if s % NT == 3 and s // NT + 1 < 8:
                    split_hi(s // NT + 1)
                if s < NQK:
                    r = ROWS[steps[s][2]]
                    act.wait_ge(s_pr, s + 1)
                    if s >= 2:
                        act.wait_ge(s_hms, s - 1)
                    act.activation(sq[s % 2][0:r, :], proj_ps(s)[0:r, :], ACT.Square).then_inc(s_sq, 1)
                elif s < NS:
                    _, half, t = steps[s]
                    r = ROWS[t]
                    if s == NQK:
                        act.wait_ge(s_ssq, NT)
                    act.wait_ge(s_pr, s + 1)
                    act.activation(vv[0:r, t, half * CG:half * CG + CG], proj_ps(s)[0:r, :],
                                   ACT.Copy).then_inc(s_v, 1)
                if 1 <= s <= NQK:
                    r = ROWS[steps[s - 1][2]]
                    act.wait_ge(s_hms, s)
                    act.activation(hr[0:r, (s - 1) % 2, :], hs[0:r, (s - 1) % 2, :], ACT.Sqrt).then_inc(s_hrms, 1)
                if 3 <= s < NQK + 3:
                    kind, half, t = steps[s - 3]
                    r = ROWS[t]
                    act.wait_ge(s_kt, s - 2)
                    dst = qT if kind == "q" else kT
                    act.activation(dst[:, 2 * half:2 * half + 2, row0(t):row0(t) + r],
                                   head_ps(s - 3)[:, :, 0:r], ACT.Copy).then_inc(s_ke, 1)
            split_hi(7)

            act.wait_ge(s_pad, 1)
            act.wait_ge(s_ht, 1)
            act.activation(es[:, :, :, 1:16],
                           bank[:, 6, 0:NG * DB * HIST].rearrange("p (g b i) -> p g b i", g=NG, b=DB),
                           ACT.Copy).then_inc(s_uc, 1)
            for i, (g, piece) in enumerate(usteps):
                s = NS + i
                lo, n = PIECES[piece]
                act.wait_ge(s_pr, s + 1)
                if piece < 2:
                    act.activation(u_ext[:, g, 16 + lo:16 + lo + n], wide_ps(s)[:, 0:n], ACT.Copy).then_inc(s_uc, 1)
                else:
                    act.activation(u_ext[:, g, 16 + lo:16 + TP], wide_ps(s)[:, 0:TAILP], ACT.Copy).then_inc(s_uc, 1)
                    act.activation(es[:, g, :, 16:20], wide_ps(s)[:, TAILP:TAILP + TS].rearrange("p (b j) -> p b j", j=DS),
                                   ACT.Copy).then_inc(s_uc, 1)
                    act.activation(us_cols[:, g, :], wide_ps(s)[:, TAILP:TAILP + TS], ACT.Copy).then_inc(s_uc, 1)
            act.wait_ge(s_ut, 1)
            act.activation(up_rows[:, :], bank[0:TAILP, 6, :], ACT.Copy).then_inc(s_ur, 1)
            act.activation(us_rows[:, :], bank[0:TS, 7, :], ACT.Copy).then_inc(s_ur, 1)
            act.wait_ge(s_cst2, 16 * NCONST)
            for i, (g, piece) in enumerate(usteps):
                lo, n = PIECES[piece]
                act.wait_ge(s_pm, i + 1)
                act.activation(xh[:, g, lo:lo + n], wide_ps(NS + NUS + i)[:, 0:n], ACT.Copy,
                               scale=pscale[:, g:g + 1]).then_inc(s_ph, 1)

            def sigmoid(u):
                kind, w = units[u][0], width(u)
                act.wait_ge(s_z, u + 1)
                if u >= 2:
                    act.wait_ge(s_am, u - 1)
                elif u == 0:
                    act.wait_ge(s_pm, NUS)
                    act.wait_ge(s_d, NG)
                    act.wait_ge(s_pr, NS + NUS)
                    act.wait_ge(s_mask, 2)
                bias = (bias_bc[:, units[u][2]:units[u][2] + 1] if kind == "full" else
                        bias_tail[:, units[u][1]:units[u][1] + 1] if kind == "tail" else bias_smp[:, 0:1])
                act.activation(sg[u % 2][:, NK - w:NK], z_ps(u)[:, 0:w], ACT.Sigmoid, bias=bias,
                               scale=HD ** -0.5).then_inc(s_sg, 1)

            def copy_banks(u):
                for j, group in enumerate(groups(u)):
                    n = first_group(u) + j
                    act.wait_ge(s_t, n + 1)
                    if j == 0 and u >= 2:
                        act.wait_ge(s_av, summed_at(u - 2))
                    full = [c for c in group if c[1] == P]
                    if full:
                        last = act.activation(aT[u % 2][:, full[0][0]:full[-1][0] + 1, :], t_ps(n)[:, 0:len(full), :], ACT.Copy)
                    if len(full) < len(group):
                        c, keys = group[-1]
                        last = act.activation(aT[u % 2][0:keys, c, :], t_ps(n)[0:keys, len(full), :], ACT.Copy)
                    last.then_inc(s_te, 1)

            def copy_o(u):
                i, ends = out_of(u)
                if ends and i < NT:
                    act.wait_ge(s_av, summed_at(u))
                    if i >= 1:
                        act.wait_ge(s_oT, i)
                    act.activation(o_sb[0:P if i < LAST else TAILP, :], o_ps(i)[0:P if i < LAST else TAILP, :],
                                   ACT.Copy).then_inc(s_os, 1)

            def hi_o(u):
                i, ends = out_of(u)
                if ends and i < NT:
                    r = P if i < LAST else TAILP
                    act.wait_ge(s_oT, i + 1)
                    act.activation(xh[:, HP:KT, row0(i):row0(i) + r],
                                   o_ps(i).rearrange("p (c n) -> p c n", n=P)[:, :, 0:r], ACT.Copy).then_inc(s_oh, 1)
                if i >= NT:
                    act.wait_ge(s_av, summed_at(u))
                    for half in range(2):
                        rows = slice(64 * half, 64 * half + 64)
                        last = act.activation(smp_out(xh, i - NT, rows), smp_in(i, half, rows), ACT.Copy)
                        if half == 0:
                            last.then_inc(s_act, 1)
                    last.then_inc(s_oh, 1)

            def copy_keys(g):
                for b in range(4 * g, 4 * g + 4):
                    for hp in range(HP):
                        n = key_group(b, hp)
                        act.wait_ge(s_t, n + 1)
                        if b >= 1:
                            act.wait_ge(s_kTs, b)
                        last = act.activation(kTs[:, hp, :], bank[:, 4 + n % 2, :], ACT.Copy)
                        last.then_inc(s_te, 1)

            for i in range(NU + 6):
                if i < NU:
                    if units[i][0] == "smp":
                        copy_keys(units[i][1])
                    sigmoid(i)
                if 2 <= i < NU + 2:
                    copy_banks(i - 2)
                if 4 <= i < NU + 4:
                    copy_o(i - 4)
                if 6 <= i:
                    hi_o(i - 6)

            def split_out_hi(n):
                act.wait_ge(s_wld[n % 2], 16 * (4 + n // 2 + 1))
                if n >= 2:
                    act.wait_ge(s_wo, NT * (n - 1))
                act.activation(w_hi[n % 2][:, :, :], w_raw[n % 2][:, :, :], ACT.Copy).then_inc(s_whi, 1)

            for n in range(D // CG):
                split_out_hi(n)

            for t in range(NT):
                r = ROWS[t]
                act.wait_ge(s_xm, (D // CG - 1) * NT + t + 1)
                if t >= 1:
                    act.wait_ge(s_ssq2, t)
                if t >= 2:
                    act.wait_ge(s_ms2, t - 1)
                act.activation(junk2[0:r, :], xmid[0:r, t, :], ACT.Square,
                               accum_out=ss[0:r, t % 2:t % 2 + 1]).then_inc(s_ssq2, 1)
                act.wait_ge(s_ms2, t + 1)
                act.activation(rs[0:r, t % 2:t % 2 + 1], ss[0:r, t % 2:t % 2 + 1], ACT.Sqrt).then_inc(s_rms2, 1)
                act.wait_ge(s_n2T, t + 1)
                if t >= 2:
                    act.wait_ge(s_lgp, t - 1)
                act.activation(nT[t % 2][:, :, 0:r], xT_ps[:, :, 0:r], ACT.Copy).then_inc(s_n2c, 1)
            act.wait_ge(s_gx, 1)
            act.activation(gex[:, :, :], gex[:, :, :], ACT.Exp).then_inc(s_ge, 1)
            act.wait_ge(s_gx, 2)
            act.activation(gt[:, 1, :], gt[:, 1, :], ACT.Exp).then_inc(s_ge, 1)

            def copy_block(i, b):
                act.wait_ge(s_xt, b + 1)
                if not (type(b) is int and b < 2):
                    act.wait_ge(s_up, b - 1)
                act.activation(xTe[i][:, :, :], xT_ps[:, :, 0:CAP], ACT.Copy).then_inc(s_xc, 1)

            def block_act(i, b):
                early = type(b) is int and b < 2
                act.wait_ge(s_gp, b + 1)
                if not early:
                    act.wait_ge(s_h, b - 1)
                act.activation(sgl[i][:, :, :], gate_ps(i), ACT.Silu).then_inc(s_si, 1)
                copy_block(1 - i, b + 1)
                act.wait_ge(s_dp, 2 * b + 1)
                act.wait_ge(s_sx, b + 1)
                act.activation(yo[i][:, 0:512], bank[0:CAP, 6, :], ACT.Copy, scale=gcol[i][:, 0:1]).then_inc(s_ya, 1)

            copy_block(0, 0)
            blocks(act, block_act)

        @block.vector
        def _(dve):
            chain = Chain(dve, s_dve)

            def norm_tile(t):
                r = ROWS[t]
                c = slice(t % 2, t % 2 + 1)
                dve.wait_ge(s_ssq, t + 1)
                dve.tensor_scalar(ss[0:r, c], ss[0:r, c], 1.0 / D, EPS, ALU.mult, ALU.add).then_inc(s_ms, 1)
                dve.wait_ge(s_rms, t + 1)
                chain.link(dve.reciprocal(rs[0:r, c], rs[0:r, c]))
                dve.scalar_tensor_tensor(out=xt[t % 3][0:r, :], in0=xt[t % 3][0:r, :], scalar=rs[0:r, c],
                                         in1=gmix[0:r, :], op0=ALU.mult, op1=ALU.mult).then_inc(s_xs, 1)
                dve.wait_ge(s_xh, t + 1)
                dve.tensor_tensor(xl[:, :, row0(t):row0(t) + r], xT_ps[:, :, 0:r],
                                  xh[:, :, row0(t):row0(t) + r].bitcast(F32), ALU.subtract).then_inc(s_xl, 1)

            def split_lo(n):
                dve.wait_ge(s_whi, n + 1)
                if n >= 2:
                    dve.wait_ge(s_pr, NT * (n - 1))
                dve.tensor_tensor(w_lo[n % 2][:, :, :], w_raw[n % 2][:, :, :], w_hi[n % 2][:, :, :].bitcast(F32),
                                  ALU.subtract).then_inc(s_wlo, 1)

            def norm_heads(s):
                kind, half, t = steps[s]
                r = ROWS[t]
                dve.wait_ge(s_hrms, s + 1)
                chain.link(dve.reciprocal(hr[0:r, s % 2, :], hr[0:r, s % 2, :]))
                if s >= NKN:
                    dve.wait_ge(s_kt, s - NKN + 1)
                    if steps[s - NKN][0] == "k":
                        dve.wait_ge(s_kst[s % NKN], 16 * (s // NKN))
                out = kn[s % NKN][0:r, :].rearrange("p (h d) -> p h d", d=HD)
                inv = hr[0:r, s % 2, :].rearrange("p (h a) -> p h a", a=1).to_broadcast([r, 4, HD])
                chain.link(dve.tensor_tensor(out, proj_ps(s)[0:r, :].rearrange("p (h d) -> p h d", d=HD), inv, ALU.mult))
                g = (gq_bc if kind == "q" else gk_bc)[0:r, :].rearrange("p (a d) -> p a d", a=1)
                dve.tensor_tensor(out, out, g.to_broadcast([r, 4, HD]), ALU.mult).then_inc(s_kn, 1)

            dve.wait_ge(s_const, 48)
            split_lo(0)
            norm_tile(0)
            for s in range(NQK + 1):
                if s + 1 < NT:
                    norm_tile(s + 1)
                if s % NT == 3 and s // NT + 1 < 8:
                    split_lo(s // NT + 1)
                if s < NQK:
                    r = ROWS[steps[s][2]]
                    dve.wait_ge(s_sq, s + 1)
                    chain.link(dve.reduce_sum(hs[0:r, s % 2, :], sq[s % 2][0:r, :].rearrange("p (h d) -> p h d", d=HD),
                                              axis=AXX))
                    dve.tensor_scalar(hs[0:r, s % 2, :], hs[0:r, s % 2, :], 1.0 / HD, EPS,
                                      ALU.mult, ALU.add).then_inc(s_hms, 1)
                if s >= 1:
                    norm_heads(s - 1)
            split_lo(5)
            dve.wait_ge(s_mask, 1)
            dve.wait_ge(s_cst2, 16 * NCONST)
            chain.done(dve.tensor_scalar(pint[:, 1:2], pint[:, 0:1], 3, None, ALU.bitwise_and))
            chain.done(dve.tensor_scalar(pint[:, 2:3], pint[:, 0:1], 5, None, ALU.logical_shift_right))
            chain.done(dve.tensor_scalar(pint[:, 3:4], pint[:, 0:1], 2, 7, ALU.logical_shift_right, ALU.bitwise_and))
            chain.settle()
            chain.link(dve.tensor_copy(pflt[:, 0:3], pint[:, 1:4]))
            for g in range(2):
                chain.link(dve.tensor_scalar(pflt[:, 3:4], pflt[:, 1:2], float(DS), float(TAILP + 16 * g), ALU.mult, ALU.add))
                chain.link(dve.tensor_tensor(pflt[:, 4:5], pflt[:, 3:4], pflt[:, 0:1], ALU.add))
                chain.link(dve.tensor_scalar(smp_mask[:, g, :], col48[:, :], pflt[:, 3:4], None, ALU.is_ge))
                chain.link(dve.scalar_tensor_tensor(out=smp_mask[:, g, :], in0=col48[:, :], scalar=pflt[:, 4:5],
                                                    in1=smp_mask[:, g, :], op0=ALU.is_lt, op1=ALU.mult))
            chain.link(dve.memset(bias_smp[:, :], 0.0))
            for h in range(H):
                chain.link(dve.tensor_scalar(pflt[:, 5:6], pflt[:, 2:3], float(h), None, ALU.is_equal))
                chain.link(dve.scalar_tensor_tensor(out=bias_smp[:, :], in0=pflt[:, 5:6], scalar=bias_bc[:, h:h + 1],
                                                    in1=bias_smp[:, :], op0=ALU.mult, op1=ALU.add))
            for h in range(H):
                rows = slice(32 * (h % 4), 32 * (h % 4) + 32)
                chain.done(dve.tensor_copy(bias_tail[rows, h // 4:h // 4 + 1], bias_bc[rows, h:h + 1]))
            dve.reciprocal(rcnt[:, :], rcnt[:, :]).then_inc(s_mask, 1)
            dve.wait_ge(s_mask, 2)
            split_lo(6)
            split_lo(7)

            def diff(g):
                w = WINDOWS[g]
                dve.wait_ge(s_uc, u_copies(3 * g + 2))
                if g == 0:
                    dve.wait_ge(s_pr, NS + 6)
                    dve.wait_ge(s_wlo, 8)
                    dve.wait_ge(s_whi, 8)
                src, n = u_ext[:, g, :], 1
                srcs = es[:, g, :, :]
                small = [wsmall0, wsmall1]
                k = 0
                while n < w:
                    dst, dsts = wsum[k % 2], small[k % 2]
                    chain.done(dve.tensor_tensor(dst[:, 2 * n - 1:16 + TP], src[:, 2 * n - 1:16 + TP],
                                                 src[:, n - 1:16 + TP - n], ALU.add))
                    chain.done(dve.tensor_tensor(dsts[:, :, 2 * n - 1 + 1:20], srcs[:, :, 2 * n - 1 + 1:20],
                                                 srcs[:, :, n:20 - n], ALU.add))
                    chain.settle()
                    src, srcs, n, k = dst, dsts, 2 * n, k + 1
                if g >= 1:
                    dve.wait_ge(s_pm, 3 * g)
                chain.done(dve.scalar_tensor_tensor(out=dT[:, w - 1:TP], in0=src[:, 16 + w - 1:16 + TP], scalar=1.0 / w,
                                                    in1=u_ext[:, g, 16 + w - 1:16 + TP], op0=ALU.mult, op1=ALU.subtract))
                chain.link(dve.tensor_tensor(dT[:, 0:w - 1], src[:, 16:16 + w - 1], rcnt[:, 0:w - 1], ALU.mult))
                chain.link(dve.tensor_tensor(dT[:, 0:w - 1], dT[:, 0:w - 1], u_ext[:, g, 16:16 + w - 1], ALU.subtract))
                dve.scalar_tensor_tensor(out=dT[:, TP:T].rearrange("p (b j) -> p b j", j=DS), in0=srcs[:, :, 16:20],
                                         scalar=1.0 / w, in1=es[:, g, :, 16:20], op0=ALU.mult,
                                         op1=ALU.subtract).then_inc(s_d, 1)
                dve.wait_ge(s_d, g + 1)

            def pool_lo(g):
                for piece in range(3):
                    i = 3 * g + piece
                    lo, n = PIECES[piece]
                    dve.wait_ge(s_ph, i + 1)
                    dve.scalar_tensor_tensor(out=xl[:, g, lo:lo + n], in0=wide_ps(NS + NUS + i)[:, 0:n],
                                             scalar=pscale[:, g:g + 1], in1=xh[:, g, lo:lo + n].bitcast(F32),
                                             op0=ALU.mult, op1=ALU.subtract).then_inc(s_pl, 1)

            for g in range(NG):
                diff(g)
                if g >= 1:
                    pool_lo(g - 1)
            pool_lo(NG - 1)

            dve.wait_ge(s_pad, 2)
            dve.wait_ge(s_ke, NQK)
            for h in range(H):
                rows = slice(64 * (h % 2), 64 * (h % 2) + 64)
                last = dve.tensor_copy(qz[rows, :, h // 2, DS * h:DS * h + DS],
                                       qT[rows, h // 2, TP:T].rearrange("p (b j) -> p b j", j=DS))
                if h < H - 1:
                    chain.done(last)
            last.then_inc(s_qz, 1)

            def weigh(u):
                kind, w = units[u][0], width(u)
                lo = NK - w
                row, prod = sg[u % 2], pb[u % 2]
                dve.wait_ge(s_sg, u + 1)
                if kind == "full":
                    chain.link(dve.tensor_tensor(row[:, NK - P:NK], row[:, NK - P:NK], diag_mask[:, :], ALU.mult))
                elif kind == "tail":
                    chain.link(dve.tensor_tensor(row[:, NK - TAILP:NK], row[:, NK - TAILP:NK], tail_mask[:, :], ALU.mult))
                else:
                    n = ROWS[-1]
                    chain.link(dve.tensor_tensor(row[:, NK - n:NK], row[:, NK - n:NK], smp_mask[:, units[u][1], :], ALU.mult))
                chain.link(dve.tensor_scalar(kp[:, lo:NK], row[:, lo:NK], -1.0, 1.0, ALU.mult, ALU.add))
                chain.link(dve.tensor_tensor_scan(prod[:, lo:NK][:, ::-1], kp[:, lo:NK][:, ::-1], kp[:, lo:NK][:, ::-1],
                                                  1.0, ALU.mult, ALU.bypass))
                if u >= 2:
                    dve.wait_ge(s_t, first_group(u - 2) + len(groups(u - 2)))
                dve.tensor_tensor(am[u % 2][:, lo:NK], row[:, lo:NK], prod[:, lo + 1:NK + 1], ALU.mult).then_inc(s_am, 1)
                dve.wait_ge(s_am, u + 1)

            def lo_o(u):
                i, ends = out_of(u)
                if ends and i < NT:
                    r = P if i < LAST else TAILP
                    dve.wait_ge(s_oh, i + 1)
                    dve.tensor_tensor(xl[:, HP:KT, row0(i):row0(i) + r],
                                      o_ps(i).rearrange("p (c n) -> p c n", n=P)[:, :, 0:r],
                                      xh[:, HP:KT, row0(i):row0(i) + r].bitcast(F32), ALU.subtract).then_inc(s_ol, 1)
                if i >= NT:
                    dve.wait_ge(s_oh, i + 1)
                    dve.wait_ge(s_act, i - NT + 1)
                    for half in range(2):
                        rows = slice(64 * half, 64 * half + 64)
                        last = dve.tensor_tensor(smp_out(xl, i - NT, rows), smp_in(i, half, rows),
                                                 smp_out(xh, i - NT, rows).bitcast(F32), ALU.subtract)
                        if half == 0:
                            chain.done(last)
                    last.then_inc(s_ol, 1)

            for i in range(2):
                chain.link(dve.memset(pb[i][:, NK:NK + 1], 1.0))
            for i in range(NU + 6):
                if i < NU:
                    weigh(i)
                if 6 <= i:
                    lo_o(i - 6)

            def split_out_lo(n):
                dve.wait_ge(s_whi, 8 + n + 1)
                if n >= 2:
                    dve.wait_ge(s_wo, NT * (n - 1))
                dve.tensor_tensor(w_lo[n % 2][:, :, :], w_raw[n % 2][:, :, :], w_hi[n % 2][:, :, :].bitcast(F32),
                                  ALU.subtract).then_inc(s_wlo, 1)

            split_out_lo(0)
            for s, (n, t) in enumerate(wsteps):
                if t == 2 and n + 1 < D // CG:
                    split_out_lo(n + 1)
                r = ROWS[t]
                if n == 0:
                    dve.wait_ge(s_xr[t], 32)
                dve.wait_ge(s_wo, s + 1)
                dst = xmid[0:r, t, n * CG:n * CG + CG]
                dve.tensor_tensor(dst, wide_ps(s)[0:r, 0:CG], dst, ALU.add).then_inc(s_xm, 1)

            dve.wait_ge(s_wr, 48)
            dve.wait_ge(s_tbl, 1)

            def copy_logits(t):
                dve.wait_ge(s_lgp, t + 1)
                dve.tensor_copy(lg[0:ROWS[t], t, :], wide_ps(t)[0:ROWS[t], 0:NGRP + NE]).then_inc(s_lg, 1)

            for t in range(NT):
                r = ROWS[t]
                c = slice(t % 2, t % 2 + 1)
                dve.wait_ge(s_ssq2, t + 1)
                dve.tensor_scalar(ss[0:r, c], ss[0:r, c], 1.0 / D, EPS, ALU.mult, ALU.add).then_inc(s_ms2, 1)
                dve.wait_ge(s_rms2, t + 1)
                chain.link(dve.reciprocal(rs[0:r, c], rs[0:r, c]))
                if t >= 2:
                    dve.wait_ge(s_n2T, t - 1)
                    dve.wait_ge(s_nst[t % 2], 16 * (t // 2))
                dve.scalar_tensor_tensor(out=xg[t % 2][0:r, :], in0=xmid[0:r, t, :], scalar=rs[0:r, c],
                                         in1=gffn[0:r, :], op0=ALU.mult, op1=ALU.mult).then_inc(s_n2, 1)
                if t >= 1:
                    copy_logits(t - 1)
            copy_logits(LAST)
            dve.wait_ge(s_lg, NT)

            def wide(ap, n):
                return ap.rearrange("p (a x) -> p a x", x=1).to_broadcast([P, ap.shape[1], n])

            def over(ap, n):
                return ap.rearrange("p (x a) -> p x a", x=1).to_broadcast([P, n, ap.shape[1]])

            def first_best(out, best, values, steps_, n):
                chain.link(dve.reduce_max(best, values, axis=AXX))
                chain.link(dve.tensor_tensor(out, values, wide(best, n), ALU.is_equal))
                chain.link(dve.tensor_tensor(out, out, over(steps_[:, :], NT), ALU.mult))
                chain.link(dve.tensor_reduce(rsum[:, :], out, axis=AXX, op=ALU.min))
                chain.link(dve.tensor_tensor(out, over(steps_[:, :], NT), wide(rsum[:, :], n), ALU.is_equal))

            first_best(goh[:, :, :], gmx[:, :], lg[:, :, 0:NGRP], io4, NGRP)
            dve.tensor_tensor(gex[:, :, :], lg[:, :, 0:NGRP], wide(gmx[:, :], NGRP), ALU.subtract).then_inc(s_gx, 1)
            for g in range(NGRP):
                part = lg[:, :, NGRP + EPG * g:NGRP + EPG * (g + 1)]
                chain.link(dve.tensor_tensor((le if g == 0 else tmp8)[:, :, :], part, wide(goh[:, :, g], EPG), ALU.mult))
                if g:
                    chain.link(dve.tensor_tensor(le[:, :, :], le[:, :, :], tmp8[:, :, :], ALU.add))
            first_best(oh[:, 0, :, :], mx[:, 0, :], le[:, :, :], io8, EPG)
            chain.link(dve.scalar_tensor_tensor(out=le[:, :, :], in0=oh[:, 0, :, :], scalar=-3.0e38, in1=le[:, :, :],
                                                op0=ALU.mult, op1=ALU.add))
            first_best(oh[:, 1, :, :], mx[:, 1, :], le[:, :, :], io8, EPG)
            dve.tensor_tensor(gt[:, 1, :], mx[:, 1, :], mx[:, 0, :], ALU.subtract).then_inc(s_gx, 1)
            chain.link(dve.tensor_scalar(valid[:, :], tok[:, :], 0.0, None, ALU.is_lt))
            chain.link(dve.tensor_tensor(goh[:, :, :], goh[:, :, :], wide(valid[:, :], NGRP), ALU.mult))
            for k in range(2):
                for g in range(NGRP):
                    chain.done(dve.tensor_tensor(ek[:, k, :, EPG * g:EPG * (g + 1)], oh[:, k, :, :], wide(goh[:, :, g], EPG),
                                                 ALU.mult))
            chain.settle()
            dve.tensor_tensor(eb[:, :, :], ek[:, 0, :, :], ek[:, 1, :, :], ALU.add).then_inc(s_eb, 1)
            dve.wait_ge(s_ge, 2)
            chain.link(dve.reduce_sum(gw[:, :], gex[:, :, :], axis=AXX))
            chain.link(dve.reciprocal(gw[:, :], gw[:, :]))
            chain.link(dve.tensor_scalar(gt[:, 0, :], gt[:, 1, :], 1.0, None, ALU.add))
            chain.link(dve.reciprocal(gt[:, 0, :], gt[:, 0, :]))
            chain.link(dve.tensor_tensor(gt[:, 0, :], gt[:, 0, :], gw[:, :], ALU.mult))
            chain.link(dve.tensor_tensor(gt[:, 1, :], gt[:, 1, :], gt[:, 0, :], ALU.mult))
            dve.wait_ge(s_rkp, 1)
            totals = bank[:, 7, 0:NT * NE].rearrange("p (t e) -> p t e", t=NT)
            chain.link(dve.memset(cum[:, 0, :], 0.0))
            for t in range(1, NT):
                chain.link(dve.tensor_tensor(cum[:, t, :], totals[:, t - 1, :], cum[:, t - 1, :], ALU.add))
            chain.link(dve.tensor_tensor(cnt[:, :], totals[:, LAST, :], cum[:, LAST, :], ALU.add))
            chain.link(dve.tensor_tensor(cum[:, :, :], bank[:, 6, 0:NT * NE].rearrange("p (t e) -> p t e", t=NT),
                                         cum[:, :, :], ALU.add))
            chain.link(dve.tensor_tensor(cmp_[:, :, :], wide(cnt[:, :], OVMAX), over(jt[:, :], NE), ALU.is_gt))
            chain.link(dve.reduce_sum(nov[:, :], cmp_[:, :, :], axis=AXX))
            chain.link(dve.tensor_tensor_scan(ovend[:, :], nov[:, :], nov[:, :], 0.0, ALU.add, ALU.bypass))
            chain.link(dve.tensor_tensor(ovst[:, :], ovend[:, :], nov[:, :], ALU.subtract))

            def picked(out, values):
                for k in range(2):
                    chain.link(dve.tensor_tensor(eb2[:, :, :], ek[:, k, :, :], values, ALU.mult))
                    chain.link(dve.reduce_sum(out[:, k, :], eb2[:, :, :], axis=AXX))

            eb2 = eb
            picked(rk, cum[:, :, :])
            picked(eid, over(io128[:, 0:NE], NT))
            picked(ovs, over(ovst[:, :], NT))
            flat = [x[:, :, :].rearrange("p k t -> p (k t)") for x in (rk, bk, rw, cl, eid, ovs)]
            rk_, bk_, rw_, cl_, eid_, ovs_ = flat
            part = cmp_[:, 0:2 * NT, :]
            chain.link(dve.tensor_tensor(part, wide(rk_, OVMAX), over(jt[:, :], 2 * NT), ALU.is_ge))
            chain.link(dve.reduce_sum(bk_, part, axis=AXX))
            chain.link(dve.scalar_tensor_tensor(out=rw_, in0=bk_, scalar=-float(CAP), in1=rk_, op0=ALU.mult, op1=ALU.add))
            chain.link(dve.tensor_tensor(cl_, ovs_, bk_, ALU.add))
            chain.link(dve.tensor_tensor(cl_, cl_, eid_, ALU.subtract))
            chain.link(dve.tensor_scalar(cl_, cl_, float(NE - 1), None, ALU.add))
            chain.link(dve.tensor_scalar(ovs_, bk_, 0.0, None, ALU.is_gt))
            chain.link(dve.tensor_tensor(cl_, cl_, ovs_, ALU.mult))
            chain.link(dve.tensor_tensor(cl_, cl_, eid_, ALU.add))
            for k in range(2):
                chain.done(dve.tensor_tensor(row_oh[:, :, k, :], over(io128[:, 0:CAP], NT), wide(rw[:, k, :], CAP), ALU.is_equal))
                chain.done(dve.tensor_tensor(col_oh[:, :, k, 0:NCOL], over(io128[:, 0:NCOL], NT), wide(cl[:, k, :], NCOL),
                                             ALU.is_equal))
            chain.settle()
            for k in range(2):
                chain.done(dve.tensor_tensor(row_oh[:, :, k, :], row_oh[:, :, k, :], wide(valid[:, :], CAP), ALU.mult))
                chain.done(dve.tensor_tensor(col_oh[:, :, k, NCOL:2 * NCOL], col_oh[:, :, k, 0:NCOL], wide(gt[:, k, :], NCOL),
                                             ALU.mult))
            chain.settle()
            for k in range(2):
                last = dve.tensor_tensor(col_oh[:, :, k, 0:NCOL], col_oh[:, :, k, 0:NCOL], wide(tok[:, :], NCOL), ALU.mult)
                if k == 0:
                    chain.done(last)
            last.then_inc(s_ohr, 1)
            chain.link(dve.tensor_copy(ovm[0:1, OVB:OVB + 1], ovend[0:1, NE - 1:NE]))
            for o in range(OVB):
                chain.link(dve.tensor_scalar(nov[0:1, :], ovend[0:1, :], float(o), 0.0, ALU.is_le, ALU.add,
                                             accum_out=ovm[0:1, o:o + 1]))
            chain.link(dve.tensor_scalar(ovm[0:1, 0:OVB], ovm[0:1, 0:OVB], float(NE - 1), None, ALU.min))
            chain.link(dve.tensor_copy(ovmi[0:1, 0:OVB + 1], ovm[0:1, 0:OVB + 1]))
            dve.wait_ge(s_tbp, 1)
            chain.link(dve.tensor_scalar(vld[:, :], bank[0:CAP, 5, 0:NCOL], 0.0, None, ALU.is_lt))
            chain.link(dve.tensor_scalar(tabf[:, :], bank[0:CAP, 5, 0:NCOL], prow[0:CAP, :], None, ALU.add))
            chain.link(dve.scalar_tensor_tensor(out=tabf[:, :], in0=vld[:, :], scalar=nprow[0:CAP, :], in1=tabf[:, :],
                                                op0=ALU.mult, op1=ALU.add))
            chain.link(dve.tensor_copy(gtab[:, :], bank[0:CAP, 5, NCOL:2 * NCOL]))
            dve.tensor_copy(tab[:, :], tabf[:, :]).then_inc(s_tab, 1)
            dve.wait_ge(s_tab, 1)
            for b in range(2):
                dve.tensor_copy(gidx[b][:, :], tab[:, b:b + 1]).then_inc(s_ix, 1)

            def block_dve(i, b):
                early = type(b) is int and b < 2
                dve.wait_ge(s_gl[i], 16 * (b // 2 + 1) if type(b) is int else 8 * (b - i) + 16)
                dve.tensor_copy(gidx[i][:, :], tab[:, bass.ds(b + 2, 1)]).then_inc(s_ix, 1)
                if not early:
                    dve.wait_ge(s_sc, 16 * b - 16)
                    dve.wait_ge(s_ya, b - 1)
                chain_free = dve.tensor_copy(sidx[i][:, :], tab[:, bass.ds(b, 1)])
                chain_free.then_inc(s_sx2, 1)
                dve.tensor_copy(gcol[i][:, :], gtab[:, bass.ds(b, 1)]).then_inc(s_sx, 1)
                dve.wait_ge(s_up, b + 1)
                dve.wait_ge(s_si, b + 1)
                if not early:
                    dve.wait_ge(s_dp, 2 * b - 2)
                dve.tensor_tensor(hT[i][:, :, :], up_ps(i), sgl[i][:, :, :], ALU.mult).then_inc(s_h, 1)
                dve.wait_ge(s_dp, 2 * b + 2)
                dve.wait_ge(s_sx, b + 1)
                dve.tensor_scalar(yo[i][:, 512:D], bank[0:CAP, 7, :], gcol[i][:, 0:1], None, ALU.mult).then_inc(s_yd, 1)

            blocks(dve, block_dve)

        @block.tensor
        def _(pe):
            def transpose_x(t):
                r = ROWS[t]
                pe.wait_ge(s_xs, t + 1)
                if t == 0:
                    pe.wait_ge(s_ident, 1)
                else:
                    pe.wait_ge(s_xh, t)
                    pe.wait_ge(s_xl, t)
                for k in range(KT):
                    last = pe.transpose(xT_ps[:, k, 0:r], xt[t % 3][0:r, k * P:(k + 1) * P], ident[0:r, 0:r])
                last.then_inc(s_xT, 1)

            def freed(s):
                if s < NQK:
                    pe.wait_ge(s_kn, s + 1)
                else:
                    pe.wait_ge(s_v, s - NQK + 1)

            def project(s):
                kind, half, t = steps[s]
                r, n = ROWS[t], s // NT
                if s < NT:
                    pe.wait_ge(s_xl, t + 1)
                if t == 0:
                    pe.wait_ge(s_whi, n + 1)
                    pe.wait_ge(s_wlo, n + 1)
                if s >= 4:
                    freed(s - 4)
                for k in range(KT):
                    for j, (a, b) in enumerate(((xh, w_hi), (xh, w_lo), (xl, w_hi))):
                        last = pe.matmul(proj_ps(s)[0:r, :], a[:, k, row0(t):row0(t) + r], b[n % 2][:, k, :],
                                         start=(k == 0 and j == 0), stop=(k == KT - 1 and j == 2))
                last.then_inc(s_pr, 1)

            def transpose_heads(s):
                r = ROWS[steps[s][2]]
                pe.wait_ge(s_kn, s + 1)
                if s >= 2:
                    pe.wait_ge(s_ke, s - 1)
                for c in range(2):
                    last = pe.transpose(head_ps(s)[:, c, 0:r], kn[s % NKN][0:r, c * P:(c + 1) * P], ident[0:r, 0:r])
                last.then_inc(s_kt, 1)

            transpose_x(0)
            for s in range(NS + 2):
                if s + 1 < NT:
                    transpose_x(s + 1)
                if s < NS:
                    project(s)
                if 2 <= s < NQK + 2:
                    transpose_heads(s - 2)

            pe.wait_ge(s_hld, 16)
            pe.wait_ge(s_ke, NQK)
            n = DB * HIST
            for g in range(NG):
                last = pe.transpose(bank[:, 6, g * n:(g + 1) * n], hist[0:n, g * P:(g + 1) * P], ident[0:n, 0:n])
            last.then_inc(s_ht, 1)
            for i, (g, piece) in enumerate(usteps):
                s, n = NS + i, 6 + g // 2
                lo, cols = PIECES[piece]
                if i == 0 or i == NUS // 2:
                    pe.wait_ge(s_whi, n + 1)
                    pe.wait_ge(s_wlo, n + 1)
                if i < 4:
                    freed(s - 4)
                else:
                    pe.wait_ge(s_uc, u_copies(i - 4))
                c = (g % 2) * P
                for k in range(KT):
                    for j, (a, b) in enumerate(((w_hi, xh), (w_hi, xl), (w_lo, xh))):
                        last = pe.matmul(wide_ps(s)[:, 0:cols], a[n % 2][:, k, c:c + P], b[:, k, lo:lo + cols],
                                         start=(k == 0 and j == 0), stop=(k == KT - 1 and j == 2))
                last.then_inc(s_pr, 1)
            pe.wait_ge(s_uc, u_copies(NUS - 1))
            for g in range(NG):
                pe.transpose(bank[0:TAILP, 6, g * P:(g + 1) * P], u_ext[:, g, TP:16 + TP], ident[:, :])
            for g in range(NG):
                last = pe.transpose(bank[0:TS, 7, g * P:(g + 1) * P], us_cols[:, g, :], ident[:, :])
            last.then_inc(s_ut, 1)
            pe.wait_ge(s_cst2, 16 * NCONST)
            for i, (g, piece) in enumerate(usteps):
                lo, cols = PIECES[piece]
                pe.wait_ge(s_d, g + 1)
                if i >= 4:
                    pe.wait_ge(s_pl, i - 3)
                pe.matmul(wide_ps(NS + NUS + i)[:, 0:cols], wp_sb[:, g, :], dT[:, lo:lo + cols],
                          start=True, stop=True).then_inc(s_pm, 1)

            def scores(u):
                kind, w = units[u][0], width(u)
                if u == 0:
                    pe.wait_ge(s_pl, NUS)
                    pe.wait_ge(s_ur, 2)
                if u >= 2:
                    pe.wait_ge(s_sg, u - 1 if kind == "full" else u)
                z = z_ps(u)
                if kind == "full":
                    _, t, h = units[u]
                    rows = slice(64 * (h % 2), 64 * (h % 2) + 64)
                    for lo in range(0, w, 512):
                        n = min(512, w - lo)
                        last = pe.matmul(z[:, lo:lo + n], qT[rows, h // 2, row0(t):row0(t) + P],
                                         kT[rows, h // 2, lo:lo + n], start=True, stop=True)
                elif kind == "tail":
                    for j in range(4):
                        h = 4 * units[u][1] + j
                        rows = slice(64 * (h % 2), 64 * (h % 2) + 64)
                        for lo in range(0, w, 512):
                            n = min(512, w - lo)
                            last = pe.matmul(z[32 * j:32 * j + 32, lo:lo + n],
                                             qT[rows, h // 2, row0(LAST):row0(LAST) + TAIL_Q],
                                             kT[rows, h // 2, lo:lo + n], start=True, stop=True)
                else:
                    g = units[u][1]
                    if g == 0:
                        pe.wait_ge(s_qz, 1)
                    for j in range(4):
                        b = 4 * g + j
                        past_keys(b)
                        pe.wait_ge(s_te, key_group(b, HP - 1) + 1)
                        for hp in range(HP):
                            last = pe.matmul(z[32 * j:32 * j + 32, 0:PAST], qz[:, b, hp, :], kTs[:, hp, :],
                                             start=(hp == 0), stop=(hp == HP - 1))
                        last.then_inc(s_kTs, 1)
                        for hp in range(HP):
                            last = pe.matmul(z[32 * j:32 * j + 32, PAST:NKS], qz[:, b, hp, :],
                                             kT[:, hp, row0(LAST):T], start=(hp == 0), stop=(hp == HP - 1))
                last.then_inc(s_z, 1)

            def past_keys(b):
                i = b
                pe.wait_ge(s_kld[i % 2], 16 * NPG * (i // 2 + 1))
                for hp in range(HP):
                    n = key_group(b, hp)
                    pe.wait_ge(s_te, n - 1)
                    for j in range(NPG):
                        last = pe.transpose(t_ps(n)[:, j, :], pg[i % 2][:, j, hp * P:(hp + 1) * P], ident[:, :])
                    last.then_inc(s_t, 1)

            def transpose_weights(u):
                pe.wait_ge(s_am, u + 1)
                lo = NK - width(u)
                for j, group in enumerate(groups(u)):
                    n = first_group(u) + j
                    if n >= 2:
                        pe.wait_ge(s_te, n - 1)
                    for k, (c, keys) in enumerate(group):
                        last = pe.transpose(t_ps(n)[0:keys, k, :], am[u % 2][:, lo + P * c:lo + P * c + keys], ident[:, :])
                    last.then_inc(s_t, 1)

            def sum_values(u):
                kind = units[u][0]
                i, _ = out_of(u)
                pe.wait_ge(s_te, first_group(u) + len(groups(u)))
                if i >= 2 and (kind == "smp" or units[u][-1] == 0):
                    pe.wait_ge(s_ol, i - 1)
                ch = chunks(u)
                if kind == "full":
                    h = units[u][2]
                    for c, keys in ch:
                        last = pe.matmul(o_ps(i)[:, h * HD:(h + 1) * HD], aT[u % 2][0:keys, c, :],
                                         vv[0:keys, c, h * HD:(h + 1) * HD], start=(c == 0), stop=(c == ch[-1][0]))
                    last.then_inc(s_av, 1)
                elif kind == "tail":
                    for j in range(4):
                        h = 4 * units[u][1] + j
                        for c, keys in ch:
                            last = pe.matmul(o_ps(i)[0:TAILP, h * HD:(h + 1) * HD],
                                             aT[u % 2][0:keys, c, 32 * j:32 * j + TAILP],
                                             vv[0:keys, c, h * HD:(h + 1) * HD], start=(c == 0), stop=(c == ch[-1][0]))
                    last.then_inc(s_av, 1)
                else:
                    g = units[u][1]
                    for j in range(4):
                        b = 4 * g + j
                        k = DB + b
                        pe.wait_ge(s_kld[k % 2], 16 * NPG * (k // 2 + 1))
                        for hp in range(HP):
                            col = (j * HP + hp) * 8
                            for c, keys in ch:
                                lhs = pg[k % 2][:, c, hp * P:(hp + 1) * P] if c < NPG else \
                                    vv[0:keys, LAST, hp * P:(hp + 1) * P]
                                last = pe.matmul(o_ps(i)[:, col:col + 8], lhs,
                                                 aT[u % 2][0:keys, c, 32 * j + 8 * hp:32 * j + 8 * hp + 8],
                                                 start=(c == 0), stop=(c == ch[-1][0]))
                        last.then_inc(s_av, 1)

            def transpose_o(u):
                i, ends = out_of(u)
                if ends and i < NT:
                    r = P if i < LAST else TAILP
                    pe.wait_ge(s_os, i + 1)
                    for c in range(HP):
                        last = pe.transpose(o_ps(i)[:, c * P:c * P + r], o_sb[0:r, c * P:(c + 1) * P], ident[0:r, 0:r])
                    last.then_inc(s_oT, 1)

            for i in range(NU + 5):
                if i < NU:
                    scores(i)
                if 2 <= i < NU + 2:
                    transpose_weights(i - 2)
                if 5 <= i < NU + 5:
                    transpose_o(i - 5)
                if 3 <= i < NU + 3:
                    sum_values(i - 3)

            pe.wait_ge(s_ol, NOUT)
            for s, (n, t) in enumerate(wsteps):
                r = ROWS[t]
                if t == 0:
                    pe.wait_ge(s_whi, 8 + n + 1)
                    pe.wait_ge(s_wlo, 8 + n + 1)
                if s >= 4:
                    pe.wait_ge(s_xm, s - 3)
                for k in range(KT):
                    for j, (a, b) in enumerate(((xh, w_hi), (xh, w_lo), (xl, w_hi))):
                        last = pe.matmul(wide_ps(s)[0:r, 0:CG], a[:, k, row0(t):row0(t) + r], b[n % 2][:, k, :],
                                         start=(k == 0 and j == 0), stop=(k == KT - 1 and j == 2))
                last.then_inc(s_wo, 1)

            pe.wait_ge(s_wr, 48)

            def logits(t):
                r = ROWS[t]
                pe.wait_ge(s_n2c, t + 1)
                pe.wait_ge(s_xm, len(wsteps))
                if t >= 4:
                    pe.wait_ge(s_lg, t - 3)
                for k in range(KT):
                    last = pe.matmul(wide_ps(t)[0:r, 0:NGRP + NE], nT[t % 2][:, k, 0:r], w_r[:, k, :],
                                     start=(k == 0), stop=(k == KT - 1))
                last.then_inc(s_lgp, 1)

            for t in range(NT):
                r = ROWS[t]
                pe.wait_ge(s_n2, t + 1)
                if t >= 1:
                    pe.wait_ge(s_n2c, t)
                for k in range(KT):
                    last = pe.transpose(xT_ps[:, k, 0:r], xg[t % 2][0:r, k * P:(k + 1) * P], ident[0:r, 0:r])
                last.then_inc(s_n2T, 1)
                if t >= 1:
                    logits(t - 1)
            logits(LAST)
            pe.wait_ge(s_eb, 1)
            marks = eb[:, :, :].rearrange("p t e -> p (t e)")
            pe.matmul(bank[:, 6, 0:NT * NE], before[:, :], marks, start=True, stop=True)
            pe.matmul(bank[:, 7, 0:NT * NE], ones[:, :], marks, start=True, stop=True).then_inc(s_rkp, 1)
            pe.wait_ge(s_ohr, 1)
            for t in range(NT):
                for k in range(2):
                    last = pe.matmul(bank[0:CAP, 5, 0:2 * NCOL], row_oh[:, t, k, :], col_oh[:, t, k, :],
                                     start=(t == 0 and k == 0), stop=(t == LAST and k == 1))
            last.then_inc(s_tbp, 1)

            def transpose_block(i, b, loaded):
                pe.wait_ge(s_gl[i], loaded)
                if not (type(b) is int and b == 0):
                    pe.wait_ge(s_xc, b)
                for k in range(KT):
                    last = pe.transpose(xT_ps[:, k, 0:CAP], xg[i][0:CAP, k * P:(k + 1) * P], ident[0:CAP, 0:CAP])
                last.then_inc(s_xt, 1)

            def block_pe(i, b):
                early = type(b) is int and b < 2
                turn = b // 2 if type(b) is int else None
                loads = 16 * (turn + 1) if turn is not None else 8 * (b - i) + 16
                next_gather = 16 * ((b + 1) // 2 + 1) if turn is not None else 8 * (b - i) + 16 + 16 * i
                pe.wait_ge(s_xc, b + 1)
                for j, (buf, ps, done) in enumerate(((wg, gate_ps(i), s_gp), (wu, up_ps(i), s_up))):
                    pe.wait_ge(s_wl[i][j], loads)
                    if not early:
                        pe.wait_ge(s_h, b - 1)
                    for ft in range(FT):
                        for k in range(KT):
                            last = pe.matmul(ps[:, ft, :], buf[i][:, k, ft * P:(ft + 1) * P], xTe[i][:, k, :],
                                             start=(k == 0), stop=(k == KT - 1))
                    last.then_inc(done, 1)
                transpose_block(1 - i, b + 1, next_gather)
                pe.wait_ge(s_h, b + 1)
                pe.wait_ge(s_wl[i][2], loads)
                for half, (n, done) in enumerate(((6, s_ya), (7, s_yd))):
                    if not (type(b) is int and b == 0):
                        pe.wait_ge(done, b)
                    for ft in range(FT):
                        last = pe.matmul(bank[0:CAP, n, :], hT[i][:, ft, :], wd[i][:, ft, 512 * half:512 * half + 512],
                                         start=(ft == 0), stop=(ft == FT - 1))
                    last.then_inc(s_dp, 1)

            transpose_block(0, 0, 16)
            blocks(pe, block_pe)


_OUTS = {"y_all": (NY, D), "k_all": (T, AW), "v_all": (T, AW), "pool_p": (HIST, PW), "pool_s": (DB, HIST, PW)}
_LAYERED = ("cache_k", "cache_v", "state_pool", "w_in", "w_pool", "w_out", "w_group", "w_expert", "w_gate", "w_up",
            "w_down")


def kernel(**inputs):
    import numpy as np
    import concourse.bacc as bacc
    from concourse.bass_utils import run_bass_kernel_spmd

    nc = bacc.Bacc("TRN2", target_bir_lowering=False, num_devices=1)
    arrays, args = {}, {}
    for name, value in inputs.items():
        a = np.ascontiguousarray(value)
        arrays[f"in_{name}"] = a
        ap = nc.dram_tensor(f"in_{name}", a.shape, mybir.dt.from_np(a.dtype), kind="ExternalInput").ap()
        args[name] = ap[0] if name in _LAYERED else ap
    for name, shape in _OUTS.items():
        args[name] = nc.dram_tensor(f"out_{name}", shape, F32, kind="ExternalOutput").ap()
    hybrid_step(nc, **args)
    r = run_bass_kernel_spmd(nc, [arrays], core_ids=[0]).results[0]
    y, k, v = r["out_y_all"], r["out_k_all"], r["out_v_all"]
    return (y[META:TP].reshape(1, SEQ, D), y[TP:T].reshape(DB, DS, D),
            k[:TP].reshape(1, 1, TP, H, HD), v[:TP].reshape(1, 1, TP, H, HD), r["out_pool_p"].reshape(1, 1, HIST, PW),
            k[TP:].reshape(1, DB, DS, H, HD), v[TP:].reshape(1, DB, DS, H, HD),
            r["out_pool_s"].reshape(1, DB, HIST, PW))
```

```python
import math

import concourse.bass as bass
from concourse import mybir

F32 = mybir.dt.float32
F32R = mybir.dt.float32r
I32 = mybir.dt.int32
U32 = mybir.dt.uint32
ACT = mybir.ActivationFunctionType
ALU = mybir.AluOpType
AXX = mybir.AxisListType.X

P = 128
D = 1024
KT = D // P
SEQ, META = 1024, 16
TP = SEQ + META
DB, DS = 8, 4
TS = DB * DS
T = TP + TS
NT = -(-T // P)
ROWS = [min(P, T - P * t) for t in range(NT)]
LAST = NT - 1
TAILP = TP - P * LAST
H, HD = 8, 64
HP = H // 2
PW = 512
AW = H * HD
WINDOWS = (2, 4, 8, 16)
NG = len(WINDOWS)
HIST = 15
PAST, PAGE = 512, 128
NPG = PAST // PAGE
EPS = 1e-6
CG = 256
NK = TP
SQ = 2
TAIL_Q = 32
NKS = PAST + ROWS[-1]
PIECES = [(0, 512), (512, 512), (1024, T - 1024)]
NE, NGRP, EPG = 32, 4, 8
F = D // 2
FT = F // P
CAP = 96
OVB = 2 * T // CAP
NBLK = NE + OVB
NCOL = NBLK + 3
OVMAX = -(-T // CAP) - 1
NY = T + CAP
NCONST = 4


def row0(t):
    return P * t


class Chain:

    def __init__(self, eng, sem):
        self.eng, self.sem, self.n = eng, sem, 0

    def done(self, ins):
        self.n += 1
        ins.then_inc(self.sem, 1)
        return self.n

    def settle(self):
        self.eng.wait_ge(self.sem, self.n)

    def link(self, ins):
        self.done(ins)
        self.settle()


def hybrid_step(nc, x_prompt, x_sample, cache_k, cache_v, state_pool, page_table, meta_tokens,
                norm_mix, w_in, g_q, g_k, sb_bias, w_pool, pool_scale, w_out, norm_ffn,
                w_group, w_expert, w_gate, w_up, w_down,
                y_all, k_all, v_all, pool_p, pool_s):
    base = 16512
    end = 229344

    def place(name, shape, dtype, at):
        size = 4
        for n in shape[1:]:
            size *= n
        size = -(-size // 32) * 32
        assert base <= at and at + size <= end, (name, at, size, end)
        return nc.alloc_sbuf_tensor_at(name, shape, dtype, offset=at), at + size

    at_x = base
    xh, at = place("xh", [P, KT, T], F32R, at_x)
    xl, at_w = place("xl", [P, KT, T], F32R, at)
    w_raw, w_hi, w_lo = [], [], []
    at = at_w
    for i in range(2):
        for lst, nm, dt in ((w_raw, "w_raw", F32), (w_hi, "w_hi", F32R), (w_lo, "w_lo", F32R)):
            tns, at = place(f"{nm}{i}", [P, KT, CG], dt, at)
            lst.append(tns)
    at_q = at
    qT, at = place("qT", [P, HP, T], F32, at_q)
    kT, at = place("kT", [P, HP, T], F32, at)
    junk, _ = place("junk", [P, D], F32, at)
    vv, at_m = place("vv", [P, NT, AW], F32, at)
    xt = []
    at = at_m
    for i in range(3):
        tns, at = place(f"xt{i}", [P, D], F32, at)
        xt.append(tns)
    gmix, at = place("gmix", [P, D], F32, at)
    NKN = 3
    sq, kn = [], []
    for i in range(2):
        tns, at = place(f"sq{i}", [P, CG], F32, at)
        sq.append(tns)
    for i in range(NKN):
        tns, at = place(f"kn{i}", [P, CG], F32, at)
        kn.append(tns)
    ss, at = place("ss", [P, 2], F32, at)
    rs, at = place("rs", [P, 2], F32, at)
    hs, at = place("hs", [P, 2, 4], F32, at)
    hr, at = place("hr", [P, 2, 4], F32, at)
    at_c = at
    wp_sb, at = place("wp_sb", [P, NG, P], F32, at_c)
    hist, at = place("hist", [P, PW], F32, at)
    up_rows, at = place("up_rows", [TAILP, PW], F32, at)
    us_rows, at = place("us_rows", [TS, PW], F32, at)
    ident, at = place("ident", [P, P], F32, at)
    gq_bc, at = place("gq_bc", [P, HD], F32, at)
    gk_bc, at = place("gk_bc", [P, HD], F32, at)
    bias_bc, at = place("bias_bc", [P, H], F32, at)
    bias_tail, at = place("bias_tail", [P, 2], F32, at)
    bias_smp, at = place("bias_smp", [P, 1], F32, at)
    diag_mask, at = place("diag_mask", [P, P], F32, at)
    tail_mask, at = place("tail_mask", [P, TAILP], F32, at)
    smp_mask, at = place("smp_mask", [P, DB // SQ, ROWS[-1]], F32, at)
    pscale, at = place("pscale", [P, NG], F32, at)
    rcnt, at = place("rcnt", [P, 16], F32, at)
    pint, at = place("pint", [P, 4], I32, at)
    pflt, at = place("pflt", [P, 8], F32, at)
    col48, at = place("col48", [P, ROWS[-1]], F32, at)
    us_cols, at = place("us_cols", [P, NG, TS], F32, at)
    pt_sb, at = place("pt_sb", [1, DB * NPG], I32, at)
    at_u = at
    u_ext, at = place("u_ext", [P, NG, 16 + TP], F32, at_m)
    es, at = place("es", [P, NG, DB, 20], F32, at)
    assert at <= at_c
    dT, at = place("dT", [P, T], F32, at_w)
    wsum = []
    for i in range(2):
        tns, at = place(f"wsum{i}", [P, 16 + TP], F32, at)
        wsum.append(tns)
    wsmall0, at = place("wsmall0", [P, DB, 20], F32, at)
    wsmall1, at = place("wsmall1", [P, DB, 20], F32, at)
    sg, am, pb, aT = [], [], [], []
    pgv0, at = place("pgv0", [PAGE, NPG, AW], F32, at_w)
    for i in range(2):
        for lst, nm, shape in ((sg, "sg", [P, NK]), (am, "am", [P, NK]), (pb, "pb", [P, NK + 1]),
                               (aT, "aT", [P, NT, P])):
            tns, at = place(f"{nm}{i}", shape, F32, at)
            lst.append(tns)
    o_sb, at = place("o_sb", [P, AW], F32, at)
    assert at <= at_q, (at, at_q)
    pgk = []
    at = at_m
    for i in range(2):
        tns, at = place(f"pgk{i}", [PAGE, NPG, AW], F32, at)
        pgk.append(tns)
    qz, at = place("qz", [P, DB, HP, 32], F32, at)
    assert at <= at_c
    pgv = [pgv0, place("pgv1", [PAGE, NPG, AW], F32, at_c)[0]]
    kTs, at_end = place("kTs", [P, HP, PAST], F32, at_u)
    w_r, at = place("w_r", [P, KT, NGRP + NE], F32, at_u + 4 * D)
    lg, at = place("lg", [P, NT, NGRP + NE], F32, at)
    xmid, at_e = place("xmid", [P, NT, D], F32, at_q)
    def weights(nm, dtype, places):
        shapes = ([P, KT, F], [P, KT, F], [P, FT, D])
        return [place(f"{nm}{j}", shapes[j], dtype, at)[0] for j, at in enumerate(places)]

    size = 4 * KT * F
    e_raw = weights("e_raw", F32, [at_x, at_x + size, at_x + 2 * size])
    e_hi = weights("e_hi", F32R, [at_w, at_w + 2 * size, at_q])
    e_lo = weights("e_lo", F32R, [at_w + size, at_e, at_q + size])
    at_r = at_x + 3 * size
    assert at_w + 3 * size <= at_q and at_q + 2 * size <= at_e
    xg, xeh, xel, yo, gidx, sidx, gcol = [], [], [], [], [], [], []
    at = at_e + size
    for i in range(2):
        for lst, nm, shape, dt in ((xg, "xg", [P, D], F32), (xeh, "xeh", [P, KT, CAP], F32R), (xel, "xel", [P, KT, CAP], F32R),
                                   (gidx, "gidx", [CAP, 1], I32), (sidx, "sidx", [CAP, 1], I32), (gcol, "gcol", [CAP, 1], F32)):
            tns, at = place(f"{nm}{i}", shape, dt, at)
            lst.append(tns)
    assert at <= at_c, (at, at_c)
    at = at_c
    for i in range(2):
        tns, at = place(f"yo{i}", [CAP, D], F32, at)
        yo.append(tns)
    zrow, _ = place("zrow", [CAP, D], F32, at_c)
    row_oh, _ = place("row_oh", [P, NT, 2, CAP], F32, at_u)
    hT_hi, at = place("hT_hi", [P, FT, CAP], F32R, at_u)
    hT_lo, at = place("hT_lo", [P, FT, CAP], F32R, at)
    sgl, at = place("sgl", [CAP, F], F32, at)
    hid, at = place("hid", [CAP, F], F32, at)
    gffn, at = place("gffn", [P, D], F32, at_u)
    nT = [place(f"nT{i}", [P, KT, P], F32, at_e + 4 * D * i)[0] for i in range(2)]
    junk2, at = place("junk2", [P, D], F32, at_e + 8 * D)
    assert at <= at_e + size
    col_oh, at = place("col_oh", [P, NT, 2, 2 * NCOL], F32, at_e)
    assert at <= at_e + size
    small = {}
    at = at_r
    for nm, shape, dt in (("gmx", [P, NT], F32), ("goh", [P, NT, NGRP], F32), ("gex", [P, NT, NGRP], F32),
                          ("gw", [P, NT], F32), ("le", [P, NT, EPG], F32), ("tmp8", [P, NT, EPG], F32),
                          ("oh", [P, 2, NT, EPG], F32), ("mx", [P, 2, NT], F32), ("gt", [P, 2, NT], F32),
                          ("ek", [P, 2, NT, NE], F32), ("eb", [P, NT, NE], F32), ("cum", [P, NT, NE], F32),
                          ("rk", [P, 2, NT], F32), ("eid", [P, 2, NT], F32), ("ovs", [P, 2, NT], F32),
                          ("bk", [P, 2, NT], F32), ("rw", [P, 2, NT], F32), ("cl", [P, 2, NT], F32),
                          ("cnt", [P, NE], F32), ("nov", [P, NE], F32), ("ovend", [P, NE], F32), ("ovst", [P, NE], F32),
                          ("tab", [CAP, NCOL], I32), ("tabf", [CAP, NCOL], F32), ("vld", [CAP, NCOL], F32),
                          ("gtab", [CAP, NCOL], F32), ("valid", [P, NT], F32), ("tok", [P, NT], F32),
                          ("io4", [P, NGRP], F32), ("io8", [P, EPG], F32), ("io128", [P, P], F32), ("jt", [P, OVMAX], F32),
                          ("prow", [P, 1], F32), ("nprow", [P, 1], F32), ("before", [P, P], F32), ("ones", [P, P], F32),
                          ("cmp", [P, NE, OVMAX], F32), ("ovm", [1, 32], F32), ("ovmi", [1, 32], I32), ("rsum", [P, NT], F32)):
        small[nm], at = place(nm, shape, dt, at)
    assert at <= at_w, (at, at_w)
    (gmx, goh, gex, gw, le, tmp8, oh, mx, gt, ek, eb, cum, rk, eid, ovs, bk, rw, cl, cnt, nov, ovend, ovst,
     tab, tabf, vld, gtab, valid, tok, io4, io8, io128, jt, prow, nprow, before, ones, cmp_, ovm, ovmi, rsum) = small.values()

    bank = nc.alloc_psum_tensor("bank", [P, 8, 512], F32)
    xT_ps = bank[:, 0:2, :].rearrange("p b (c n) -> p (b c) n", n=P)

    def proj_ps(s):
        return bank[:, 2 + s % 4, 0:CG]

    def head_ps(s):
        return bank[:, 6 + s % 2, 0:2 * P].rearrange("p (c n) -> p c n", n=P)


    def z_ps(u):
        kind = units[u][0]
        b0 = 0 if kind == "tail" else 2 * (u % 2)
        return bank[:, b0:b0 + (3 if kind == "tail" else 2), :].rearrange("p b n -> p (b n)")

    def t_ps(n):
        return bank[:, 4 + n % 2, :].rearrange("p (c n) -> p c n", n=P)

    units = []
    NSG = DB // SQ
    for t in range(LAST):
        for h in range(H):
            if h == H // 2 and LAST - 1 - NSG <= t < LAST - 1:
                units.append(("smp", t - (LAST - 1 - NSG)))
            units.append(("full", t, h))
    units += [("tail", 0), ("tail", 1)]
    NU = len(units)

    def width(u):
        kind = units[u][0]
        return P * (units[u][1] + 1) if kind == "full" else TP if kind == "tail" else NKS

    def height(u):
        return 32 * SQ if units[u][0] == "smp" else P

    def chunks(u):
        return [(c, min(P, width(u) - P * c)) for c in range(-(-width(u) // P))]

    def groups(u):
        ch = chunks(u)
        return [ch[i:i + 4] for i in range(0, len(ch), 4)]

    first_of_weights, first_of_keys, count = {}, {}, 0
    for i in range(NU + 2):
        if i < NU and units[i][0] == "smp":
            first_of_keys[units[i][1]] = count
            count += SQ * HP
        if i >= 2:
            first_of_weights[i - 2] = count
            count += len(groups(i - 2))

    def first_group(u):
        return first_of_weights[u]

    def key_group(b, hp):
        return first_of_keys[b // SQ] + (b % SQ) * HP + hp

    def summed_at(u):
        return sum(SQ if unit[0] == "smp" else 1 for unit in units[:u + 1])

    def smp_summed(b):
        return summed_at(units.index(("smp", b // SQ)) - 1) + b % SQ + 1

    def smp_out(x, g, rows):
        lo = TP + SQ * DS * g
        return x[rows, HP:KT, lo:lo + SQ * DS].rearrange("p c (b j) -> p b c j", j=DS)

    def smp_in(i, half, rows):
        v = o_ps(i)[rows, :].rearrange("p (c b e) -> p b c e", c=HP, e=32)
        return v[:, 0:SQ, :, DS * half:DS * half + DS]

    def use_of(unit):
        return ("smp", unit[1]) if unit[0] == "smp" else ("tile", unit[1] if unit[0] == "full" else LAST)

    outs, out_bank, freed_by, last_in = [], {}, {}, {}
    for u, unit in enumerate(units):
        use = use_of(unit)
        if use not in out_bank:
            out_bank[use] = use[1] % 2 if use[0] == "tile" else 1 - units[u - 1][1] % 2
            freed_by[use] = last_in.get(out_bank[use])
            last_in[out_bank[use]] = use
        if use not in [use_of(later) for later in units[u + 1:]]:
            outs.append(use)
    NOUT = len(outs)

    def out_of(u):
        use = use_of(units[u])
        return outs.index(use), use not in [use_of(later) for later in units[u + 1:]]

    def o_ps(i):
        return bank[:, 6 + out_bank[outs[i]], :]

    def tile_of(i):
        return outs[i][1] if outs[i][0] == "tile" else None

    def out_rows(i):
        return 32 * SQ if tile_of(i) is None else P if tile_of(i) < LAST else TAILP

    def sem(name):
        return nc.alloc_semaphore(name)

    s_const = sem("const_loaded")
    s_ident = sem("ident_ready")
    s_xld = [sem(f"x_loaded{i}") for i in range(3)]
    s_wld = [sem(f"w_loaded{i}") for i in range(2)]
    s_whi = sem("w_hi_ready")
    s_wlo = sem("w_lo_ready")
    s_ssq = sem("sumsq_ready")
    s_ms = sem("meansq_ready")
    s_rms = sem("rms_ready")
    s_xs = sem("x_normed")
    s_xT = sem("x_transposed")
    s_xh = sem("x_hi_ready")
    s_xl = sem("x_lo_ready")
    s_pr = sem("projected")
    s_sq = sem("head_squares")
    s_hms = sem("head_meansq")
    s_hrms = sem("head_rms")
    s_kn = sem("qk_normed")
    s_kt = sem("qk_transposed")
    s_ke = sem("qk_copied")
    s_v = sem("v_copied")
    s_kst = [sem(f"k_stored{i}") for i in range(NKN)]
    s_vst = sem("v_stored")
    s_cst2 = sem("more_const_loaded")
    s_mask = sem("masks_ready")
    s_hld = sem("history_loaded")
    s_ht = sem("history_transposed")
    s_uc = sem("u_copied")
    s_ut = sem("u_rows_transposed")
    s_ur = sem("u_rows_copied")
    s_ust = sem("u_rows_stored")
    s_uscr = sem("u_rows_in_scratch")
    s_d = sem("pool_diff_ready")
    s_pm = sem("pool_product")
    s_ph = sem("pool_hi_ready")
    s_pl = sem("pool_lo_ready")
    s_pad = sem("zero_history")
    s_z = sem("scores")
    s_sg = sem("sigmoid_ready")
    s_am = sem("weights_ready")
    s_t = sem("banks_transposed")
    s_te = sem("banks_copied")
    s_av = sem("values_summed")
    s_os = sem("o_copied")
    s_oT = sem("o_transposed")
    s_oh = sem("o_hi_ready")
    s_oh2 = sem("sample_o_hi_ready")
    s_ol = sem("o_lo_ready")
    s_kld = [sem(f"k_page_loaded{i}") for i in range(2)]
    s_vld = [sem(f"v_page_loaded{i}") for i in range(2)]
    s_kTs = sem("past_k_copied")
    s_qz = sem("q_spread")
    s_xr = [sem(f"residual_loaded{t}") for t in range(NT)]
    s_wo = sem("w_out_product")
    s_xm = sem("residual_added")
    s_wr = sem("router_weights_loaded")
    s_tbl = sem("router_tables_ready")
    s_zr = sem("zero_rows_ready")
    s_ssq2 = sem("sumsq2_ready")
    s_ms2 = sem("meansq2_ready")
    s_rms2 = sem("rms2_ready")
    s_n2 = sem("ffn_normed")
    s_n2T = sem("ffn_transposed")
    s_n2c = sem("ffn_copied")
    s_lgp = sem("logits_product")
    s_lg = sem("logits_ready")
    s_nst = [sem(f"rows_stored{i}") for i in range(2)]
    s_yst = sem("residual_stored")
    s_gx = sem("group_shifted")
    s_ge = sem("group_exp")
    s_ex = sem("pair_exp")
    s_eb = sem("experts_marked")
    s_rkp = sem("ranks_product")
    s_ohr = sem("slot_one_hots")
    s_tbp = sem("tables_product")
    s_tab = sem("tables_ready")
    s_wl = [sem(f"{nm}_loaded") for nm in ("gate", "up", "down")]
    s_eh = [sem(f"{nm}_hi_ready") for nm in ("gate", "up", "down")]
    s_el = [sem(f"{nm}_lo_ready") for nm in ("gate", "up", "down")]
    s_ix = sem("gather_rows_named")
    s_sx = sem("block_gates_ready")
    s_sx2 = sem("scatter_rows_named")
    s_gl = [sem(f"gathered{i}") for i in range(2)]
    s_xt = sem("block_transposed")
    s_xe = sem("block_hi_ready")
    s_xc = sem("block_lo_ready")
    s_hT = sem("hidden_transposed")
    s_hh = sem("hidden_hi_ready")
    s_hl = sem("hidden_lo_ready")
    s_gp = sem("gate_product")
    s_up = sem("up_product")
    s_si = sem("silu_ready")
    s_h = sem("hidden_ready")
    s_dp = sem("down_product")
    s_ya = sem("left_half_gated")
    s_yd = sem("right_half_gated")
    s_sc = sem("block_scattered")
    s_dve = sem("dve_chain")
    s_act = sem("act_chain")
    s_pool = sem("pool_chain")

    order = [("k", 0), ("k", 1), ("q", 0), ("q", 1), ("v", 0), ("v", 1), ("u", 0), ("u", 1)]
    first_col = {"u": 0, "q": PW, "k": PW + AW, "v": PW + 2 * AW}
    steps = [(kind, half, t) for kind, half in order[:6] for t in range(NT)]
    NS = len(steps)
    qk_steps = [s for s in range(NS) if steps[s][0] in "qk"]
    NQK = len(qk_steps)
    assert qk_steps == list(range(NQK))

    usteps = [(g, piece) for g in range(NG) for piece in range(3)]
    NUS = len(usteps)
    assert D // CG == 4
    wsteps = [(n, t) for n in range(2) for t in range(NT)]
    for i in range(NT + 2):
        wsteps += [(2, i)] if i < NT else []
        wsteps += [(3, i - 2)] if i >= 2 else []

    def tile_done(t):
        return wsteps.index((3, t)) + 1

    def out_ps(s):
        return bank[:, s % 4, 0:CG]

    def logit_ps(t):
        return bank[:, 6 + t % 2, 0:NGRP + NE]

    def norm_ps(t):
        return bank[:, 4:6, :].rearrange("p b (c n) -> p (b c) n", n=P)

    def wide_ps(s):
        return bank[:, 2 + s % 4, :]

    def u_copies(i):
        return 1 + i + 1 + 2 * ((i + 1) // 3)

    u_scr = nc.dram_tensor("u_scr", [TS, PW], F32).ap()
    w_in_v = w_in.rearrange("(kt p) e -> p kt e", p=P)
    n_scr = nc.dram_tensor("n_scr", [NY, D], F32).ap()
    gate_v = w_gate.rearrange("e (kt p) f -> e p kt f", p=P)
    up_v = w_up.rearrange("e (kt p) f -> e p kt f", p=P)
    down_v = w_down.rearrange("e (ft p) d -> e p ft d", p=P)
    w_out_v = w_out.rearrange("(kt p) e -> p kt e", p=P)

    def gate_ps(i):
        return bank[0:CAP, 2 + i, :]

    up_ps = bank[0:CAP, 4, :]
    hT_ps = bank[:, 5, 0:FT * CAP].rearrange("p (f n) -> p f n", f=FT)

    def since(eng, sem, value):
        if not (type(value) is int and value <= 0):
            eng.wait_ge(sem, value)

    def blocks(eng, first, body, last, further):
        first()
        for b in range(2):
            body(b, b)
        with eng.Fori(1, NE // 2 - 1) as i:
            for k in range(2):
                body(k, 2 * i + k)
        for b in range(NE - 2, NE):
            last(b)
        eng.wait_ge(s_tab, 1)
        n_over = eng.value_load(ovmi[0:1, OVB:OVB + 1], min_val=0, max_val=OVB)
        with eng.Fori(0, OVB // 2) as i:
            for k in range(2):
                with eng.If(n_over > 2 * i + k):
                    further(k, 2 * i + k + NE)

    blk = nc.Block()

    with nc.allow_non_contiguous_dma(reason="small vectors and broadcasts"), blk as block:

        @block.sync
        def _(sp):
            def load_x(t):
                if t >= 3:
                    sp.wait_ge(s_xT, t - 2)
                lo = P * t - META
                if t == 0:
                    sp.dma_start(xt[0][0:META, :], meta_tokens).then_inc(s_xld[0], 16)
                    sp.dma_start(xt[0][META:P, :], x_prompt[0, 0:P - META, :]).then_inc(s_xld[0], 16)
                elif t < LAST:
                    sp.dma_start(xt[t % 3][:, :], x_prompt[0, lo:lo + P, :]).then_inc(s_xld[t % 3], 32)
                else:
                    sp.dma_start(xt[t % 3][0:TAILP, :], x_prompt[0, lo:SEQ, :]).then_inc(s_xld[t % 3], 16)
                    sp.dma_start(xt[t % 3][TAILP:TAILP + TS, :],
                                 x_sample.rearrange("b s d -> (b s) d")).then_inc(s_xld[t % 3], 16)

            def load_w(n):
                kind, half = order[n]
                c = first_col[kind] + half * CG
                if n >= 2:
                    sp.wait_ge(s_whi, n - 1)
                    sp.wait_ge(s_wlo, n - 1)
                sp.dma_start(w_raw[n % 2][:, :, :], w_in_v[:, :, c:c + CG]).then_inc(s_wld[n % 2], 16)

            load_x(0)
            sp.dma_start(gmix[:, :], norm_mix.to_broadcast([P, D])).then_inc(s_const, 16)
            load_w(0)
            sp.dma_start(gq_bc[:, :], g_q.to_broadcast([P, HD])).then_inc(s_const, 16)
            sp.dma_start(gk_bc[:, :], g_k.to_broadcast([P, HD])).then_inc(s_const, 16)
            load_x(1)
            load_x(2)
            load_w(1)
            sp.dma_start(hist[0:DB * HIST, :], state_pool.rearrange("b h w -> (b h) w")).then_inc(s_hld, 16)
            consts = [(bias_bc[:, :], sb_bias.to_broadcast([P, H])),
                      (wp_sb[:, :, :], w_pool.rearrange("g c e -> c g e")),
                      (pscale[:, :], pool_scale.rearrange("a (g c) -> c (a g)", c=P)),
                      (pt_sb[:, :], page_table.rearrange("(a b) j -> a (b j)", a=1))]
            assert len(consts) == NCONST
            for out, src in consts:
                sp.dma_start(out, src).then_inc(s_cst2, 16)
            for s in range(NS):
                kind, half, t = steps[s]
                if s + 3 < NT:
                    load_x(s + 3)
                if t == 5 and s // NT + 2 < 8:
                    load_w(s // NT + 2)
                r = ROWS[t]
                if kind == "k":
                    sp.wait_ge(s_kn, s + 1)
                    sp.dma_start(k_all[row0(t):row0(t) + r, half * CG:half * CG + CG],
                                 kn[s % NKN][0:r, :]).then_inc(s_kst[s % NKN], 16)
                if kind == "v":
                    sp.wait_ge(s_v, s - NQK + 1)
                    sp.dma_start(v_all[row0(t):row0(t) + r, half * CG:half * CG + CG],
                                 vv[0:r, t, half * CG:half * CG + CG]).then_inc(s_vst, 16)
            sp.wait_ge(s_ur, 2)
            sp.dma_start(pool_p, up_rows[TAILP - HIST:TAILP, :]).then_inc(s_ust, 16)
            sp.dma_start(u_scr, us_rows[:, :]).then_inc(s_uscr, 16)
            sp.dma_start(pool_s[:, 0:HIST - DS, :], state_pool[:, DS:HIST, :]).then_inc(s_ust, 16)
            sp.wait_ge(s_uscr, 16)
            sp.dma_start(pool_s[:, HIST - DS:HIST, :],
                         u_scr.rearrange("(b s) w -> b s w", s=DS)).then_inc(s_ust, 16)
            sp.wait_ge(s_cst2, 16 * NCONST)
            sp.wait_ge(s_pm, NUS)
            sp.wait_ge(s_d, NG)
            sp.wait_ge(s_pl, NUS)
            sp.wait_ge(s_ut, 1)
            sp.wait_ge(s_ust, 48)

            def load_pages(cache, buf, loaded, b):
                for j in range(NPG):
                    page = sp.value_load(pt_sb[0:1, b * NPG + j:b * NPG + j + 1], min_val=0,
                                         max_val=cache_k.shape[0] - 1)
                    src = cache[bass.ds(page, 1), :, :, :]
                    sp.dma_start(buf[:, j, :], src.rearrange("a p h d -> (a p) (h d)")).then_inc(loaded, 16)

            for g in range(NSG):
                for b in range(SQ * g, SQ * g + SQ):
                    if b >= 2:
                        sp.wait_ge(s_t, key_group(b - 2, HP - 1) + 1)
                    load_pages(cache_k, pgk[b % 2], s_kld[b % 2], b)
                for b in range(SQ * g, SQ * g + SQ):
                    if b >= 2:
                        sp.wait_ge(s_av, smp_summed(b - 2))
                    load_pages(cache_v, pgv[b % 2], s_vld[b % 2], b)

            def load_w_out(n):
                if n >= 2:
                    sp.wait_ge(s_whi, 8 + n - 1)
                    sp.wait_ge(s_wlo, 8 + n - 1)
                sp.dma_start(w_raw[n % 2][:, :, :], w_out_v[:, :, n * CG:n * CG + CG]).then_inc(s_wld[n % 2], 16)

            sp.wait_ge(s_av, smp_summed(DB - 1))
            load_w_out(0)
            sp.wait_ge(s_kTs, DB)
            sp.dma_start(gffn[:, :], norm_ffn.to_broadcast([P, D])).then_inc(s_wr, 16)
            sp.dma_start(w_r[:, :, 0:NGRP], w_group.rearrange("(kt p) e -> p kt e", p=P)).then_inc(s_wr, 16)
            sp.dma_start(w_r[:, :, NGRP:NGRP + NE], w_expert.rearrange("(kt p) e -> p kt e", p=P)).then_inc(s_wr, 16)
            sp.wait_ge(s_av, summed_at(NU - 1))
            load_w_out(1)
            for t in range(NT):
                lo = P * t - META
                if t == 0:
                    sp.dma_start(xmid[0:META, 0, :], meta_tokens).then_inc(s_xr[t], 16)
                    sp.dma_start(xmid[META:P, 0, :], x_prompt[0, 0:P - META, :]).then_inc(s_xr[t], 16)
                elif t < LAST:
                    sp.dma_start(xmid[:, t, :], x_prompt[0, lo:lo + P, :]).then_inc(s_xr[t], 32)
                else:
                    sp.dma_start(xmid[0:TAILP, t, :], x_prompt[0, lo:SEQ, :]).then_inc(s_xr[t], 16)
                    sp.dma_start(xmid[TAILP:TAILP + TS, t, :],
                                 x_sample.rearrange("b s d -> (b s) d")).then_inc(s_xr[t], 16)
            load_w_out(2)
            load_w_out(3)

            def load_part(j, e, b):
                since(sp, s_el[j], b)
                part = (gate_v, up_v, down_v)[j][bass.ds(e, 1)].rearrange("a p k f -> (a p) k f")
                sp.dma_start(e_raw[j][:, :, :], part).then_inc(s_wl[j], 16)

            sp.wait_ge(s_zr, 1)
            sp.dma_start(n_scr[T:NY, :], zrow[:, :]).then_inc(s_yst, 16)
            sp.dma_start(y_all[T:NY, :], zrow[:, :]).then_inc(s_yst, 16)
            for t in range(NT):
                r = ROWS[t]
                sp.wait_ge(s_n2, t + 1)
                sp.dma_start(n_scr[row0(t):row0(t) + r, :], xg[t % 2][0:r, :]).then_inc(s_nst[t % 2], 16)
            sp.wait_ge(s_wo, len(wsteps))
            load_part(0, 0, 0)
            for t in range(NT):
                sp.dma_start(y_all[row0(t):row0(t) + ROWS[t], :], xmid[0:ROWS[t], t, :]).then_inc(s_yst, 16)
            load_part(1, 0, 0)
            load_part(2, 0, 0)
            load_part(0, 1, 1)
            load_part(1, 1, 1)
            load_part(0, 2, 2)
            load_part(2, 1, 1)
            load_part(1, 2, 2)
            with sp.Fori(3, NE) as b:
                load_part(0, b, b)
                load_part(2, b - 1, b - 1)
                load_part(1, b, b)
            load_part(2, NE - 1, NE - 1)
            sp.wait_ge(s_tab, 1)
            n_over = sp.value_load(ovmi[0:1, OVB:OVB + 1], min_val=0, max_val=OVB)
            with sp.Fori(0, OVB // 2) as i:
                for k in range(2):
                    o = 2 * i + k
                    with sp.If(n_over > o):
                        e = sp.value_load(ovmi[0:1, bass.ds(o, 1)], min_val=0, max_val=NE - 1)
                        for j in range(3):
                            load_part(j, e, o + NE)
            for i in range(NKN):
                sp.wait_ge(s_kst[i], 16 * len([s for s in range(2 * NT) if s % NKN == i]))
            sp.wait_ge(s_vst, 16 * 2 * NT)

        @block.gpsimd
        def _(pool):
            chain = Chain(pool, s_pool)
            chain.link(pool.memset(ident[:, :], 1.0))
            pool.affine_select(out=ident[:, :], in_=ident[:, :], compare_op=ALU.is_equal, fill=0.0, base=0,
                               pattern=[[-1, P]], channel_multiplier=1).then_inc(s_ident, 1)
            chain.link(pool.memset(diag_mask[:, :], 1.0))
            chain.link(pool.affine_select(out=diag_mask[:, :], in_=diag_mask[:, :], compare_op=ALU.is_gt, fill=0.0,
                                          base=0, pattern=[[-1, P]], channel_multiplier=1))
            chain.link(pool.memset(tail_mask[:, :], 1.0))
            for j in range(4):
                part = tail_mask[32 * j:32 * j + 32, :]
                chain.link(pool.affine_select(out=part, in_=part, compare_op=ALU.is_gt, fill=0.0, base=0,
                                              pattern=[[-1, TAILP]], channel_multiplier=1))
            chain.link(pool.iota(pint[:, 0:1], [[0, 1]], base=0, channel_multiplier=1))
            chain.link(pool.iota(col48[:, :], [[1, ROWS[-1]]], base=0, channel_multiplier=0,
                                 allow_small_or_imprecise_dtypes=True))
            pool.iota(rcnt[:, :], [[1, 16]], base=1, channel_multiplier=0,
                      allow_small_or_imprecise_dtypes=True).then_inc(s_mask, 1)
            pool.wait_ge(s_kn, NQK)
            pool.wait_ge(s_kt, NQK)
            pool.wait_ge(s_xT, NT)
            for i in range(NKN):
                pool.wait_ge(s_kst[i], 16 * len([s for s in range(2 * NT) if s % NKN == i]))
            chain.link(pool.memset(u_ext[:, :, 0:16], 0.0))
            pool.memset(es[:, :, :, 0:1], 0.0).then_inc(s_pad, 1)
            pool.wait_ge(s_pl, NUS)
            pool.wait_ge(s_ut, 1)
            pool.memset(qz[:, :, :, :], 0.0).then_inc(s_pad, 1)
            pool.wait_ge(s_kTs, DB)
            pool.wait_ge(s_te, key_group(DB - 1, HP - 1) + 1)
            pool.wait_ge(s_av, summed_at(NU - 1))
            chain.link(pool.memset(zrow[:, :], 0.0))
            pool.memset(lg[:, LAST, :], 0.0).then_inc(s_zr, 1)
            pool.wait_ge(s_zr, 1)
            pool.wait_ge(s_wo, len(wsteps))
            chain.link(pool.memset(ones[:, :], 1.0))
            chain.link(pool.memset(before[:, :], 1.0))
            chain.link(pool.affine_select(out=before[:, :], in_=before[:, :], compare_op=ALU.is_gt, fill=0.0,
                                          base=0, pattern=[[1, P]], channel_multiplier=-1))
            for out, pattern, first, mult in ((tok[:, :], [[P, NT]], -T, 1), (io4[:, :], [[1, NGRP]], -NGRP, 0),
                                              (io8[:, :], [[1, EPG]], -EPG, 0), (io128[:, :], [[1, P]], 0, 0),
                                              (jt[:, :], [[CAP, OVMAX]], CAP, 0), (nprow[:, :], [[0, 1]], 0, -1)):
                chain.link(pool.iota(out, pattern, base=first, channel_multiplier=mult,
                                     allow_small_or_imprecise_dtypes=True))
            pool.iota(prow[:, :], [[0, 1]], base=T, channel_multiplier=1,
                      allow_small_or_imprecise_dtypes=True).then_inc(s_tbl, 1)

            def gather(b):
                i = b % 2
                pool.wait_ge(s_ix, b + 1)
                if b >= 2:
                    pool.wait_ge(s_xt, b - 1)
                pool.indirect_dma_start(out=xg[i][0:CAP, :], out_offset=None, in_=n_scr,
                                        in_offset=bass.IndirectOffsetOnAxis(ap=gidx[i][:, 0:1].bitcast(U32), axis=0)
                                        ).then_inc(s_gl[i], 16)

            def block_io(b):
                gather(b + 3)
                pool.wait_ge(s_ya, b + 1)
                pool.wait_ge(s_yd, b + 1)
                pool.wait_ge(s_sx2, b + 1)
                pool.indirect_dma_start(out=y_all,
                                        out_offset=bass.IndirectOffsetOnAxis(ap=sidx[b % 2][:, 0:1].bitcast(U32), axis=0),
                                        in_=yo[b % 2][:, :], in_offset=None, compute_op=ALU.add,
                                        bounds_check=NY - 1).then_inc(s_sc, 16)
                pool.wait_ge(s_gl[(b + 3) % 2], 16 * ((b + 3) // 2 + 1))
                pool.wait_ge(s_sc, 16 * (b + 1))

            for i in range(2):
                pool.wait_ge(s_nst[i], 16 * len(range(i, NT, 2)))
            pool.wait_ge(s_yst, 16 * (NT + 2))
            for b in range(3):
                gather(b)
            for b in range(NE):
                block_io(b)
            pool.wait_ge(s_tab, 1)
            n_over = pool.value_load(ovmi[0:1, OVB:OVB + 1], min_val=0, max_val=OVB)
            for o in range(OVB):
                with pool.If(n_over > o):
                    block_io(NE + o)

        @block.scalar
        def _(act):
            chain = Chain(act, s_act)

            def norm_tile(t):
                r = ROWS[t]
                act.wait_ge(s_xld[t % 3], 32 * (t // 3 + 1))
                if t >= 1:
                    act.wait_ge(s_ssq, t)
                if t >= 2:
                    act.wait_ge(s_ms, t - 1)
                act.activation(junk[0:r, :], xt[t % 3][0:r, :], ACT.Square,
                               accum_out=ss[0:r, t % 2:t % 2 + 1]).then_inc(s_ssq, 1)
                act.wait_ge(s_ms, t + 1)
                act.activation(rs[0:r, t % 2:t % 2 + 1], ss[0:r, t % 2:t % 2 + 1], ACT.Sqrt).then_inc(s_rms, 1)
                act.wait_ge(s_xT, t + 1)
                act.activation(xh[:, :, row0(t):row0(t) + r], xT_ps[:, :, 0:r], ACT.Copy).then_inc(s_xh, 1)

            def split_hi(n):
                act.wait_ge(s_wld[n % 2], 16 * (n // 2 + 1))
                if n >= 2:
                    act.wait_ge(s_pr, NT * (n - 1))
                act.activation(w_hi[n % 2][:, :, :], w_raw[n % 2][:, :, :], ACT.Copy).then_inc(s_whi, 1)

            split_hi(0)
            norm_tile(0)
            for s in range(NS + 3):
                if s + 1 < NT:
                    norm_tile(s + 1)
                if s % NT == 3 and s // NT + 1 < 8:
                    split_hi(s // NT + 1)
                if s < NQK:
                    r = ROWS[steps[s][2]]
                    act.wait_ge(s_pr, s + 1)
                    if s >= 2:
                        act.wait_ge(s_hms, s - 1)
                    act.activation(sq[s % 2][0:r, :], proj_ps(s)[0:r, :], ACT.Square).then_inc(s_sq, 1)
                elif s < NS:
                    _, half, t = steps[s]
                    r = ROWS[t]
                    if s == NQK:
                        act.wait_ge(s_ssq, NT)
                    act.wait_ge(s_pr, s + 1)
                    act.activation(vv[0:r, t, half * CG:half * CG + CG], proj_ps(s)[0:r, :],
                                   ACT.Copy).then_inc(s_v, 1)
                if 1 <= s <= NQK:
                    r = ROWS[steps[s - 1][2]]
                    act.wait_ge(s_hms, s)
                    act.activation(hr[0:r, (s - 1) % 2, :], hs[0:r, (s - 1) % 2, :], ACT.Sqrt).then_inc(s_hrms, 1)
                if 3 <= s < NQK + 3:
                    kind, half, t = steps[s - 3]
                    r = ROWS[t]
                    act.wait_ge(s_kt, s - 2)
                    dst = qT if kind == "q" else kT
                    act.activation(dst[:, 2 * half:2 * half + 2, row0(t):row0(t) + r],
                                   head_ps(s - 3)[:, :, 0:r], ACT.Copy).then_inc(s_ke, 1)
            split_hi(7)

            act.wait_ge(s_pad, 1)
            act.wait_ge(s_ht, 1)
            act.activation(es[:, :, :, 1:16],
                           bank[:, 6, 0:NG * DB * HIST].rearrange("p (g b i) -> p g b i", g=NG, b=DB),
                           ACT.Copy).then_inc(s_uc, 1)
            for i, (g, piece) in enumerate(usteps):
                s = NS + i
                lo, n = PIECES[piece]
                act.wait_ge(s_pr, s + 1)
                if piece < 2:
                    act.activation(u_ext[:, g, 16 + lo:16 + lo + n], wide_ps(s)[:, 0:n], ACT.Copy).then_inc(s_uc, 1)
                else:
                    act.activation(u_ext[:, g, 16 + lo:16 + TP], wide_ps(s)[:, 0:TAILP], ACT.Copy).then_inc(s_uc, 1)
                    act.activation(es[:, g, :, 16:20], wide_ps(s)[:, TAILP:TAILP + TS].rearrange("p (b j) -> p b j", j=DS),
                                   ACT.Copy).then_inc(s_uc, 1)
                    act.activation(us_cols[:, g, :], wide_ps(s)[:, TAILP:TAILP + TS], ACT.Copy).then_inc(s_uc, 1)
            act.wait_ge(s_ut, 1)
            act.activation(up_rows[:, :], bank[0:TAILP, 6, :], ACT.Copy).then_inc(s_ur, 1)
            act.activation(us_rows[:, :], bank[0:TS, 7, :], ACT.Copy).then_inc(s_ur, 1)
            act.wait_ge(s_cst2, 16 * NCONST)
            for i, (g, piece) in enumerate(usteps):
                lo, n = PIECES[piece]
                act.wait_ge(s_pm, i + 1)
                act.activation(xh[:, g, lo:lo + n], wide_ps(NS + NUS + i)[:, 0:n], ACT.Copy,
                               scale=pscale[:, g:g + 1]).then_inc(s_ph, 1)

            def sigmoid(u):
                kind, w = units[u][0], width(u)
                act.wait_ge(s_z, u + 1)
                if u >= 2:
                    act.wait_ge(s_am, u - 1)
                elif u == 0:
                    act.wait_ge(s_pm, NUS)
                    act.wait_ge(s_d, NG)
                    act.wait_ge(s_pr, NS + NUS)
                    act.wait_ge(s_mask, 2)
                bias = (bias_bc[:, units[u][2]:units[u][2] + 1] if kind == "full" else
                        bias_tail[:, units[u][1]:units[u][1] + 1] if kind == "tail" else bias_smp[:, 0:1])
                act.activation(sg[u % 2][:, NK - w:NK], z_ps(u)[:, 0:w], ACT.Sigmoid, bias=bias,
                               scale=HD ** -0.5).then_inc(s_sg, 1)

            def copy_banks(u):
                for j, group in enumerate(groups(u)):
                    n = first_group(u) + j
                    act.wait_ge(s_t, n + 1)
                    if j == 0 and u >= 2:
                        act.wait_ge(s_av, summed_at(u - 2))
                    full = [c for c in group if c[1] == P]
                    if full:
                        last = act.activation(aT[u % 2][:, full[0][0]:full[-1][0] + 1, :], t_ps(n)[:, 0:len(full), :], ACT.Copy)
                    if len(full) < len(group):
                        c, keys = group[-1]
                        last = act.activation(aT[u % 2][0:keys, c, :], t_ps(n)[0:keys, len(full), :], ACT.Copy)
                    last.then_inc(s_te, 1)

            def copy_o(u):
                i, ends = out_of(u)
                if ends:
                    act.wait_ge(s_av, summed_at(u))
                    if i >= 1:
                        act.wait_ge(s_oT, i)
                    act.activation(o_sb[0:out_rows(i), :], o_ps(i)[0:out_rows(i), :], ACT.Copy).then_inc(s_os, 1)

            def hi_o(u):
                i, ends = out_of(u)
                t = tile_of(i)
                if ends and t is not None:
                    r = out_rows(i)
                    act.wait_ge(s_oT, i + 1)
                    act.activation(xh[:, HP:KT, row0(t):row0(t) + r],
                                   o_ps(i).rearrange("p (c n) -> p c n", n=P)[:, :, 0:r], ACT.Copy).then_inc(s_oh, 1)
                if t is None:
                    act.wait_ge(s_oT, i + 1)
                    for half in range(2):
                        rows = slice(64 * half, 64 * half + 64)
                        last = act.activation(smp_out(xh, outs[i][1], rows), smp_in(i, half, rows), ACT.Copy)
                        if half == 0:
                            last.then_inc(s_act, 1)
                    last.then_inc(s_oh, 1)

            def copy_keys(g):
                for b in range(SQ * g, SQ * g + SQ):
                    for hp in range(HP):
                        n = key_group(b, hp)
                        act.wait_ge(s_t, n + 1)
                        if b >= 1:
                            act.wait_ge(s_kTs, b)
                        last = act.activation(kTs[:, hp, :], bank[:, 4 + n % 2, :], ACT.Copy)
                        last.then_inc(s_te, 1)

            def split_out_hi(n):
                act.wait_ge(s_wld[n % 2], 16 * (4 + n // 2 + 1))
                if n < 2:
                    act.wait_ge(s_av, summed_at(NU - 2 + n))
                else:
                    act.wait_ge(s_wo, NT * (n - 1))
                act.activation(w_hi[n % 2][:, :, :], w_raw[n % 2][:, :, :], ACT.Copy).then_inc(s_whi, 1)

            assert NU % 2 == 0
            for i in range(NU + 6):
                if i < NU:
                    if units[i][0] == "smp":
                        copy_keys(units[i][1])
                    sigmoid(i)
                if 2 <= i < NU + 2:
                    copy_banks(i - 2)
                if i == NU + 2:
                    split_out_hi(0)
                if 4 <= i < NU + 4:
                    copy_o(i - 4)
                if 6 <= i:
                    hi_o(i - 6)

            for n in range(1, D // CG):
                split_out_hi(n)

            for t in range(NT + 2):
                if 1 <= t <= NT:
                    act.wait_ge(s_ms2, t)
                    c = slice((t - 1) % 2, (t - 1) % 2 + 1)
                    act.activation(rs[0:ROWS[t - 1], c], ss[0:ROWS[t - 1], c], ACT.Sqrt).then_inc(s_rms2, 1)
                if t < NT:
                    r = ROWS[t]
                    act.wait_ge(s_xm, tile_done(t))
                    if t >= 1:
                        act.wait_ge(s_ssq2, t)
                    act.activation(junk2[0:r, :], xmid[0:r, t, :], ACT.Square,
                                   accum_out=ss[0:r, t % 2:t % 2 + 1]).then_inc(s_ssq2, 1)
                if t >= 2:
                    i, r = t - 2, ROWS[t - 2]
                    act.wait_ge(s_n2T, i + 1)
                    if i >= 2:
                        act.wait_ge(s_lgp, i - 1)
                    act.activation(nT[i % 2][:, :, 0:r], norm_ps(i)[:, :, 0:r], ACT.Copy).then_inc(s_n2c, 1)
            act.wait_ge(s_gx, 1)
            act.activation(gex[:, :, :], gex[:, :, :], ACT.Exp).then_inc(s_ge, 1)
            act.wait_ge(s_gx, 2)
            act.activation(gt[:, 1, :], gt[:, 1, :], ACT.Exp).then_inc(s_ge, 1)

            def parts(j):
                return ((s_gp, 1), (s_up, 1), (s_dp, 2))[j]

            def weight_hi(j, b, half):
                if half == 0:
                    act.wait_ge(s_wl[j], 16 * b + 16)
                    done, per = parts(j)
                    since(act, done, per * b)
                h = e_raw[j].shape[1] // 2
                act.activation(e_hi[j][:, h * half:h * half + h, :], e_raw[j][:, h * half:h * half + h, :],
                               ACT.Copy).then_inc(s_eh[j], 1)

            def weight_whole(j, b):
                for half in range(2):
                    weight_hi(j, b, half)

            def block_hi(b, i):
                act.wait_ge(s_xt, b + 1)
                since(act, s_up, b - 1)
                act.activation(xeh[i][:, :, :], xT_ps[:, :, 0:CAP], ACT.Copy).then_inc(s_xe, 1)

            def silu(b, i):
                act.wait_ge(s_gp, b + 1)
                since(act, s_h, b)
                act.activation(sgl[:, :], gate_ps(i), ACT.Silu).then_inc(s_si, 1)

            def hidden_hi(b):
                act.wait_ge(s_hT, b + 1)
                since(act, s_dp, 2 * b)
                act.activation(hT_hi[:, :, :], hT_ps, ACT.Copy).then_inc(s_hh, 1)

            def left_half(b, i):
                act.wait_ge(s_dp, 2 * b + 1)
                act.wait_ge(s_sx, b + 1)
                act.activation(yo[i][:, 0:512], bank[0:CAP, 6, :], ACT.Copy, scale=gcol[i][:, 0:1]).then_inc(s_ya, 1)

            def first_act():
                weight_whole(0, 0)
                weight_whole(1, 0)
                for b in range(2):
                    block_hi(b, b)
                act.wait_ge(s_yst, 16 * (NT + 2))
                weight_whole(2, 0)
                silu(0, 0)
                weight_whole(0, 1)

            def block_act(i, b):
                weight_hi(1, b + 1, 0)
                hidden_hi(b)
                weight_hi(1, b + 1, 1)
                silu(b + 1, 1 - i)
                if not (type(b) is int and b == NE - 2):
                    weight_whole(0, b + 2)
                left_half(b, i)
                block_hi(b + 2, i)
                weight_whole(2, b + 1)

            def last_act(b):
                if b == NE - 2:
                    block_act(0, b)
                else:
                    hidden_hi(b)
                    left_half(b, 1)
                    block_hi(b + 2, 1)

            def further_act(i, b):
                for j in range(3):
                    weight_whole(j, b)
                silu(b, i)
                hidden_hi(b)
                left_half(b, i)
                block_hi(b + 2, i)

            blocks(act, first_act, block_act, last_act, further_act)

        @block.vector
        def _(dve):
            chain = Chain(dve, s_dve)

            def norm_tile(t):
                r = ROWS[t]
                c = slice(t % 2, t % 2 + 1)
                dve.wait_ge(s_ssq, t + 1)
                dve.tensor_scalar(ss[0:r, c], ss[0:r, c], 1.0 / D, EPS, ALU.mult, ALU.add).then_inc(s_ms, 1)
                dve.wait_ge(s_rms, t + 1)
                chain.link(dve.reciprocal(rs[0:r, c], rs[0:r, c]))
                dve.scalar_tensor_tensor(out=xt[t % 3][0:r, :], in0=xt[t % 3][0:r, :], scalar=rs[0:r, c],
                                         in1=gmix[0:r, :], op0=ALU.mult, op1=ALU.mult).then_inc(s_xs, 1)
                dve.wait_ge(s_xh, t + 1)
                dve.tensor_tensor(xl[:, :, row0(t):row0(t) + r], xT_ps[:, :, 0:r],
                                  xh[:, :, row0(t):row0(t) + r].bitcast(F32), ALU.subtract).then_inc(s_xl, 1)

            def split_lo(n):
                dve.wait_ge(s_whi, n + 1)
                if n >= 2:
                    dve.wait_ge(s_pr, NT * (n - 1))
                dve.tensor_tensor(w_lo[n % 2][:, :, :], w_raw[n % 2][:, :, :], w_hi[n % 2][:, :, :].bitcast(F32),
                                  ALU.subtract).then_inc(s_wlo, 1)

            def norm_heads(s):
                kind, half, t = steps[s]
                r = ROWS[t]
                dve.wait_ge(s_hrms, s + 1)
                chain.link(dve.reciprocal(hr[0:r, s % 2, :], hr[0:r, s % 2, :]))
                if s >= NKN:
                    dve.wait_ge(s_kt, s - NKN + 1)
                    if steps[s - NKN][0] == "k":
                        dve.wait_ge(s_kst[s % NKN], 16 * (s // NKN))
                out = kn[s % NKN][0:r, :].rearrange("p (h d) -> p h d", d=HD)
                inv = hr[0:r, s % 2, :].rearrange("p (h a) -> p h a", a=1).to_broadcast([r, 4, HD])
                chain.link(dve.tensor_tensor(out, proj_ps(s)[0:r, :].rearrange("p (h d) -> p h d", d=HD), inv, ALU.mult))
                g = (gq_bc if kind == "q" else gk_bc)[0:r, :].rearrange("p (a d) -> p a d", a=1)
                dve.tensor_tensor(out, out, g.to_broadcast([r, 4, HD]), ALU.mult).then_inc(s_kn, 1)

            dve.wait_ge(s_const, 48)
            split_lo(0)
            norm_tile(0)
            for s in range(NQK + 1):
                if s + 1 < NT:
                    norm_tile(s + 1)
                if s % NT == 3 and s // NT + 1 < 8:
                    split_lo(s // NT + 1)
                if s < NQK:
                    r = ROWS[steps[s][2]]
                    dve.wait_ge(s_sq, s + 1)
                    chain.link(dve.reduce_sum(hs[0:r, s % 2, :], sq[s % 2][0:r, :].rearrange("p (h d) -> p h d", d=HD),
                                              axis=AXX))
                    dve.tensor_scalar(hs[0:r, s % 2, :], hs[0:r, s % 2, :], 1.0 / HD, EPS,
                                      ALU.mult, ALU.add).then_inc(s_hms, 1)
                if s >= 1:
                    norm_heads(s - 1)
            split_lo(5)
            dve.wait_ge(s_mask, 1)
            dve.wait_ge(s_cst2, 16 * NCONST)
            chain.done(dve.tensor_scalar(pint[:, 1:2], pint[:, 0:1], 3, None, ALU.bitwise_and))
            chain.done(dve.tensor_scalar(pint[:, 2:3], pint[:, 0:1], 5, None, ALU.logical_shift_right))
            chain.done(dve.tensor_scalar(pint[:, 3:4], pint[:, 0:1], 2, 7, ALU.logical_shift_right, ALU.bitwise_and))
            chain.settle()
            chain.link(dve.tensor_copy(pflt[:, 0:3], pint[:, 1:4]))
            for g in range(NSG):
                chain.link(dve.tensor_scalar(pflt[:, 3:4], pflt[:, 1:2], float(DS), float(TAILP + DS * SQ * g), ALU.mult, ALU.add))
                chain.link(dve.tensor_tensor(pflt[:, 4:5], pflt[:, 3:4], pflt[:, 0:1], ALU.add))
                chain.link(dve.tensor_scalar(smp_mask[:, g, :], col48[:, :], pflt[:, 3:4], None, ALU.is_ge))
                chain.link(dve.scalar_tensor_tensor(out=smp_mask[:, g, :], in0=col48[:, :], scalar=pflt[:, 4:5],
                                                    in1=smp_mask[:, g, :], op0=ALU.is_lt, op1=ALU.mult))
            chain.link(dve.memset(bias_smp[:, :], 0.0))
            for h in range(H):
                chain.link(dve.tensor_scalar(pflt[:, 5:6], pflt[:, 2:3], float(h), None, ALU.is_equal))
                chain.link(dve.scalar_tensor_tensor(out=bias_smp[:, :], in0=pflt[:, 5:6], scalar=bias_bc[:, h:h + 1],
                                                    in1=bias_smp[:, :], op0=ALU.mult, op1=ALU.add))
            for h in range(H):
                rows = slice(32 * (h % 4), 32 * (h % 4) + 32)
                chain.done(dve.tensor_copy(bias_tail[rows, h // 4:h // 4 + 1], bias_bc[rows, h:h + 1]))
            dve.reciprocal(rcnt[:, :], rcnt[:, :]).then_inc(s_mask, 1)
            dve.wait_ge(s_mask, 2)
            split_lo(6)
            split_lo(7)

            def diff(g):
                w = WINDOWS[g]
                dve.wait_ge(s_uc, u_copies(3 * g + 2))
                if g == 0:
                    dve.wait_ge(s_pr, NS + 6)
                    dve.wait_ge(s_wlo, 8)
                    dve.wait_ge(s_whi, 8)
                src, n = u_ext[:, g, :], 1
                srcs = es[:, g, :, :]
                small = [wsmall0, wsmall1]
                k = 0
                while n < w:
                    dst, dsts = wsum[k % 2], small[k % 2]
                    chain.done(dve.tensor_tensor(dst[:, 2 * n - 1:16 + TP], src[:, 2 * n - 1:16 + TP],
                                                 src[:, n - 1:16 + TP - n], ALU.add))
                    chain.done(dve.tensor_tensor(dsts[:, :, 2 * n - 1 + 1:20], srcs[:, :, 2 * n - 1 + 1:20],
                                                 srcs[:, :, n:20 - n], ALU.add))
                    chain.settle()
                    src, srcs, n, k = dst, dsts, 2 * n, k + 1
                if g >= 1:
                    dve.wait_ge(s_pm, 3 * g)
                chain.done(dve.scalar_tensor_tensor(out=dT[:, w - 1:TP], in0=src[:, 16 + w - 1:16 + TP], scalar=1.0 / w,
                                                    in1=u_ext[:, g, 16 + w - 1:16 + TP], op0=ALU.mult, op1=ALU.subtract))
                chain.link(dve.tensor_tensor(dT[:, 0:w - 1], src[:, 16:16 + w - 1], rcnt[:, 0:w - 1], ALU.mult))
                chain.link(dve.tensor_tensor(dT[:, 0:w - 1], dT[:, 0:w - 1], u_ext[:, g, 16:16 + w - 1], ALU.subtract))
                dve.scalar_tensor_tensor(out=dT[:, TP:T].rearrange("p (b j) -> p b j", j=DS), in0=srcs[:, :, 16:20],
                                         scalar=1.0 / w, in1=es[:, g, :, 16:20], op0=ALU.mult,
                                         op1=ALU.subtract).then_inc(s_d, 1)
                dve.wait_ge(s_d, g + 1)

            def pool_lo(g):
                for piece in range(3):
                    i = 3 * g + piece
                    lo, n = PIECES[piece]
                    dve.wait_ge(s_ph, i + 1)
                    dve.scalar_tensor_tensor(out=xl[:, g, lo:lo + n], in0=wide_ps(NS + NUS + i)[:, 0:n],
                                             scalar=pscale[:, g:g + 1], in1=xh[:, g, lo:lo + n].bitcast(F32),
                                             op0=ALU.mult, op1=ALU.subtract).then_inc(s_pl, 1)

            for g in range(NG):
                diff(g)
                if g >= 1:
                    pool_lo(g - 1)
            pool_lo(NG - 1)

            dve.wait_ge(s_pad, 2)
            dve.wait_ge(s_ke, NQK)
            for h in range(H):
                rows = slice(64 * (h % 2), 64 * (h % 2) + 64)
                last = dve.tensor_copy(qz[rows, :, h // 2, DS * h:DS * h + DS],
                                       qT[rows, h // 2, TP:T].rearrange("p (b j) -> p b j", j=DS))
                if h < H - 1:
                    chain.done(last)
            last.then_inc(s_qz, 1)

            def weigh(u):
                kind, w = units[u][0], width(u)
                lo = NK - w
                row, prod = sg[u % 2], pb[u % 2]
                dve.wait_ge(s_sg, u + 1)
                if kind == "full":
                    chain.link(dve.tensor_tensor(row[:, NK - P:NK], row[:, NK - P:NK], diag_mask[:, :], ALU.mult))
                elif kind == "tail":
                    chain.link(dve.tensor_tensor(row[:, NK - TAILP:NK], row[:, NK - TAILP:NK], tail_mask[:, :], ALU.mult))
                else:
                    n = ROWS[-1]
                    chain.link(dve.tensor_tensor(row[:, NK - n:NK], row[:, NK - n:NK], smp_mask[:, units[u][1], :], ALU.mult))
                chain.link(dve.tensor_scalar(prod[:, lo:NK], row[:, lo:NK], -1.0, 1.0, ALU.mult, ALU.add))
                back = prod[:, lo:NK][:, ::-1]
                chain.link(dve.tensor_tensor_scan(back, back, back, 1.0, ALU.mult, ALU.bypass))
                if u >= 2:
                    dve.wait_ge(s_t, first_group(u - 2) + len(groups(u - 2)))
                dve.tensor_tensor(am[u % 2][:, lo:NK], row[:, lo:NK], prod[:, lo + 1:NK + 1], ALU.mult).then_inc(s_am, 1)
                dve.wait_ge(s_am, u + 1)

            def lo_o(u):
                i, ends = out_of(u)
                t = tile_of(i)
                if ends and t is not None:
                    r = P if t < LAST else TAILP
                    dve.wait_ge(s_oh, i + 1)
                    dve.tensor_tensor(xl[:, HP:KT, row0(t):row0(t) + r],
                                      o_ps(i).rearrange("p (c n) -> p c n", n=P)[:, :, 0:r],
                                      xh[:, HP:KT, row0(t):row0(t) + r].bitcast(F32), ALU.subtract).then_inc(s_ol, 1)
                if t is None:
                    dve.wait_ge(s_oh, i + 1)
                    dve.wait_ge(s_act, outs[i][1] + 1)
                    for half in range(2):
                        rows = slice(64 * half, 64 * half + 64)
                        last = dve.tensor_tensor(smp_out(xl, outs[i][1], rows), smp_in(i, half, rows),
                                                 smp_out(xh, outs[i][1], rows).bitcast(F32), ALU.subtract)
                        if half == 0:
                            chain.done(last)
                    last.then_inc(s_ol, 1)

            for i in range(2):
                chain.link(dve.memset(pb[i][:, NK:NK + 1], 1.0))
            def split_out_lo(n):
                dve.wait_ge(s_whi, 8 + n + 1)
                if n >= 2:
                    dve.wait_ge(s_wo, NT * (n - 1))
                dve.tensor_tensor(w_lo[n % 2][:, :, :], w_raw[n % 2][:, :, :], w_hi[n % 2][:, :, :].bitcast(F32),
                                  ALU.subtract).then_inc(s_wlo, 1)

            for i in range(NU + 6):
                if i < NU:
                    weigh(i)
                if i == NU + 2:
                    split_out_lo(0)
                if 6 <= i:
                    lo_o(i - 6)

            def norm_scale(t):
                r = ROWS[t]
                c = slice(t % 2, t % 2 + 1)
                dve.wait_ge(s_ssq2, t + 1)
                dve.tensor_scalar(ss[0:r, c], ss[0:r, c], 1.0 / D, EPS, ALU.mult, ALU.add).then_inc(s_ms2, 1)
                dve.wait_ge(s_rms2, t + 1)
                chain.link(dve.reciprocal(rs[0:r, c], rs[0:r, c]))
                if t >= 2:
                    dve.wait_ge(s_n2T, t - 1)
                    dve.wait_ge(s_nst[t % 2], 16 * (t // 2))
                dve.scalar_tensor_tensor(out=xg[t % 2][0:r, :], in0=xmid[0:r, t, :], scalar=rs[0:r, c],
                                         in1=gffn[0:r, :], op0=ALU.mult, op1=ALU.mult).then_inc(s_n2, 1)

            def copy_logits(t):
                dve.wait_ge(s_lgp, t + 1)
                dve.tensor_copy(lg[0:ROWS[t], t, :], logit_ps(t)[0:ROWS[t], :]).then_inc(s_lg, 1)

            dve.wait_ge(s_wr, 48)
            dve.wait_ge(s_zr, 1)
            for s, (n, t) in enumerate(wsteps):
                if s in (2, NT + 2, 2 * NT):
                    split_out_lo({2: 1, NT + 2: 2, 2 * NT: 3}[s])
                r = ROWS[t]
                if n == 0:
                    dve.wait_ge(s_xr[t], 32)
                dve.wait_ge(s_wo, s + 1)
                dst = xmid[0:r, t, n * CG:n * CG + CG]
                dve.tensor_tensor(dst, out_ps(s)[0:r, :], dst, ALU.add).then_inc(s_xm, 1)
                if n == 3 and t >= 1:
                    norm_scale(t - 1)
                if n == 3 and t >= 4:
                    copy_logits(t - 4)
            norm_scale(LAST)
            for t in range(NT - 4, NT):
                copy_logits(t)
            dve.wait_ge(s_tbl, 1)
            dve.wait_ge(s_lg, NT)

            def wide(ap, n):
                return ap.rearrange("p (a x) -> p a x", x=1).to_broadcast([P, ap.shape[1], n])

            def over(ap, n):
                return ap.rearrange("p (x a) -> p x a", x=1).to_broadcast([P, n, ap.shape[1]])

            def first_best(out, best, values, steps_, n):
                chain.link(dve.reduce_max(best, values, axis=AXX))
                chain.link(dve.tensor_tensor(out, values, wide(best, n), ALU.is_equal))
                chain.link(dve.tensor_tensor(out, out, over(steps_[:, :], NT), ALU.mult))
                chain.link(dve.tensor_reduce(rsum[:, :], out, axis=AXX, op=ALU.min))
                chain.link(dve.tensor_tensor(out, over(steps_[:, :], NT), wide(rsum[:, :], n), ALU.is_equal))

            first_best(goh[:, :, :], gmx[:, :], lg[:, :, 0:NGRP], io4, NGRP)
            dve.tensor_tensor(gex[:, :, :], lg[:, :, 0:NGRP], wide(gmx[:, :], NGRP), ALU.subtract).then_inc(s_gx, 1)
            for g in range(NGRP):
                part = lg[:, :, NGRP + EPG * g:NGRP + EPG * (g + 1)]
                chain.link(dve.tensor_tensor((le if g == 0 else tmp8)[:, :, :], part, wide(goh[:, :, g], EPG), ALU.mult))
                if g:
                    chain.link(dve.tensor_tensor(le[:, :, :], le[:, :, :], tmp8[:, :, :], ALU.add))
            first_best(oh[:, 0, :, :], mx[:, 0, :], le[:, :, :], io8, EPG)
            chain.link(dve.scalar_tensor_tensor(out=le[:, :, :], in0=oh[:, 0, :, :], scalar=-3.0e38, in1=le[:, :, :],
                                                op0=ALU.mult, op1=ALU.add))
            first_best(oh[:, 1, :, :], mx[:, 1, :], le[:, :, :], io8, EPG)
            dve.tensor_tensor(gt[:, 1, :], mx[:, 1, :], mx[:, 0, :], ALU.subtract).then_inc(s_gx, 1)
            chain.link(dve.tensor_scalar(valid[:, :], tok[:, :], 0.0, None, ALU.is_lt))
            chain.link(dve.tensor_tensor(goh[:, :, :], goh[:, :, :], wide(valid[:, :], NGRP), ALU.mult))
            for k in range(2):
                for g in range(NGRP):
                    chain.done(dve.tensor_tensor(ek[:, k, :, EPG * g:EPG * (g + 1)], oh[:, k, :, :], wide(goh[:, :, g], EPG),
                                                 ALU.mult))
            chain.settle()
            dve.tensor_tensor(eb[:, :, :], ek[:, 0, :, :], ek[:, 1, :, :], ALU.add).then_inc(s_eb, 1)
            dve.wait_ge(s_ge, 2)
            chain.link(dve.reduce_sum(gw[:, :], gex[:, :, :], axis=AXX))
            chain.link(dve.reciprocal(gw[:, :], gw[:, :]))
            chain.link(dve.tensor_scalar(gt[:, 0, :], gt[:, 1, :], 1.0, None, ALU.add))
            chain.link(dve.reciprocal(gt[:, 0, :], gt[:, 0, :]))
            chain.link(dve.tensor_tensor(gt[:, 0, :], gt[:, 0, :], gw[:, :], ALU.mult))
            chain.link(dve.tensor_tensor(gt[:, 1, :], gt[:, 1, :], gt[:, 0, :], ALU.mult))
            dve.wait_ge(s_rkp, 1)
            totals = bank[:, 7, 0:NT * NE].rearrange("p (t e) -> p t e", t=NT)
            chain.link(dve.memset(cum[:, 0, :], 0.0))
            for t in range(1, NT):
                chain.link(dve.tensor_tensor(cum[:, t, :], totals[:, t - 1, :], cum[:, t - 1, :], ALU.add))
            chain.link(dve.tensor_tensor(cnt[:, :], totals[:, LAST, :], cum[:, LAST, :], ALU.add))
            chain.link(dve.tensor_tensor(cum[:, :, :], bank[:, 6, 0:NT * NE].rearrange("p (t e) -> p t e", t=NT),
                                         cum[:, :, :], ALU.add))
            chain.link(dve.tensor_tensor(cmp_[:, :, :], wide(cnt[:, :], OVMAX), over(jt[:, :], NE), ALU.is_gt))
            chain.link(dve.reduce_sum(nov[:, :], cmp_[:, :, :], axis=AXX))
            chain.link(dve.tensor_tensor_scan(ovend[:, :], nov[:, :], nov[:, :], 0.0, ALU.add, ALU.bypass))
            chain.link(dve.tensor_tensor(ovst[:, :], ovend[:, :], nov[:, :], ALU.subtract))

            def picked(out, values):
                for k in range(2):
                    chain.link(dve.tensor_tensor(eb2[:, :, :], ek[:, k, :, :], values, ALU.mult))
                    chain.link(dve.reduce_sum(out[:, k, :], eb2[:, :, :], axis=AXX))

            eb2 = eb
            picked(rk, cum[:, :, :])
            picked(eid, over(io128[:, 0:NE], NT))
            picked(ovs, over(ovst[:, :], NT))
            flat = [x[:, :, :].rearrange("p k t -> p (k t)") for x in (rk, bk, rw, cl, eid, ovs)]
            rk_, bk_, rw_, cl_, eid_, ovs_ = flat
            part = cmp_[:, 0:2 * NT, :]
            chain.link(dve.tensor_tensor(part, wide(rk_, OVMAX), over(jt[:, :], 2 * NT), ALU.is_ge))
            chain.link(dve.reduce_sum(bk_, part, axis=AXX))
            chain.link(dve.scalar_tensor_tensor(out=rw_, in0=bk_, scalar=-float(CAP), in1=rk_, op0=ALU.mult, op1=ALU.add))
            chain.link(dve.tensor_tensor(cl_, ovs_, bk_, ALU.add))
            chain.link(dve.tensor_tensor(cl_, cl_, eid_, ALU.subtract))
            chain.link(dve.tensor_scalar(cl_, cl_, float(NE - 1), None, ALU.add))
            chain.link(dve.tensor_scalar(ovs_, bk_, 0.0, None, ALU.is_gt))
            chain.link(dve.tensor_tensor(cl_, cl_, ovs_, ALU.mult))
            chain.link(dve.tensor_tensor(cl_, cl_, eid_, ALU.add))
            for k in range(2):
                chain.done(dve.tensor_tensor(row_oh[:, :, k, :], over(io128[:, 0:CAP], NT), wide(rw[:, k, :], CAP), ALU.is_equal))
                chain.done(dve.tensor_tensor(col_oh[:, :, k, 0:NCOL], over(io128[:, 0:NCOL], NT), wide(cl[:, k, :], NCOL),
                                             ALU.is_equal))
            chain.settle()
            for k in range(2):
                chain.done(dve.tensor_tensor(row_oh[:, :, k, :], row_oh[:, :, k, :], wide(valid[:, :], CAP), ALU.mult))
                chain.done(dve.tensor_tensor(col_oh[:, :, k, NCOL:2 * NCOL], col_oh[:, :, k, 0:NCOL], wide(gt[:, k, :], NCOL),
                                             ALU.mult))
            chain.settle()
            for k in range(2):
                last = dve.tensor_tensor(col_oh[:, :, k, 0:NCOL], col_oh[:, :, k, 0:NCOL], wide(tok[:, :], NCOL), ALU.mult)
                if k == 0:
                    chain.done(last)
            last.then_inc(s_ohr, 1)
            chain.link(dve.tensor_copy(ovm[0:1, OVB:OVB + 1], ovend[0:1, NE - 1:NE]))
            for o in range(OVB):
                chain.link(dve.tensor_scalar(nov[0:1, :], ovend[0:1, :], float(o), 0.0, ALU.is_le, ALU.add,
                                             accum_out=ovm[0:1, o:o + 1]))
            chain.link(dve.tensor_scalar(ovm[0:1, 0:OVB], ovm[0:1, 0:OVB], float(NE - 1), None, ALU.min))
            chain.link(dve.tensor_copy(ovmi[0:1, 0:OVB + 1], ovm[0:1, 0:OVB + 1]))
            dve.wait_ge(s_tbp, 1)
            chain.link(dve.tensor_scalar(vld[:, :], bank[0:CAP, 5, 0:NCOL], 0.0, None, ALU.is_lt))
            chain.link(dve.tensor_scalar(tabf[:, :], bank[0:CAP, 5, 0:NCOL], prow[0:CAP, :], None, ALU.add))
            chain.link(dve.scalar_tensor_tensor(out=tabf[:, :], in0=vld[:, :], scalar=nprow[0:CAP, :], in1=tabf[:, :],
                                                op0=ALU.mult, op1=ALU.add))
            chain.link(dve.tensor_copy(gtab[:, :], bank[0:CAP, 5, NCOL:2 * NCOL]))
            dve.tensor_copy(tab[:, :], tabf[:, :]).then_inc(s_tab, 1)
            dve.wait_ge(s_tab, 1)
            for b in range(2):
                dve.tensor_copy(gidx[b][:, :], tab[:, b:b + 1]).then_inc(s_ix, 1)

            def name_gather(b, i):
                dve.wait_ge(s_gl[i], 16 * (b // 2) if type(b) is int else 8 * (b - i))
                dve.tensor_copy(gidx[i][:, :], tab[:, bass.ds(b, 1)]).then_inc(s_ix, 1)

            def name_scatter(b, i):
                if not (type(b) is int and b < 2):
                    dve.wait_ge(s_sc, 16 * b - 16)
                    dve.wait_ge(s_ya, b - 1)
                dve.tensor_copy(sidx[i][:, :], tab[:, bass.ds(b, 1)]).then_inc(s_sx2, 1)
                dve.tensor_copy(gcol[i][:, :], gtab[:, bass.ds(b, 1)]).then_inc(s_sx, 1)

            def weight_lo(j, b):
                h = e_raw[j].shape[1] // 2
                for half in range(2):
                    k = slice(h * half, h * half + h)
                    dve.wait_ge(s_eh[j], 2 * b + half + 1)
                    last = dve.tensor_tensor(e_lo[j][:, k, :], e_raw[j][:, k, :], e_hi[j][:, k, :].bitcast(F32), ALU.subtract)
                    if half == 0:
                        chain.done(last)
                last.then_inc(s_el[j], 1)

            def block_lo(b, i):
                dve.wait_ge(s_xe, b + 1)
                dve.tensor_tensor(xel[i][:, :, :], xT_ps[:, :, 0:CAP], xeh[i][:, :, :].bitcast(F32),
                                  ALU.subtract).then_inc(s_xc, 1)

            def hidden(b):
                dve.wait_ge(s_up, b + 1)
                dve.wait_ge(s_si, b + 1)
                since(dve, s_hT, b)
                dve.tensor_tensor(hid[:, :], up_ps, sgl[:, :], ALU.mult).then_inc(s_h, 1)

            def hidden_lo(b):
                dve.wait_ge(s_hh, b + 1)
                dve.tensor_tensor(hT_lo[:, :, :], hT_ps, hT_hi[:, :, :].bitcast(F32), ALU.subtract).then_inc(s_hl, 1)

            def right_half(b, i):
                dve.wait_ge(s_dp, 2 * b + 2)
                dve.wait_ge(s_sx, b + 1)
                dve.tensor_scalar(yo[i][:, 512:D], bank[0:CAP, 7, :], gcol[i][:, 0:1], None, ALU.mult).then_inc(s_yd, 1)

            def first_dve():
                name_gather(2, 0)
                weight_lo(0, 0)
                block_lo(0, 0)
                weight_lo(1, 0)
                block_lo(1, 1)
                weight_lo(2, 0)
                weight_lo(0, 1)

            def block_dve(i, b):
                hidden(b)
                hidden_lo(b)
                name_gather(b + 3, 1 - i)
                name_scatter(b, i)
                weight_lo(1, b + 1)
                if not (type(b) is int and b == NE - 2):
                    weight_lo(0, b + 2)
                right_half(b, i)
                block_lo(b + 2, i)
                weight_lo(2, b + 1)

            def last_dve(b):
                if b == NE - 2:
                    block_dve(0, b)
                else:
                    hidden(b)
                    hidden_lo(b)
                    name_gather(b + 3, 0)
                    name_scatter(b, 1)
                    right_half(b, 1)
                    block_lo(b + 2, 1)

            def further_dve(i, b):
                for j in range(3):
                    weight_lo(j, b)
                hidden(b)
                hidden_lo(b)
                name_gather(b + 3, 1 - i)
                name_scatter(b, i)
                right_half(b, i)
                block_lo(b + 2, i)

            blocks(dve, first_dve, block_dve, last_dve, further_dve)

        @block.tensor
        def _(pe):
            def transpose_x(t):
                r = ROWS[t]
                pe.wait_ge(s_xs, t + 1)
                if t == 0:
                    pe.wait_ge(s_ident, 1)
                else:
                    pe.wait_ge(s_xh, t)
                    pe.wait_ge(s_xl, t)
                for k in range(KT):
                    last = pe.transpose(xT_ps[:, k, 0:r], xt[t % 3][0:r, k * P:(k + 1) * P], ident[0:r, 0:r])
                last.then_inc(s_xT, 1)

            def freed(s):
                if s < NQK:
                    pe.wait_ge(s_kn, s + 1)
                else:
                    pe.wait_ge(s_v, s - NQK + 1)

            def project(s):
                kind, half, t = steps[s]
                r, n = ROWS[t], s // NT
                if s < NT:
                    pe.wait_ge(s_xl, t + 1)
                if t == 0:
                    pe.wait_ge(s_whi, n + 1)
                    pe.wait_ge(s_wlo, n + 1)
                if s >= 4:
                    freed(s - 4)
                for k in range(KT):
                    for j, (a, b) in enumerate(((xh, w_hi), (xh, w_lo), (xl, w_hi))):
                        last = pe.matmul(proj_ps(s)[0:r, :], a[:, k, row0(t):row0(t) + r], b[n % 2][:, k, :],
                                         start=(k == 0 and j == 0), stop=(k == KT - 1 and j == 2))
                last.then_inc(s_pr, 1)

            def transpose_heads(s):
                r = ROWS[steps[s][2]]
                pe.wait_ge(s_kn, s + 1)
                if s >= 2:
                    pe.wait_ge(s_ke, s - 1)
                for c in range(2):
                    last = pe.transpose(head_ps(s)[:, c, 0:r], kn[s % NKN][0:r, c * P:(c + 1) * P], ident[0:r, 0:r])
                last.then_inc(s_kt, 1)

            transpose_x(0)
            for s in range(NS + 2):
                if s + 1 < NT:
                    transpose_x(s + 1)
                if s < NS:
                    project(s)
                if 2 <= s < NQK + 2:
                    transpose_heads(s - 2)

            pe.wait_ge(s_hld, 16)
            pe.wait_ge(s_ke, NQK)
            n = DB * HIST
            for g in range(NG):
                last = pe.transpose(bank[:, 6, g * n:(g + 1) * n], hist[0:n, g * P:(g + 1) * P], ident[0:n, 0:n])
            last.then_inc(s_ht, 1)
            for i, (g, piece) in enumerate(usteps):
                s, n = NS + i, 6 + g // 2
                lo, cols = PIECES[piece]
                if i == 0 or i == NUS // 2:
                    pe.wait_ge(s_whi, n + 1)
                    pe.wait_ge(s_wlo, n + 1)
                if i < 4:
                    freed(s - 4)
                else:
                    pe.wait_ge(s_uc, u_copies(i - 4))
                c = (g % 2) * P
                for k in range(KT):
                    for j, (a, b) in enumerate(((w_hi, xh), (w_hi, xl), (w_lo, xh))):
                        last = pe.matmul(wide_ps(s)[:, 0:cols], a[n % 2][:, k, c:c + P], b[:, k, lo:lo + cols],
                                         start=(k == 0 and j == 0), stop=(k == KT - 1 and j == 2))
                last.then_inc(s_pr, 1)
            pe.wait_ge(s_uc, u_copies(NUS - 1))
            for g in range(NG):
                pe.transpose(bank[0:TAILP, 6, g * P:(g + 1) * P], u_ext[:, g, TP:16 + TP], ident[:, :])
            for g in range(NG):
                last = pe.transpose(bank[0:TS, 7, g * P:(g + 1) * P], us_cols[:, g, :], ident[:, :])
            last.then_inc(s_ut, 1)
            pe.wait_ge(s_cst2, 16 * NCONST)
            for i, (g, piece) in enumerate(usteps):
                lo, cols = PIECES[piece]
                pe.wait_ge(s_d, g + 1)
                if i >= 4:
                    pe.wait_ge(s_pl, i - 3)
                pe.matmul(wide_ps(NS + NUS + i)[:, 0:cols], wp_sb[:, g, :], dT[:, lo:lo + cols],
                          start=True, stop=True).then_inc(s_pm, 1)

            def scores(u):
                kind, w = units[u][0], width(u)
                if u == 0:
                    pe.wait_ge(s_pl, NUS)
                    pe.wait_ge(s_ur, 2)
                if u >= 2:
                    pe.wait_ge(s_sg, u if kind == "tail" else u - 1)
                z = z_ps(u)
                if kind == "full":
                    _, t, h = units[u]
                    rows = slice(64 * (h % 2), 64 * (h % 2) + 64)
                    for lo in range(0, w, 512):
                        n = min(512, w - lo)
                        last = pe.matmul(z[:, lo:lo + n], qT[rows, h // 2, row0(t):row0(t) + P],
                                         kT[rows, h // 2, lo:lo + n], start=True, stop=True)
                elif kind == "tail":
                    for j in range(4):
                        h = 4 * units[u][1] + j
                        rows = slice(64 * (h % 2), 64 * (h % 2) + 64)
                        for lo in range(0, w, 512):
                            n = min(512, w - lo)
                            last = pe.matmul(z[32 * j:32 * j + 32, lo:lo + n],
                                             qT[rows, h // 2, row0(LAST):row0(LAST) + TAIL_Q],
                                             kT[rows, h // 2, lo:lo + n], start=True, stop=True)
                else:
                    g = units[u][1]
                    if g == 0:
                        pe.wait_ge(s_qz, 1)
                    for j in range(SQ):
                        b = SQ * g + j
                        past_keys(b)
                        pe.wait_ge(s_te, key_group(b, HP - 1) + 1)
                        for hp in range(HP):
                            last = pe.matmul(z[32 * j:32 * j + 32, 0:PAST], qz[:, b, hp, :], kTs[:, hp, :],
                                             start=(hp == 0), stop=(hp == HP - 1))
                        last.then_inc(s_kTs, 1)
                        for hp in range(HP):
                            last = pe.matmul(z[32 * j:32 * j + 32, PAST:NKS], qz[:, b, hp, :],
                                             kT[:, hp, row0(LAST):T], start=(hp == 0), stop=(hp == HP - 1))
                last.then_inc(s_z, 1)

            def past_keys(b):
                i = b
                pe.wait_ge(s_kld[i % 2], 16 * NPG * (i // 2 + 1))
                for hp in range(HP):
                    n = key_group(b, hp)
                    pe.wait_ge(s_te, n - 1)
                    for j in range(NPG):
                        last = pe.transpose(t_ps(n)[:, j, :], pgk[i % 2][:, j, hp * P:(hp + 1) * P], ident[:, :])
                    last.then_inc(s_t, 1)

            def transpose_weights(u):
                pe.wait_ge(s_am, u + 1)
                lo, rows = NK - width(u), height(u)
                for j, group in enumerate(groups(u)):
                    n = first_group(u) + j
                    if n >= 2:
                        pe.wait_ge(s_te, n - 1)
                    for k, (c, keys) in enumerate(group):
                        last = pe.transpose(t_ps(n)[0:keys, k, 0:rows], am[u % 2][0:rows, lo + P * c:lo + P * c + keys],
                                            ident[0:rows, 0:rows])
                    last.then_inc(s_t, 1)

            def sum_values(u):
                kind = units[u][0]
                i, _ = out_of(u)
                pe.wait_ge(s_te, first_group(u) + len(groups(u)))
                if freed_by[outs[i]] is not None and (kind == "smp" or units[u][-1] == 0):
                    pe.wait_ge(s_ol, outs.index(freed_by[outs[i]]) + 1)
                ch = chunks(u)
                if kind == "full":
                    h = units[u][2]
                    for c, keys in ch:
                        last = pe.matmul(o_ps(i)[:, h * HD:(h + 1) * HD], aT[u % 2][0:keys, c, :],
                                         vv[0:keys, c, h * HD:(h + 1) * HD], start=(c == 0), stop=(c == ch[-1][0]))
                    last.then_inc(s_av, 1)
                elif kind == "tail":
                    for j in range(4):
                        h = 4 * units[u][1] + j
                        for c, keys in ch:
                            last = pe.matmul(o_ps(i)[0:TAILP, h * HD:(h + 1) * HD],
                                             aT[u % 2][0:keys, c, 32 * j:32 * j + TAILP],
                                             vv[0:keys, c, h * HD:(h + 1) * HD], start=(c == 0), stop=(c == ch[-1][0]))
                    last.then_inc(s_av, 1)
                else:
                    g = units[u][1]
                    for j in range(SQ):
                        b = SQ * g + j
                        pe.wait_ge(s_vld[b % 2], 16 * NPG * (b // 2 + 1))
                        for c, keys in ch:
                            values = pgv[b % 2][:, c, :] if c < NPG else vv[0:keys, LAST, :]
                            last = pe.matmul(o_ps(i)[32 * j:32 * j + 32, :], aT[u % 2][0:keys, c, 32 * j:32 * j + 32],
                                             values, start=(c == 0), stop=(c == ch[-1][0]))
                        last.then_inc(s_av, 1)

            def transpose_o(u):
                i, ends = out_of(u)
                if ends:
                    r, step = out_rows(i), P if tile_of(i) is not None else P - 2 * DS
                    pe.wait_ge(s_os, i + 1)
                    for c in range(HP):
                        last = pe.transpose(o_ps(i)[:, c * step:c * step + r], o_sb[0:r, c * P:(c + 1) * P],
                                            ident[0:r, 0:r])
                    last.then_inc(s_oT, 1)

            def out_product(s):
                n, t = wsteps[s]
                r = ROWS[t]
                if s == 0:
                    pe.wait_ge(s_sg, NU)
                    pe.wait_ge(s_ol, NOUT - 1)
                elif s == LAST:
                    pe.wait_ge(s_ol, NOUT)
                if wsteps.index((n, 0)) == s:
                    pe.wait_ge(s_whi, 8 + n + 1)
                    pe.wait_ge(s_wlo, 8 + n + 1)
                if s >= 4:
                    pe.wait_ge(s_xm, s - 3)
                for k in range(KT):
                    for j, (a, b) in enumerate(((xh, w_hi), (xh, w_lo), (xl, w_hi))):
                        last = pe.matmul(out_ps(s)[0:r, :], a[:, k, row0(t):row0(t) + r], b[n % 2][:, k, :],
                                         start=(k == 0 and j == 0), stop=(k == KT - 1 and j == 2))
                last.then_inc(s_wo, 1)

            for i in range(NU + 5):
                if i < NU:
                    scores(i)
                if 2 <= i < NU + 2:
                    transpose_weights(i - 2)
                if 5 <= i < NU + 5:
                    transpose_o(i - 5)
                if 3 <= i < NU + 3:
                    sum_values(i - 3)
                if i == NU + 3:
                    for s in range(2):
                        out_product(s)

            pe.wait_ge(s_wr, 48)

            def logits(t):
                r = ROWS[t]
                pe.wait_ge(s_n2c, t + 1)
                if t >= 2:
                    pe.wait_ge(s_lg, t - 1)
                for k in range(KT):
                    last = pe.matmul(logit_ps(t)[0:r, :], nT[t % 2][:, k, 0:r], w_r[:, k, :],
                                     start=(k == 0), stop=(k == KT - 1))
                last.then_inc(s_lgp, 1)

            def transpose_norm(t):
                r = ROWS[t]
                pe.wait_ge(s_n2, t + 1)
                if t >= 1:
                    pe.wait_ge(s_n2c, t)
                for k in range(KT):
                    last = pe.transpose(norm_ps(t)[:, k, 0:r], xg[t % 2][0:r, k * P:(k + 1) * P], ident[0:r, 0:r])
                last.then_inc(s_n2T, 1)

            def follow(t):
                if 0 <= t - 2 < NT:
                    transpose_norm(t - 2)
                if 0 <= t - 3 < NT:
                    logits(t - 3)

            for s in range(2, len(wsteps)):
                out_product(s)
                if wsteps[s][0] == 3:
                    follow(wsteps[s][1])
            for t in range(NT, NT + 3):
                follow(t)
            pe.wait_ge(s_eb, 1)
            marks = eb[:, :, :].rearrange("p t e -> p (t e)")
            pe.matmul(bank[:, 6, 0:NT * NE], before[:, :], marks, start=True, stop=True)
            pe.matmul(bank[:, 7, 0:NT * NE], ones[:, :], marks, start=True, stop=True).then_inc(s_rkp, 1)
            pe.wait_ge(s_ohr, 1)
            for t in range(NT):
                for k in range(2):
                    last = pe.matmul(bank[0:CAP, 5, 0:2 * NCOL], row_oh[:, t, k, :], col_oh[:, t, k, :],
                                     start=(t == 0 and k == 0), stop=(t == LAST and k == 1))
            last.then_inc(s_tbp, 1)

            def transpose_block(b, i, loaded):
                pe.wait_ge(s_gl[i], loaded)
                if not (type(b) is int and b == 0):
                    pe.wait_ge(s_xc, b)
                for k in range(KT):
                    last = pe.transpose(xT_ps[:, k, 0:CAP], xg[i][0:CAP, k * P:(k + 1) * P], ident[0:CAP, 0:CAP])
                last.then_inc(s_xt, 1)

            def turns(b, i):
                return 16 * (b // 2 + 1) if type(b) is int else 8 * (b - i) + 16

            def hidden_product(b, i, j, ks):
                ps, done = ((gate_ps(i), s_gp), (up_ps, s_up))[j]
                if ks[0] == 0:
                    pe.wait_ge(s_xc, b + 1)
                    pe.wait_ge(s_el[j], b + 1)
                    since(pe, *((s_si, b - 1), (s_h, b))[j])
                for k in ks:
                    for n, (x, w) in enumerate(((xeh, e_hi), (xeh, e_lo), (xel, e_hi))):
                        last = pe.matmul(ps, x[i][:, k, :], w[j][:, k, :], start=(k == 0 and n == 0),
                                         stop=(k == KT - 1 and n == 2))
                if ks[-1] == KT - 1:
                    last.then_inc(done, 1)

            def transpose_hidden(b):
                pe.wait_ge(s_h, b + 1)
                since(pe, s_hl, b)
                for ft in range(FT):
                    last = pe.transpose(hT_ps[:, ft, :], hid[:, ft * P:(ft + 1) * P], ident[0:CAP, 0:CAP])
                last.then_inc(s_hT, 1)

            def down_product(b):
                pe.wait_ge(s_hl, b + 1)
                pe.wait_ge(s_el[2], b + 1)
                for half, (m, done) in enumerate(((6, s_ya), (7, s_yd))):
                    since(pe, done, b)
                    for ft in range(FT):
                        for n, (x, w) in enumerate(((hT_hi, e_hi), (hT_hi, e_lo), (hT_lo, e_hi))):
                            last = pe.matmul(bank[0:CAP, m, :], x[:, ft, :], w[2][:, ft, 512 * half:512 * half + 512],
                                             start=(ft == 0 and n == 0), stop=(ft == FT - 1 and n == 2))
                    last.then_inc(s_dp, 1)

            def first_pe():
                for b in range(2):
                    transpose_block(b, b, 16)
                for j in range(2):
                    hidden_product(0, 0, j, range(KT))

            def block_pe(i, b):
                hidden_product(b + 1, 1 - i, 0, range(3))
                transpose_hidden(b)
                hidden_product(b + 1, 1 - i, 0, range(3, KT))
                down_product(b)
                transpose_block(b + 2, i, turns(b, i) + 16)
                hidden_product(b + 1, 1 - i, 1, range(KT))

            def last_pe(b):
                if b == NE - 2:
                    block_pe(0, b)
                else:
                    transpose_hidden(b)
                    down_product(b)
                    transpose_block(b + 2, 1, turns(b, 1) + 16)

            def further_pe(i, b):
                for j in range(2):
                    hidden_product(b, i, j, range(KT))
                transpose_hidden(b)
                down_product(b)
                transpose_block(b + 2, i, turns(b, i) + 16)

            blocks(pe, first_pe, block_pe, last_pe, further_pe)


_OUTS = {"y_all": (NY, D), "k_all": (T, AW), "v_all": (T, AW), "pool_p": (HIST, PW), "pool_s": (DB, HIST, PW)}
_LAYERED = ("cache_k", "cache_v", "state_pool", "w_in", "w_pool", "w_out", "w_group", "w_expert", "w_gate", "w_up",
            "w_down")


def kernel(**inputs):
    import numpy as np
    import concourse.bacc as bacc
    from concourse.bass_utils import run_bass_kernel_spmd

    nc = bacc.Bacc("TRN2", target_bir_lowering=False, num_devices=1)
    arrays, args = {}, {}
    for name, value in inputs.items():
        a = np.ascontiguousarray(value)
        arrays[f"in_{name}"] = a
        ap = nc.dram_tensor(f"in_{name}", a.shape, mybir.dt.from_np(a.dtype), kind="ExternalInput").ap()
        args[name] = ap[0] if name in _LAYERED else ap
    for name, shape in _OUTS.items():
        args[name] = nc.dram_tensor(f"out_{name}", shape, F32, kind="ExternalOutput").ap()
    hybrid_step(nc, **args)
    r = run_bass_kernel_spmd(nc, [arrays], core_ids=[0]).results[0]
    y, k, v = r["out_y_all"], r["out_k_all"], r["out_v_all"]
    return (y[META:TP].reshape(1, SEQ, D), y[TP:T].reshape(DB, DS, D),
            k[:TP].reshape(1, 1, TP, H, HD), v[:TP].reshape(1, 1, TP, H, HD), r["out_pool_p"].reshape(1, 1, HIST, PW),
            k[TP:].reshape(1, DB, DS, H, HD), v[TP:].reshape(1, DB, DS, H, HD),
            r["out_pool_s"].reshape(1, DB, HIST, PW))
```

```python
import math

import concourse.bass as bass
from concourse import mybir

F32 = mybir.dt.float32
F32R = mybir.dt.float32r
I32 = mybir.dt.int32
U32 = mybir.dt.uint32
ACT = mybir.ActivationFunctionType
ALU = mybir.AluOpType
AXX = mybir.AxisListType.X

P = 128
D = 1024
KT = D // P
SEQ, META = 1024, 16
TP = SEQ + META
DB, DS = 8, 4
TS = DB * DS
T = TP + TS
NT = -(-T // P)
ROWS = [min(P, T - P * t) for t in range(NT)]
LAST = NT - 1
TAILP = TP - P * LAST
H, HD = 8, 64
HP = H // 2
PW = 512
AW = H * HD
WINDOWS = (2, 4, 8, 16)
NG = len(WINDOWS)
HIST = 15
PAST, PAGE = 512, 128
NPG = PAST // PAGE
EPS = 1e-6
CG = 256
NK = TP
SQ = 2
TAIL_Q = 32
NKS = PAST + ROWS[-1]
PIECES = [(0, 512), (512, 512), (1024, T - 1024)]
UCOLS = -(-T // 3)
UPIECES = [(UCOLS * i, min(UCOLS, T - UCOLS * i)) for i in range(3)]
NE, NGRP, EPG = 32, 4, 8
F = D // 2
FT = F // P
CAP = 96
OVB = 2 * T // CAP
NBLK = NE + OVB
NCOL = NBLK + 3
OVMAX = -(-T // CAP) - 1
NY = T + CAP
NCONST = 4
RANK_BITS = 12
RANKS = 1 << RANK_BITS


def row0(t):
    return P * t


class Chain:

    def __init__(self, eng, sem):
        self.eng, self.sem, self.n = eng, sem, 0

    def done(self, ins):
        self.n += 1
        ins.then_inc(self.sem, 1)
        return self.n

    def settle(self):
        self.eng.wait_ge(self.sem, self.n)

    def link(self, ins):
        self.done(ins)
        self.settle()


def hybrid_step(nc, x_prompt, x_sample, cache_k, cache_v, state_pool, page_table, meta_tokens,
                norm_mix, w_in, g_q, g_k, sb_bias, w_pool, pool_scale, w_out, norm_ffn,
                w_group, w_expert, w_gate, w_up, w_down,
                y_all, k_all, v_all, pool_p, pool_s):
    base = 16512
    end = 229344

    def place(name, shape, dtype, at):
        size = 4
        for n in shape[1:]:
            size *= n
        size = -(-size // 32) * 32
        assert base <= at and at + size <= end, (name, at, size, end)
        return nc.alloc_sbuf_tensor_at(name, shape, dtype, offset=at), at + size

    at_x = base
    xh, at = place("xh", [P, KT, T], F32R, at_x)
    xl, at_w = place("xl", [P, KT, T], F32R, at)
    w_raw, w_hi, w_lo = [], [], []
    at = at_w
    for i in range(2):
        for lst, nm, dt in ((w_raw, "w_raw", F32), (w_hi, "w_hi", F32R), (w_lo, "w_lo", F32R)):
            tns, at = place(f"{nm}{i}", [P, KT, CG], dt, at)
            lst.append(tns)
    at_q = at
    qT, at = place("qT", [P, HP, T], F32, at_q)
    kT, at = place("kT", [P, HP, T], F32, at)
    junk, _ = place("junk", [P, D], F32, at)
    vv, at_m = place("vv", [P, NT, AW], F32, at)
    xt = []
    at = at_m
    for i in range(3):
        tns, at = place(f"xt{i}", [P, D], F32, at)
        xt.append(tns)
    gmix, at = place("gmix", [P, D], F32, at)
    NKN = 3
    sq, kn = [], []
    for i in range(2):
        tns, at = place(f"sq{i}", [P, CG], F32, at)
        sq.append(tns)
    for i in range(NKN):
        tns, at = place(f"kn{i}", [P, CG], F32, at)
        kn.append(tns)
    ss, at = place("ss", [P, 2], F32, at)
    rs, at = place("rs", [P, 2], F32, at)
    hs, at = place("hs", [P, 2, 4], F32, at)
    hr, at = place("hr", [P, 2, 4], F32, at)
    at_c = at
    wp_sb, at = place("wp_sb", [P, NG, P], F32, at_c)
    hist, at = place("hist", [P, PW], F32, at)
    up_rows, at = place("up_rows", [TAILP, PW], F32, at)
    us_rows, at = place("us_rows", [TS, PW], F32, at)
    ident, at = place("ident", [P, P], F32, at)
    gq_bc, at = place("gq_bc", [P, HD], F32, at)
    gk_bc, at = place("gk_bc", [P, HD], F32, at)
    bias_bc, at = place("bias_bc", [P, H], F32, at)
    bias_tail, at = place("bias_tail", [P, 2], F32, at)
    bias_smp, at = place("bias_smp", [P, 1], F32, at)
    diag_mask, at = place("diag_mask", [P, P], F32, at)
    tail_mask, at = place("tail_mask", [P, TAILP], F32, at)
    smp_mask, at = place("smp_mask", [P, DB // SQ, ROWS[-1]], F32, at)
    pscale, at = place("pscale", [P, NG], F32, at)
    rcnt, at = place("rcnt", [P, 16], F32, at)
    pint, at = place("pint", [P, 4], I32, at)
    pflt, at = place("pflt", [P, 8], F32, at)
    col48, at = place("col48", [P, ROWS[-1]], F32, at)
    us_cols, at = place("us_cols", [P, NG, TS], F32, at)
    pt_sb, at = place("pt_sb", [1, DB * NPG], I32, at)
    at_u = at
    u_ext, at = place("u_ext", [P, NG, 16 + TP], F32, at_m)
    es, at = place("es", [P, NG, DB, 20], F32, at)
    d_tail, at = place("d_tail", [P, NG, ROWS[-1]], F32, at)
    wsmall = []
    for i in range(2):
        tns, at = place(f"wsmall{i}", [P, DB, 20], F32, at)
        wsmall.append(tns)
    assert at <= at_c
    wsum, at = [], at_u
    for i in range(2):
        tns, at = place(f"wsum{i}", [P, 16 + TP], F32, at)
        wsum.append(tns)
    sg, am, pb, aT = [], [], [], []
    pgv0, at = place("pgv0", [PAGE, NPG, AW], F32, at_w)
    for i in range(2):
        for lst, nm, shape in ((sg, "sg", [P, NK]), (am, "am", [P, NK]), (pb, "pb", [P, NK + 1]),
                               (aT, "aT", [P, NT, P])):
            tns, at = place(f"{nm}{i}", shape, F32, at)
            lst.append(tns)
    o_sb, at = place("o_sb", [P, AW], F32, at)
    assert at <= at_q, (at, at_q)
    pgk = []
    at = at_m
    for i in range(2):
        tns, at = place(f"pgk{i}", [PAGE, NPG, AW], F32, at)
        pgk.append(tns)
    qz, at = place("qz", [P, HP, DB, 32], F32, at)
    assert at <= at_c
    pgv = [pgv0, place("pgv1", [PAGE, NPG, AW], F32, at_c)[0]]
    kTs, at_end = place("kTs", [P, HP, PAST], F32, at_u)
    w_r, at = place("w_r", [P, KT, NGRP + NE], F32, at_u + 4 * D)
    lg, at = place("lg", [P, NT, NGRP + NE], F32, at)
    xmid, at_e = place("xmid", [P, NT, D], F32, at_q)
    def weights(nm, dtype, places):
        shapes = ([P, KT, F], [P, KT, F], [P, FT, D])
        return [place(f"{nm}{j}", shapes[j], dtype, at)[0] for j, at in enumerate(places)]

    size = 4 * KT * F
    e_raw = weights("e_raw", F32, [at_x, at_x + size, at_x + 2 * size])
    e_hi = weights("e_hi", F32R, [at_w, at_w + 2 * size, at_q])
    e_lo = weights("e_lo", F32R, [at_w + size, at_e, at_q + size])
    at_r = at_x + 3 * size
    assert at_w + 3 * size <= at_q and at_q + 2 * size <= at_e
    xg, xeh, xel, yo, gidx, sidx, gcol = [], [], [], [], [], [], []
    at = at_e + size
    for i in range(2):
        tns, at = place(f"xg{i}", [P, D], F32, at)
        xg.append(tns)
    at_x2 = at
    for i in range(2):
        for lst, nm, shape, dt in ((xeh, "xeh", [P, KT, CAP], F32R), (xel, "xel", [P, KT, CAP], F32R),
                                   (gidx, "gidx", [CAP, 1], I32), (sidx, "sidx", [CAP, 1], I32), (gcol, "gcol", [CAP, 1], F32)):
            tns, at = place(f"{nm}{i}", shape, dt, at)
            lst.append(tns)
    assert at <= at_c, (at, at_c)
    at = at_c
    for i in range(2):
        tns, at = place(f"yo{i}", [CAP, D], F32, at)
        yo.append(tns)
    zrow, _ = place("zrow", [CAP, D], F32, at_c)
    row_oh, _ = place("row_oh", [P, NT, 2, CAP], F32, at_u)
    hT_hi, at = place("hT_hi", [P, FT, CAP], F32R, at_u)
    hT_lo, at = place("hT_lo", [P, FT, CAP], F32R, at)
    sgl, at = place("sgl", [CAP, F], F32, at)
    hid, at = place("hid", [CAP, F], F32, at)
    gffn, at = place("gffn", [P, D], F32, at_u)
    nT = [place(f"nT{i}", [P, KT, P], F32, at_e + 4 * D * i)[0] for i in range(2)]
    junk2, at = place("junk2", [P, D], F32, at_e + 8 * D)
    assert at <= at_e + size
    col_oh, at = place("col_oh", [P, NT, 2, 2 * NCOL], F32, at_x2)
    assert at <= at_x2 + 16 * KT * CAP
    small, small_at = {}, {}
    at = at_r
    for nm, shape, dt in (("gmx", [P, NT], F32), ("goh", [P, NT, NGRP], F32), ("gex", [P, NT, NGRP], F32),
                          ("gw", [P, NT], F32), ("le", [P, NT, EPG], F32), ("tmp8", [P, NT, EPG], F32),
                          ("oh", [P, 2, NT, EPG], F32), ("mx", [P, 2, NT], F32), ("gt", [P, 2, NT], F32),
                          ("ek", [P, 2, NT, NE], F32), ("eb", [P, NT, NE], F32), ("cum", [P, NT, NE], F32),
                          ("key", [P, 2, NT], F32), ("keyi", [P, 2, NT], I32),
                          ("fieldi", [P, 3, 2, NT], I32), ("field", [P, 3, 2, NT], F32), ("kcol", [P, NE], F32),
                          ("bk", [P, 2, NT], F32), ("rw", [P, 2, NT], F32), ("cl", [P, 2, NT], F32),
                          ("cnt", [P, NE], F32), ("nov", [P, NE], F32), ("ovend", [P, NE], F32), ("ovst", [P, NE], F32),
                          ("tab", [CAP, NCOL], I32), ("tabf", [CAP, NCOL], F32), ("vld", [CAP, NCOL], F32),
                          ("gtab", [CAP, NCOL], F32), ("valid", [P, NT], F32), ("tok", [P, NT], F32),
                          ("io4", [P, NGRP], F32), ("io8", [P, EPG], F32), ("io128", [P, P], F32), ("io_one", [P, P], F32),
                          ("jt", [P, OVMAX], F32),
                          ("prow", [P, 1], F32), ("nprow", [P, 1], F32), ("before", [P, P], F32), ("ones", [P, P], F32),
                          ("cmp", [P, NE, OVMAX], F32), ("ovm", [1, 32], F32), ("ovmi", [1, 32], I32), ("rsum", [P, NT], F32)):
        small_at[nm] = at
        small[nm], at = place(nm, shape, dt, at)
    assert at <= at_w, (at, at_w)
    past, at = place("past", [1, OVB, NE], F32, small_at["ek"])
    assert at <= small_at["cum"]
    (gmx, goh, gex, gw, le, tmp8, oh, mx, gt, ek, eb, cum, key, keyi, fieldi, field, kcol, bk, rw, cl, cnt, nov, ovend, ovst,
     tab, tabf, vld, gtab, valid, tok, io4, io8, io128, io_one, jt, prow, nprow, before, ones, cmp_, ovm, ovmi, rsum) = small.values()

    bank = nc.alloc_psum_tensor("bank", [P, 8, 512], F32)
    xT_ps = bank[:, 0:2, :].rearrange("p b (c n) -> p (b c) n", n=P)

    def proj_ps(s):
        return bank[:, 2 + turn(s) % 4, 0:CG]

    def head_ps(s):
        return bank[:, 6 + s % 2, 0:2 * P].rearrange("p (c n) -> p c n", n=P)


    def z_ps(u):
        kind = units[u][0]
        b0 = 0 if kind == "tail" else 2 * (u % 2)
        return bank[:, b0:b0 + (3 if kind == "tail" else 2), :].rearrange("p b n -> p (b n)")

    def t_ps(n):
        return bank[:, 4 + n % 2, :].rearrange("p (c n) -> p c n", n=P)

    units = []
    NSG = DB // SQ
    for t in range(LAST):
        for h in range(H):
            if h == H // 2 and 1 <= t < 1 + NSG:
                units.append(("smp", t - 1))
            units.append(("full", t, h))
    units += [("tail", 0), ("tail", 1)]
    NU = len(units)

    def width(u):
        kind = units[u][0]
        return P * (units[u][1] + 1) if kind == "full" else TP if kind == "tail" else NKS

    def height(u):
        return 32 * SQ if units[u][0] == "smp" else P

    def chunks(u):
        return [(c, min(P, width(u) - P * c)) for c in range(-(-width(u) // P))]

    def groups(u):
        ch = chunks(u)
        return [ch[i:i + 4] for i in range(0, len(ch), 4)]

    first_of_weights, first_of_keys, count = {}, {}, 0
    for i in range(NU + 2):
        if i < NU and units[i][0] == "smp":
            first_of_keys[units[i][1]] = count
            count += SQ * HP
        if i >= 2:
            first_of_weights[i - 2] = count
            count += len(groups(i - 2))

    def first_group(u):
        return first_of_weights[u]

    def key_group(b, hp):
        return first_of_keys[b // SQ] + (b % SQ) * HP + hp

    def summed_at(u):
        return sum(SQ if unit[0] == "smp" else 1 for unit in units[:u + 1])

    def smp_summed(b):
        return summed_at(units.index(("smp", b // SQ)) - 1) + b % SQ + 1

    def smp_out(x, g, rows):
        lo = TP + SQ * DS * g
        return x[rows, HP:KT, lo:lo + SQ * DS].rearrange("p c (b j) -> p b c j", j=DS)

    def smp_in(i, half, rows):
        v = o_ps(i)[rows, :].rearrange("p (c b e) -> p b c e", c=HP, e=32)
        return v[:, 0:SQ, :, DS * half:DS * half + DS]

    def use_of(unit):
        return ("smp", unit[1]) if unit[0] == "smp" else ("tile", unit[1] if unit[0] == "full" else LAST)

    outs, out_bank, freed_by, last_in = [], {}, {}, {}
    for u, unit in enumerate(units):
        use = use_of(unit)
        if use not in out_bank:
            out_bank[use] = use[1] % 2 if use[0] == "tile" else 1 - units[u - 1][1] % 2
            freed_by[use] = last_in.get(out_bank[use])
            last_in[out_bank[use]] = use
        if use not in [use_of(later) for later in units[u + 1:]]:
            outs.append(use)
    NOUT = len(outs)

    def out_of(u):
        use = use_of(units[u])
        return outs.index(use), use not in [use_of(later) for later in units[u + 1:]]

    def o_ps(i):
        return bank[:, 6 + out_bank[outs[i]], :]

    def tile_of(i):
        return outs[i][1] if outs[i][0] == "tile" else None

    def out_rows(i):
        return 32 * SQ if tile_of(i) is None else P if tile_of(i) < LAST else TAILP

    def sem(name):
        return nc.alloc_semaphore(name)

    s_const = sem("gain_loaded")
    s_gain = sem("head_gains_loaded")
    s_ident = sem("ident_ready")
    s_xld = [sem(f"x_loaded{i}") for i in range(3)]
    s_wld = [sem(f"w_loaded{i}") for i in range(2)]
    s_whi = sem("w_hi_ready")
    s_wlo = sem("w_lo_ready")
    s_ssq = sem("sumsq_ready")
    s_ms = sem("meansq_ready")
    s_rms = sem("rms_ready")
    s_xs = sem("x_normed")
    s_xT = sem("x_transposed")
    s_xh = sem("x_hi_ready")
    s_xl = sem("x_lo_ready")
    s_pr = sem("projected")
    s_sq = sem("head_squares")
    s_hms = sem("head_meansq")
    s_hrms = sem("head_rms")
    s_kn = sem("qk_normed")
    s_kt = sem("qk_transposed")
    s_ke = sem("qk_copied")
    s_v = sem("v_copied")
    s_kst = [sem(f"k_stored{i}") for i in range(NKN)]
    s_vst = sem("v_stored")
    s_cst2 = sem("more_const_loaded")
    s_mask = sem("masks_ready")
    s_hld = sem("history_loaded")
    s_ht = sem("history_transposed")
    s_uc = sem("u_copied")
    s_ut = sem("u_rows_transposed")
    s_ur = sem("u_rows_copied")
    s_ust = sem("u_rows_stored")
    s_uscr = sem("u_rows_in_scratch")
    s_d = sem("pool_diff_ready")
    s_pm = sem("pool_product")
    s_ph = sem("pool_hi_ready")
    s_pl = sem("pool_lo_ready")
    s_pad = sem("zero_history")
    s_z = sem("scores")
    s_sg = sem("sigmoid_ready")
    s_am = sem("weights_ready")
    s_t = sem("banks_transposed")
    s_te = sem("banks_copied")
    s_av = sem("values_summed")
    s_os = sem("o_copied")
    s_oT = sem("o_transposed")
    s_oh = sem("o_hi_ready")
    s_ol = sem("o_lo_ready")
    s_kld = [sem(f"k_page_loaded{i}") for i in range(2)]
    s_vld = [sem(f"v_page_loaded{i}") for i in range(2)]
    s_kTs = sem("past_k_copied")
    s_qz = sem("q_spread")
    s_xr = [sem(f"residual_loaded{t}") for t in range(NT)]
    s_wo = sem("w_out_product")
    s_xm = sem("residual_added")
    s_wr = sem("router_weights_loaded")
    s_tbl = sem("router_tables_ready")
    s_zr = sem("zero_rows_ready")
    s_ssq2 = sem("sumsq2_ready")
    s_ms2 = sem("meansq2_ready")
    s_rms2 = sem("rms2_ready")
    s_n2 = sem("ffn_normed")
    s_n2T = sem("ffn_transposed")
    s_n2c = sem("ffn_copied")
    s_lgp = sem("logits_product")
    s_lg = sem("logits_ready")
    s_nst = [sem(f"rows_stored{i}") for i in range(2)]
    s_yst = sem("residual_stored")
    s_gx = sem("group_shifted")
    s_ge = sem("group_exp")
    s_eb = sem("experts_marked")
    s_rkp = sem("ranks_product")
    s_ohr = sem("slot_one_hots")
    s_tbp = sem("tables_product")
    s_tab = sem("tables_ready")
    s_wl = [[sem(f"{nm}_loaded{half}") for half in range(2)] for nm in ("gate", "up", "down")]
    s_eh = [sem(f"{nm}_hi_ready") for nm in ("gate", "up", "down")]
    s_el = [sem(f"{nm}_lo_ready") for nm in ("gate", "up", "down")]
    s_ix = sem("gather_rows_named")
    s_sx = sem("block_gates_ready")
    s_sx2 = sem("scatter_rows_named")
    s_gl = [sem(f"gathered{i}") for i in range(2)]
    s_xt = sem("block_transposed")
    s_xe = sem("block_hi_ready")
    s_xc = sem("block_lo_ready")
    s_hT = sem("hidden_transposed")
    s_hh = sem("hidden_hi_ready")
    s_hl = sem("hidden_lo_ready")
    s_gp = sem("gate_product")
    s_up = sem("up_product")
    s_si = sem("silu_ready")
    s_h = sem("hidden_ready")
    s_dp = sem("down_product")
    s_ya = sem("left_half_gated")
    s_yd = sem("right_half_gated")
    s_sc = sem("block_scattered")
    s_dve = sem("dve_chain")
    s_act = sem("act_chain")
    s_pool = sem("pool_chain")

    order = [("k", 0), ("k", 1), ("q", 0), ("q", 1), ("u", 0), ("u", 1), ("v", 0), ("v", 1)]
    first_col = {"u": 0, "q": PW, "k": PW + AW, "v": PW + 2 * AW}
    steps = []
    for i in range(NT + 2):
        steps += [("k", 0, i)] if i < NT else []
        steps += [("k", 1, i - 2)] if i >= 2 else []
    steps += [(kind, half, t) for kind, half in (("q", 0), ("q", 1), ("v", 0), ("v", 1)) for t in range(NT)]
    NS = len(steps)
    NQK = 4 * NT
    assert all(steps[s][0] in "qk" for s in range(NQK))

    usteps = [(g, piece) for g in range(NG) for piece in range(3)]
    NUS = len(usteps)

    def turn(s):
        return s if s < NQK else s + NUS

    ends = [steps.index(("k", 0, LAST)) + 1, 2 * NT, 3 * NT, 4 * NT, NQK + NUS // 2, NQK + NUS, NQK + NUS + NT, NS + NUS]
    assert D // CG == 4
    wsteps = [(n, t) for n in range(2) for t in range(NT)]
    for i in range(NT + 2):
        wsteps += [(2, i)] if i < NT else []
        wsteps += [(3, i - 2)] if i >= 2 else []

    def tile_done(t):
        return wsteps.index((3, t)) + 1

    def out_ps(s):
        return bank[:, s % 4, 0:CG]

    def logit_ps(t):
        return bank[:, 6 + t % 2, 0:NGRP + NE]

    def norm_ps(t):
        return bank[:, 4:6, :].rearrange("p b (c n) -> p (b c) n", n=P)

    def wide_ps(s):
        return bank[:, 2 + s % 4, :]

    def pool_ps(i):
        return bank[:, 4 + i % 4, :]

    def u_copies(i):
        return 1 + i + 1 + 2 * ((i + 1) // 3)

    u_scr = nc.dram_tensor("u_scr", [TS, PW], F32).ap()
    w_in_v = w_in.rearrange("(kt p) e -> p kt e", p=P)
    n_scr = nc.dram_tensor("n_scr", [NY, D], F32).ap()
    gate_v = w_gate.rearrange("e (kt p) f -> e p kt f", p=P)
    up_v = w_up.rearrange("e (kt p) f -> e p kt f", p=P)
    down_v = w_down.rearrange("e (ft p) d -> e p ft d", p=P)
    w_out_v = w_out.rearrange("(kt p) e -> p kt e", p=P)

    def gate_ps(i):
        return bank[0:CAP, 2 + i, :]

    up_ps = bank[0:CAP, 4, :]
    hT_ps = bank[:, 5, 0:FT * CAP].rearrange("p (f n) -> p f n", f=FT)

    def since(eng, sem, value):
        if not (type(value) is int and value <= 0):
            eng.wait_ge(sem, value)

    def blocks(eng, first, body, last, further):
        first()
        for b in range(2):
            body(b, b)
        with eng.Fori(1, NE // 2 - 1) as i:
            for k in range(2):
                body(k, 2 * i + k)
        for b in range(NE - 2, NE):
            last(b)
        eng.wait_ge(s_tab, 1)
        n_over = eng.value_load(ovmi[0:1, OVB:OVB + 1], min_val=0, max_val=OVB)
        with eng.If(n_over > 0):
            with eng.Fori(0, OVB // 2) as i:
                for k in range(2):
                    with eng.If(n_over > 2 * i + k):
                        further(k, 2 * i + k + NE)

    blk = nc.Block()

    with nc.allow_non_contiguous_dma(reason="small vectors and broadcasts"), blk as block:

        @block.sync
        def _(sp):
            def load_x(t):
                if t >= 3:
                    sp.wait_ge(s_xT, t - 2)
                lo = P * t - META
                if t == 0:
                    sp.dma_start(xt[0][0:META, :], meta_tokens).then_inc(s_xld[0], 16)
                    sp.dma_start(xt[0][META:P, :], x_prompt[0, 0:P - META, :]).then_inc(s_xld[0], 16)
                elif t < LAST:
                    sp.dma_start(xt[t % 3][:, :], x_prompt[0, lo:lo + P, :]).then_inc(s_xld[t % 3], 32)
                else:
                    sp.dma_start(xt[t % 3][0:TAILP, :], x_prompt[0, lo:SEQ, :]).then_inc(s_xld[t % 3], 16)
                    sp.dma_start(xt[t % 3][TAILP:TAILP + TS, :],
                                 x_sample.rearrange("b s d -> (b s) d")).then_inc(s_xld[t % 3], 16)

            def load_w(n):
                kind, half = order[n]
                c = first_col[kind] + half * CG
                if n >= 2:
                    sp.wait_ge(s_whi, n - 1)
                    sp.wait_ge(s_wlo, n - 1)
                sp.dma_start(w_raw[n % 2][:, :, :], w_in_v[:, :, c:c + CG]).then_inc(s_wld[n % 2], 16)

            load_x(0)
            sp.dma_start(gmix[:, :], norm_mix.to_broadcast([P, D])).then_inc(s_const, 16)
            load_x(1)
            load_w(0)
            load_x(2)
            load_w(1)
            load_x(3)
            sp.dma_start(gq_bc[:, :], g_q.to_broadcast([P, HD])).then_inc(s_gain, 16)
            sp.dma_start(gk_bc[:, :], g_k.to_broadcast([P, HD])).then_inc(s_gain, 16)
            for s in range(NQK):
                kind, half, t = steps[s]
                if s == 0:
                    load_x(4)
                if s < 3:
                    load_x(s + 5)
                elif (kind, half) == ("k", 1) and t + 8 < NT:
                    load_x(t + 8)
                if s % NT == 5 and s // NT + 2 < 6:
                    load_w(s // NT + 2)
                if s == 2 * NT:
                    sp.dma_start(hist[0:DB * HIST, :], state_pool.rearrange("b h w -> (b h) w")).then_inc(s_hld, 16)
                    consts = [(bias_bc[:, :], sb_bias.to_broadcast([P, H])),
                              (wp_sb[:, :, :], w_pool.rearrange("g c e -> c g e")),
                              (pscale[:, :], pool_scale.rearrange("a (g c) -> c (a g)", c=P)),
                              (pt_sb[:, :], page_table.rearrange("(a b) j -> a (b j)", a=1))]
                    assert len(consts) == NCONST
                    for out, src in consts:
                        sp.dma_start(out, src).then_inc(s_cst2, 16)
                r = ROWS[t]
                if kind == "k":
                    sp.wait_ge(s_kn, s + 1)
                    sp.dma_start(k_all[row0(t):row0(t) + r, half * CG:half * CG + CG],
                                 kn[s % NKN][0:r, :]).then_inc(s_kst[s % NKN], 16)
            load_w(6)
            load_w(7)
            sp.wait_ge(s_ur, 2)
            sp.dma_start(pool_p, up_rows[TAILP - HIST:TAILP, :]).then_inc(s_ust, 16)
            sp.dma_start(u_scr, us_rows[:, :]).then_inc(s_uscr, 16)
            sp.dma_start(pool_s[:, 0:HIST - DS, :], state_pool[:, DS:HIST, :]).then_inc(s_ust, 16)
            sp.wait_ge(s_uscr, 16)
            sp.dma_start(pool_s[:, HIST - DS:HIST, :],
                         u_scr.rearrange("(b s) w -> b s w", s=DS)).then_inc(s_ust, 16)
            for s in range(NQK, NS):
                _, half, t = steps[s]
                r = ROWS[t]
                sp.wait_ge(s_v, s - NQK + 1)
                sp.dma_start(v_all[row0(t):row0(t) + r, half * CG:half * CG + CG],
                             vv[0:r, t, half * CG:half * CG + CG]).then_inc(s_vst, 16)
            sp.wait_ge(s_cst2, 16 * NCONST)
            sp.wait_ge(s_pm, NUS)
            sp.wait_ge(s_d, NG)
            sp.wait_ge(s_pl, NUS)
            sp.wait_ge(s_ut, 1)
            sp.wait_ge(s_ust, 48)

            def load_pages(cache, buf, loaded, b):
                for j in range(NPG):
                    page = sp.value_load(pt_sb[0:1, b * NPG + j:b * NPG + j + 1], min_val=0,
                                         max_val=cache_k.shape[0] - 1)
                    src = cache[bass.ds(page, 1), :, :, :]
                    sp.dma_start(buf[:, j, :], src.rearrange("a p h d -> (a p) (h d)")).then_inc(loaded, 16)

            for g in range(NSG):
                for b in range(SQ * g, SQ * g + SQ):
                    if b >= 2:
                        sp.wait_ge(s_t, key_group(b - 2, HP - 1) + 1)
                    load_pages(cache_k, pgk[b % 2], s_kld[b % 2], b)
                for b in range(SQ * g, SQ * g + SQ):
                    if b >= 2:
                        sp.wait_ge(s_av, smp_summed(b - 2))
                    load_pages(cache_v, pgv[b % 2], s_vld[b % 2], b)

            def load_w_out(n):
                if n >= 2:
                    sp.wait_ge(s_whi, 8 + n - 1)
                    sp.wait_ge(s_wlo, 8 + n - 1)
                sp.dma_start(w_raw[n % 2][:, :, :], w_out_v[:, :, n * CG:n * CG + CG]).then_inc(s_wld[n % 2], 16)

            sp.wait_ge(s_av, smp_summed(DB - 1))
            load_w_out(0)
            sp.wait_ge(s_kTs, DB * HP)
            sp.dma_start(gffn[:, :], norm_ffn.to_broadcast([P, D])).then_inc(s_wr, 16)
            sp.dma_start(w_r[:, :, 0:NGRP], w_group.rearrange("(kt p) e -> p kt e", p=P)).then_inc(s_wr, 16)
            sp.dma_start(w_r[:, :, NGRP:NGRP + NE], w_expert.rearrange("(kt p) e -> p kt e", p=P)).then_inc(s_wr, 16)
            sp.wait_ge(s_av, summed_at(NU - 1))
            load_w_out(1)
            for t in range(NT):
                lo = P * t - META
                if t == 0:
                    sp.dma_start(xmid[0:META, 0, :], meta_tokens).then_inc(s_xr[t], 16)
                    sp.dma_start(xmid[META:P, 0, :], x_prompt[0, 0:P - META, :]).then_inc(s_xr[t], 16)
                elif t < LAST:
                    sp.dma_start(xmid[:, t, :], x_prompt[0, lo:lo + P, :]).then_inc(s_xr[t], 32)
                else:
                    sp.dma_start(xmid[0:TAILP, t, :], x_prompt[0, lo:SEQ, :]).then_inc(s_xr[t], 16)
                    sp.dma_start(xmid[TAILP:TAILP + TS, t, :],
                                 x_sample.rearrange("b s d -> (b s) d")).then_inc(s_xr[t], 16)
            load_w_out(2)
            load_w_out(3)

            def load_part(j, e, b):
                part = (gate_v, up_v, down_v)[j][bass.ds(e, 1)].rearrange("a p k f -> (a p) k f")
                h = e_raw[j].shape[1] // 2
                for half in range(2):
                    since(sp, s_el[j], 2 * b - 1 + half)
                    k = slice(h * half, h * half + h)
                    sp.dma_start(e_raw[j][:, k, :], part[:, k, :]).then_inc(s_wl[j][half], 16)

            sp.wait_ge(s_zr, 1)
            sp.dma_start(n_scr[T:NY, :], zrow[:, :]).then_inc(s_yst, 16)
            sp.dma_start(y_all[T:NY, :], zrow[:, :]).then_inc(s_yst, 16)
            for t in range(NT):
                r = ROWS[t]
                sp.wait_ge(s_n2, t + 1)
                sp.dma_start(n_scr[row0(t):row0(t) + r, :], xg[t % 2][0:r, :]).then_inc(s_nst[t % 2], 16)
                sp.dma_start(y_all[row0(t):row0(t) + r, :], xmid[0:r, t, :]).then_inc(s_yst, 16)
            sp.wait_ge(s_wo, len(wsteps))
            load_part(0, 0, 0)
            load_part(1, 0, 0)
            load_part(2, 0, 0)
            load_part(0, 1, 1)
            load_part(1, 1, 1)
            for i in range(2):
                sp.wait_ge(s_gl[i], 16)
            load_part(2, 1, 1)
            load_part(0, 2, 2)
            load_part(1, 2, 2)
            with sp.Fori(3, NE) as b:
                load_part(0, b, b)
                load_part(2, b - 1, b - 1)
                load_part(1, b, b)
            load_part(2, NE - 1, NE - 1)
            sp.wait_ge(s_tab, 1)
            n_over = sp.value_load(ovmi[0:1, OVB:OVB + 1], min_val=0, max_val=OVB)
            with sp.If(n_over > 0):
                with sp.Fori(0, OVB) as o:
                    with sp.If(n_over > o):
                        e = sp.value_load(ovmi[0:1, bass.ds(o, 1)], min_val=0, max_val=NE - 1)
                        for j in range(3):
                            load_part(j, e, o + NE)
            for i in range(NKN):
                sp.wait_ge(s_kst[i], 16 * len([s for s in range(2 * NT) if s % NKN == i]))
            sp.wait_ge(s_vst, 16 * 2 * NT)

        @block.gpsimd
        def _(pool):
            chain = Chain(pool, s_pool)
            chain.link(pool.memset(ident[:, :], 1.0))
            pool.affine_select(out=ident[:, :], in_=ident[:, :], compare_op=ALU.is_equal, fill=0.0, base=0,
                               pattern=[[-1, P]], channel_multiplier=1).then_inc(s_ident, 1)
            chain.link(pool.memset(diag_mask[:, :], 1.0))
            chain.link(pool.affine_select(out=diag_mask[:, :], in_=diag_mask[:, :], compare_op=ALU.is_gt, fill=0.0,
                                          base=0, pattern=[[-1, P]], channel_multiplier=1))
            chain.link(pool.memset(tail_mask[:, :], 1.0))
            for j in range(4):
                part = tail_mask[32 * j:32 * j + 32, :]
                chain.link(pool.affine_select(out=part, in_=part, compare_op=ALU.is_gt, fill=0.0, base=0,
                                              pattern=[[-1, TAILP]], channel_multiplier=1))
            chain.link(pool.iota(pint[:, 0:1], [[0, 1]], base=0, channel_multiplier=1))
            chain.link(pool.iota(col48[:, :], [[1, ROWS[-1]]], base=0, channel_multiplier=0,
                                 allow_small_or_imprecise_dtypes=True))
            pool.iota(rcnt[:, :], [[1, 16]], base=1, channel_multiplier=0,
                      allow_small_or_imprecise_dtypes=True).then_inc(s_mask, 1)
            pool.wait_ge(s_kn, NQK)
            pool.wait_ge(s_kt, NQK)
            pool.wait_ge(s_xT, NT)
            for i in range(NKN):
                pool.wait_ge(s_kst[i], 16 * len([s for s in range(2 * NT) if s % NKN == i]))
            chain.link(pool.memset(u_ext[:, :, 0:16], 0.0))
            pool.memset(es[:, :, :, 0:1], 0.0).then_inc(s_pad, 1)
            pool.wait_ge(s_pl, NUS)
            pool.wait_ge(s_ut, 1)
            pool.memset(qz[:, :, :, :], 0.0).then_inc(s_pad, 1)
            pool.wait_ge(s_kTs, DB * HP)
            pool.wait_ge(s_te, key_group(DB - 1, HP - 1) + 1)
            pool.wait_ge(s_av, summed_at(NU - 1))
            chain.link(pool.memset(zrow[:, :], 0.0))
            pool.memset(lg[:, LAST, :], 0.0).then_inc(s_zr, 1)
            pool.wait_ge(s_zr, 1)
            pool.wait_ge(s_wo, len(wsteps))
            chain.link(pool.memset(ones[:, :], 1.0))
            chain.link(pool.memset(before[:, :], 1.0))
            chain.link(pool.affine_select(out=before[:, :], in_=before[:, :], compare_op=ALU.is_gt, fill=0.0,
                                          base=0, pattern=[[1, P]], channel_multiplier=-1))
            for out, pattern, first, mult in ((tok[:, :], [[P, NT]], -T, 1), (io4[:, :], [[1, NGRP]], -NGRP, 0),
                                              (io8[:, :], [[1, EPG]], -EPG, 0), (io128[:, :], [[1, P]], 0, 0), (io_one[:, :], [[1, P]], 1, 0),
                                              (jt[:, :], [[CAP, OVMAX]], CAP, 0), (nprow[:, :], [[0, 1]], 0, -1)):
                chain.link(pool.iota(out, pattern, base=first, channel_multiplier=mult,
                                     allow_small_or_imprecise_dtypes=True))
            pool.iota(prow[:, :], [[0, 1]], base=T, channel_multiplier=1,
                      allow_small_or_imprecise_dtypes=True).then_inc(s_tbl, 1)

            pool.wait_ge(s_lgp, NT)
            for j in range(2):
                for half in range(2):
                    k = slice(KT // 2 * half, KT // 2 * (half + 1))
                    pool.wait_ge(s_eh[j], half + 1)
                    pool.tensor_tensor(e_lo[j][:, k, :], e_raw[j][:, k, :], e_hi[j][:, k, :].bitcast(F32),
                                       ALU.subtract).then_inc(s_el[j], 1)

            def gather(b):
                i = b % 2
                pool.wait_ge(s_ix, b + 1)
                if b >= 2:
                    pool.wait_ge(s_xt, b - 1)
                pool.indirect_dma_start(out=xg[i][0:CAP, :], out_offset=None, in_=n_scr,
                                        in_offset=bass.IndirectOffsetOnAxis(ap=gidx[i][:, 0:1].bitcast(U32), axis=0)
                                        ).then_inc(s_gl[i], 16)

            def block_io(b):
                gather(b + 3)
                pool.wait_ge(s_ya, b + 1)
                pool.wait_ge(s_yd, b + 1)
                pool.wait_ge(s_sx2, b + 1)
                pool.indirect_dma_start(out=y_all,
                                        out_offset=bass.IndirectOffsetOnAxis(ap=sidx[b % 2][:, 0:1].bitcast(U32), axis=0),
                                        in_=yo[b % 2][:, :], in_offset=None, compute_op=ALU.add,
                                        bounds_check=NY - 1).then_inc(s_sc, 16)
                pool.wait_ge(s_gl[(b + 3) % 2], 16 * ((b + 3) // 2 + 1))
                pool.wait_ge(s_sc, 16 * (b + 1))

            for i in range(2):
                pool.wait_ge(s_nst[i], 16 * len(range(i, NT, 2)))
            pool.wait_ge(s_yst, 16 * (NT + 2))
            for b in range(3):
                gather(b)
            for b in range(NE):
                block_io(b)
            pool.wait_ge(s_tab, 1)
            n_over = pool.value_load(ovmi[0:1, OVB:OVB + 1], min_val=0, max_val=OVB)
            with pool.If(n_over > 0):
                for o in range(OVB):
                    with pool.If(n_over > o):
                        block_io(NE + o)

        @block.scalar
        def _(act):
            chain = Chain(act, s_act)

            def square(t):
                r = ROWS[t]
                act.wait_ge(s_xld[t % 3], 32 * (t // 3 + 1))
                if t >= 1:
                    act.wait_ge(s_ssq, t)
                if t >= 2:
                    act.wait_ge(s_rms, t - 1)
                act.activation(junk[0:r, :], xt[t % 3][0:r, :], ACT.Square,
                               accum_out=ss[0:r, t % 2:t % 2 + 1]).then_inc(s_ssq, 1)

            def norm_stages(i):
                if 1 <= i <= NT:
                    t, r = i - 1, ROWS[i - 1]
                    act.wait_ge(s_xT, t + 1)
                    act.activation(xh[:, :, row0(t):row0(t) + r], xT_ps[:, :, 0:r], ACT.Copy).then_inc(s_xh, 1)
                if i + 1 < NT:
                    square(i + 1)
                if i < NT:
                    act.wait_ge(s_ms, i + 1)
                    if i >= 2:
                        act.wait_ge(s_xs, i - 1)
                    act.activation(rs[0:ROWS[i], i % 2:i % 2 + 1], ss[0:ROWS[i], i % 2:i % 2 + 1],
                                   ACT.Sqrt).then_inc(s_rms, 1)

            def split_hi(n):
                act.wait_ge(s_wld[n % 2], 16 * (n // 2 + 1))
                if n >= 2:
                    act.wait_ge(s_pr, ends[n - 2])
                act.activation(w_hi[n % 2][:, :, :], w_raw[n % 2][:, :, :], ACT.Copy).then_inc(s_whi, 1)

            square(0)
            norm_stages(0)
            split_hi(0)
            norm_stages(1)
            for s in range(NQK + 4):
                if s < NS and steps[s][0:2] == ("k", 0):
                    norm_stages(steps[s][2] + 2)
                if s == 1:
                    split_hi(1)
                if s < NQK:
                    r = ROWS[steps[s][2]]
                    act.wait_ge(s_pr, s + 1)
                    if s >= 2:
                        act.wait_ge(s_hms, s - 1)
                    act.activation(sq[s % 2][0:r, :], proj_ps(s)[0:r, :], ACT.Square).then_inc(s_sq, 1)
                if s == ends[0]:
                    split_hi(2)
                if 2 * NT < s < NQK and s % NT == 3:
                    split_hi(s // NT + 1)
                if 1 <= s <= NQK:
                    r = ROWS[steps[s - 1][2]]
                    act.wait_ge(s_hms, s)
                    act.activation(hr[0:r, (s - 1) % 2, :], hs[0:r, (s - 1) % 2, :], ACT.Sqrt).then_inc(s_hrms, 1)
                if 4 <= s < NQK + 4:
                    kind, half, t = steps[s - 4]
                    r = ROWS[t]
                    act.wait_ge(s_kt, s - 3)
                    dst = qT if kind == "q" else kT
                    act.activation(dst[:, 2 * half:2 * half + 2, row0(t):row0(t) + r],
                                   head_ps(s - 4)[:, :, 0:r], ACT.Copy).then_inc(s_ke, 1)
            split_hi(5)

            act.wait_ge(s_pad, 1)
            act.wait_ge(s_ht, 1)
            act.activation(es[:, :, :, 1:16],
                           bank[:, 6, 0:NG * DB * HIST].rearrange("p (g b i) -> p g b i", g=NG, b=DB),
                           ACT.Copy).then_inc(s_uc, 1)
            for i, (g, piece) in enumerate(usteps):
                lo, n = UPIECES[piece]
                if i == NUS // 2 + 1:
                    split_hi(6)
                act.wait_ge(s_pr, NQK + i + 1)
                ps = wide_ps(NQK + i)
                if piece < 2:
                    act.activation(u_ext[:, g, 16 + lo:16 + lo + n], ps[:, 0:n], ACT.Copy).then_inc(s_uc, 1)
                else:
                    act.activation(u_ext[:, g, 16 + lo:16 + TP], ps[:, 0:TP - lo], ACT.Copy).then_inc(s_uc, 1)
                    act.activation(es[:, g, :, 16:20], ps[:, TP - lo:T - lo].rearrange("p (b j) -> p b j", j=DS),
                                   ACT.Copy).then_inc(s_uc, 1)
                    act.activation(us_cols[:, g, :], ps[:, TP - lo:T - lo], ACT.Copy).then_inc(s_uc, 1)
            act.wait_ge(s_ut, 1)
            act.activation(up_rows[:, :], bank[0:TAILP, 6, :], ACT.Copy).then_inc(s_ur, 1)
            act.activation(us_rows[:, :], bank[0:TS, 7, :], ACT.Copy).then_inc(s_ur, 1)
            split_hi(7)
            act.wait_ge(s_ssq, NT)
            for s in range(NQK, NS):
                _, half, t = steps[s]
                r = ROWS[t]
                act.wait_ge(s_pr, turn(s) + 1)
                act.activation(vv[0:r, t, half * CG:half * CG + CG], proj_ps(s)[0:r, :], ACT.Copy).then_inc(s_v, 1)
            def pooling_hi():
                act.wait_ge(s_cst2, 16 * NCONST)
                for i, (g, piece) in enumerate(usteps):
                    lo, n = PIECES[piece]
                    act.wait_ge(s_pm, i + 1)
                    act.activation(xh[:, g, lo:lo + n], pool_ps(i)[:, 0:n], ACT.Copy,
                                   scale=pscale[:, g:g + 1]).then_inc(s_ph, 1)

            def sigmoid(u):
                kind, w = units[u][0], width(u)
                act.wait_ge(s_z, u + 1)
                if u >= 2:
                    act.wait_ge(s_am, u - 1)
                elif u == 0:
                    act.wait_ge(s_pr, NS + NUS)
                    act.wait_ge(s_wlo, 8)
                    act.wait_ge(s_mask, 2)
                rows = height(u)
                bias = (bias_bc[:, units[u][2]:units[u][2] + 1] if kind == "full" else
                        bias_tail[:, units[u][1]:units[u][1] + 1] if kind == "tail" else bias_smp[0:rows, 0:1])
                act.activation(sg[u % 2][0:rows, NK - w:NK], z_ps(u)[0:rows, 0:w], ACT.Sigmoid, bias=bias,
                               scale=HD ** -0.5).then_inc(s_sg, 1)

            def copy_banks(u):
                rows = height(u)
                for j, group in enumerate(groups(u)):
                    n = first_group(u) + j
                    act.wait_ge(s_t, n + 1)
                    if j == 0 and u >= 2:
                        act.wait_ge(s_av, summed_at(u - 2))
                    full = [c for c in group if c[1] == P]
                    if full:
                        last = act.activation(aT[u % 2][:, full[0][0]:full[-1][0] + 1, 0:rows],
                                              t_ps(n)[:, 0:len(full), 0:rows], ACT.Copy)
                    if len(full) < len(group):
                        c, keys = group[-1]
                        last = act.activation(aT[u % 2][0:keys, c, 0:rows], t_ps(n)[0:keys, len(full), 0:rows], ACT.Copy)
                    last.then_inc(s_te, 1)

            def copy_o(u):
                i, ends = out_of(u)
                if ends:
                    act.wait_ge(s_av, summed_at(u))
                    if i >= 1:
                        act.wait_ge(s_oT, i)
                    if units[u][0] == "tail":
                        for h in range(H):
                            cols = slice(HD * h, HD * (h + 1))
                            last = act.activation(o_sb[0:TAILP, cols], o_ps(i)[32 * (h % 4):32 * (h % 4) + TAILP, cols],
                                                  ACT.Copy)
                    else:
                        last = act.activation(o_sb[0:out_rows(i), :], o_ps(i)[0:out_rows(i), :], ACT.Copy)
                    last.then_inc(s_os, 1)

            def hi_o(u):
                i, ends = out_of(u)
                t = tile_of(i)
                if ends and t is not None:
                    r = out_rows(i)
                    act.wait_ge(s_oT, i + 1)
                    act.activation(xh[:, HP:KT, row0(t):row0(t) + r],
                                   o_ps(i).rearrange("p (c n) -> p c n", n=P)[:, :, 0:r], ACT.Copy).then_inc(s_oh, 1)
                if t is None:
                    act.wait_ge(s_oT, i + 1)
                    for half in range(2):
                        rows = slice(64 * half, 64 * half + 64)
                        last = act.activation(smp_out(xh, outs[i][1], rows), smp_in(i, half, rows), ACT.Copy)
                        if half == 0:
                            last.then_inc(s_act, 1)
                    last.then_inc(s_oh, 1)

            def copy_keys(g):
                for b in range(SQ * g, SQ * g + SQ):
                    for hp in range(HP):
                        n = key_group(b, hp)
                        act.wait_ge(s_t, n + 1)
                        if b >= 1:
                            act.wait_ge(s_kTs, HP * (b - 1) + hp + 1)
                        last = act.activation(kTs[:, hp, :], bank[:, 4 + n % 2, :], ACT.Copy)
                        last.then_inc(s_te, 1)

            def split_out_hi(n):
                act.wait_ge(s_wld[n % 2], 16 * (4 + n // 2 + 1))
                if n < 2:
                    act.wait_ge(s_av, summed_at(NU - 2 + n))
                else:
                    act.wait_ge(s_wo, NT * (n - 1))
                act.activation(w_hi[n % 2][:, :, :], w_raw[n % 2][:, :, :], ACT.Copy).then_inc(s_whi, 1)

            assert NU % 2 == 0
            for i in range(NU + 6):
                if i == 2:
                    pooling_hi()
                if i < NU:
                    if units[i][0] == "smp":
                        copy_keys(units[i][1])
                    sigmoid(i)
                if 2 <= i < NU + 2:
                    copy_banks(i - 2)
                if i == NU + 2:
                    split_out_hi(0)
                if 4 <= i < NU + 4:
                    copy_o(i - 4)
                if 6 <= i:
                    hi_o(i - 6)

            for n in range(1, D // CG):
                split_out_hi(n)

            for t in range(NT + 2):
                if 1 <= t <= NT:
                    act.wait_ge(s_ms2, t)
                    c = slice((t - 1) % 2, (t - 1) % 2 + 1)
                    act.activation(rs[0:ROWS[t - 1], c], ss[0:ROWS[t - 1], c], ACT.Sqrt).then_inc(s_rms2, 1)
                if t < NT:
                    r = ROWS[t]
                    act.wait_ge(s_xm, tile_done(t))
                    if t >= 1:
                        act.wait_ge(s_ssq2, t)
                    act.activation(junk2[0:r, :], xmid[0:r, t, :], ACT.Square,
                                   accum_out=ss[0:r, t % 2:t % 2 + 1]).then_inc(s_ssq2, 1)
                if t >= 2:
                    i, r = t - 2, ROWS[t - 2]
                    act.wait_ge(s_n2T, i + 1)
                    if i >= 2:
                        act.wait_ge(s_lgp, i - 1)
                    act.activation(nT[i % 2][:, :, 0:r], norm_ps(i)[:, :, 0:r], ACT.Copy).then_inc(s_n2c, 1)
            act.wait_ge(s_gx, 1)
            act.activation(gex[:, :, :], gex[:, :, :], ACT.Exp).then_inc(s_ge, 1)
            act.wait_ge(s_gx, 2)
            act.activation(gt[:, 1, :], gt[:, 1, :], ACT.Exp).then_inc(s_ge, 1)

            def parts(j):
                return ((s_gp, 1), (s_up, 1), (s_dp, 2))[j]

            def weight_hi(j, b, half):
                act.wait_ge(s_wl[j][half], 16 * b + 16)
                if half == 0:
                    done, per = parts(j)
                    since(act, done, per * b)
                h = e_raw[j].shape[1] // 2
                act.activation(e_hi[j][:, h * half:h * half + h, :], e_raw[j][:, h * half:h * half + h, :],
                               ACT.Copy).then_inc(s_eh[j], 1)

            def weight_whole(j, b):
                for half in range(2):
                    weight_hi(j, b, half)

            def block_hi(b, i):
                act.wait_ge(s_xt, b + 1)
                since(act, s_up, b - 1)
                act.activation(xeh[i][:, :, :], xT_ps[:, :, 0:CAP], ACT.Copy).then_inc(s_xe, 1)

            def silu(b, i):
                act.wait_ge(s_gp, b + 1)
                since(act, s_h, b)
                act.activation(sgl[:, :], gate_ps(i), ACT.Silu).then_inc(s_si, 1)

            def hidden_hi(b):
                act.wait_ge(s_hT, b + 1)
                since(act, s_dp, 2 * b)
                act.activation(hT_hi[:, :, :], hT_ps, ACT.Copy).then_inc(s_hh, 1)

            def left_half(b, i):
                act.wait_ge(s_dp, 2 * b + 1)
                act.wait_ge(s_sx, b + 1)
                act.activation(yo[i][:, 0:512], bank[0:CAP, 6, :], ACT.Copy, scale=gcol[i][:, 0:1]).then_inc(s_ya, 1)

            def first_act():
                weight_whole(0, 0)
                weight_whole(1, 0)
                act.wait_ge(s_yst, 16 * (NT + 2))
                weight_whole(2, 0)
                for b in range(2):
                    block_hi(b, b)
                silu(0, 0)
                weight_whole(0, 1)

            def block_act(i, b):
                weight_hi(1, b + 1, 0)
                hidden_hi(b)
                weight_hi(1, b + 1, 1)
                silu(b + 1, 1 - i)
                if not (type(b) is int and b == NE - 2):
                    weight_whole(0, b + 2)
                left_half(b, i)
                block_hi(b + 2, i)
                weight_whole(2, b + 1)

            def last_act(b):
                if b == NE - 2:
                    block_act(0, b)
                else:
                    hidden_hi(b)
                    left_half(b, 1)
                    block_hi(b + 2, 1)

            def further_act(i, b):
                for j in range(3):
                    weight_whole(j, b)
                silu(b, i)
                hidden_hi(b)
                left_half(b, i)
                block_hi(b + 2, i)

            blocks(act, first_act, block_act, last_act, further_act)

        @block.vector
        def _(dve):
            chain = Chain(dve, s_dve)

            def mean_square(t):
                c = slice(t % 2, t % 2 + 1)
                dve.wait_ge(s_ssq, t + 1)
                dve.tensor_scalar(ss[0:ROWS[t], c], ss[0:ROWS[t], c], 1.0 / D, EPS, ALU.mult, ALU.add).then_inc(s_ms, 1)

            def norm_stages(i):
                if 1 <= i <= NT:
                    t, r = i - 1, ROWS[i - 1]
                    dve.wait_ge(s_xh, t + 1)
                    dve.tensor_tensor(xl[:, :, row0(t):row0(t) + r], xT_ps[:, :, 0:r],
                                      xh[:, :, row0(t):row0(t) + r].bitcast(F32), ALU.subtract).then_inc(s_xl, 1)
                if i < NT:
                    r, c = ROWS[i], slice(i % 2, i % 2 + 1)
                    dve.wait_ge(s_rms, i + 1)
                    chain.link(dve.reciprocal(rs[0:r, c], rs[0:r, c]))
                    dve.scalar_tensor_tensor(out=xt[i % 3][0:r, :], in0=xt[i % 3][0:r, :], scalar=rs[0:r, c],
                                             in1=gmix[0:r, :], op0=ALU.mult, op1=ALU.mult).then_inc(s_xs, 1)
                if i + 1 < NT:
                    mean_square(i + 1)

            def split_lo(n):
                dve.wait_ge(s_whi, n + 1)
                if n >= 2:
                    dve.wait_ge(s_pr, ends[n - 2])
                dve.tensor_tensor(w_lo[n % 2][:, :, :], w_raw[n % 2][:, :, :], w_hi[n % 2][:, :, :].bitcast(F32),
                                  ALU.subtract).then_inc(s_wlo, 1)

            def norm_heads(s):
                kind, half, t = steps[s]
                r = ROWS[t]
                dve.wait_ge(s_hrms, s + 1)
                chain.link(dve.reciprocal(hr[0:r, s % 2, :], hr[0:r, s % 2, :]))
                if s >= NKN:
                    dve.wait_ge(s_kt, s - NKN + 1)
                    if steps[s - NKN][0] == "k":
                        dve.wait_ge(s_kst[s % NKN], 16 * (s // NKN))
                out = kn[s % NKN][0:r, :].rearrange("p (h d) -> p h d", d=HD)
                inv = hr[0:r, s % 2, :].rearrange("p (h a) -> p h a", a=1).to_broadcast([r, 4, HD])
                chain.link(dve.tensor_tensor(out, proj_ps(s)[0:r, :].rearrange("p (h d) -> p h d", d=HD), inv, ALU.mult))
                g = (gq_bc if kind == "q" else gk_bc)[0:r, :].rearrange("p (a d) -> p a d", a=1)
                dve.tensor_tensor(out, out, g.to_broadcast([r, 4, HD]), ALU.mult).then_inc(s_kn, 1)

            dve.wait_ge(s_const, 16)
            mean_square(0)
            norm_stages(0)
            split_lo(0)
            norm_stages(1)
            for s in range(NQK + 1):
                if s < NS and steps[s][0:2] == ("k", 0):
                    norm_stages(steps[s][2] + 2)
                if s == 1:
                    split_lo(1)
                    dve.wait_ge(s_gain, 32)
                if s < NQK:
                    r = ROWS[steps[s][2]]
                    dve.wait_ge(s_sq, s + 1)
                    chain.link(dve.reduce_sum(hs[0:r, s % 2, :], sq[s % 2][0:r, :].rearrange("p (h d) -> p h d", d=HD),
                                              axis=AXX))
                    dve.tensor_scalar(hs[0:r, s % 2, :], hs[0:r, s % 2, :], 1.0 / HD, EPS,
                                      ALU.mult, ALU.add).then_inc(s_hms, 1)
                if s == ends[0] + 1:
                    split_lo(2)
                if 2 * NT < s < NQK and s % NT == 4:
                    split_lo(s // NT + 1)
                if s >= 1:
                    norm_heads(s - 1)
            split_lo(5)
            dve.wait_ge(s_mask, 1)
            dve.wait_ge(s_cst2, 16 * NCONST)
            chain.done(dve.tensor_scalar(pint[:, 1:2], pint[:, 0:1], 3, None, ALU.bitwise_and))
            chain.done(dve.tensor_scalar(pint[:, 2:3], pint[:, 0:1], 5, None, ALU.logical_shift_right))
            chain.done(dve.tensor_scalar(pint[:, 3:4], pint[:, 0:1], 2, 7, ALU.logical_shift_right, ALU.bitwise_and))
            chain.settle()
            chain.link(dve.tensor_copy(pflt[:, 0:3], pint[:, 1:4]))
            for g in range(NSG):
                chain.link(dve.tensor_scalar(pflt[:, 3:4], pflt[:, 1:2], float(DS), float(TAILP + DS * SQ * g), ALU.mult, ALU.add))
                chain.link(dve.tensor_tensor(pflt[:, 4:5], pflt[:, 3:4], pflt[:, 0:1], ALU.add))
                chain.link(dve.tensor_scalar(smp_mask[:, g, :], col48[:, :], pflt[:, 3:4], None, ALU.is_ge))
                chain.link(dve.scalar_tensor_tensor(out=smp_mask[:, g, :], in0=col48[:, :], scalar=pflt[:, 4:5],
                                                    in1=smp_mask[:, g, :], op0=ALU.is_lt, op1=ALU.mult))
            chain.link(dve.memset(bias_smp[:, :], 0.0))
            for h in range(H):
                chain.link(dve.tensor_scalar(pflt[:, 5:6], pflt[:, 2:3], float(h), None, ALU.is_equal))
                chain.link(dve.scalar_tensor_tensor(out=bias_smp[:, :], in0=pflt[:, 5:6], scalar=bias_bc[:, h:h + 1],
                                                    in1=bias_smp[:, :], op0=ALU.mult, op1=ALU.add))
            for h in range(H):
                rows = slice(32 * (h % 4), 32 * (h % 4) + 32)
                chain.done(dve.tensor_copy(bias_tail[rows, h // 4:h // 4 + 1], bias_bc[rows, h:h + 1]))
            dve.reciprocal(rcnt[:, :], rcnt[:, :]).then_inc(s_mask, 1)
            dve.wait_ge(s_mask, 2)
            split_lo(6)

            def diff(g):
                w = WINDOWS[g]
                if g == 0:
                    dve.wait_ge(s_uc, u_copies(NUS - 1))
                    dve.wait_ge(s_ut, 1)
                src, n = u_ext[:, g, :], 1
                srcs = es[:, g, :, :]
                k = 0
                while n < w:
                    dst, dsts = wsum[k % 2], wsmall[k % 2]
                    chain.done(dve.tensor_tensor(dst[:, 2 * n - 1:16 + TP], src[:, 2 * n - 1:16 + TP],
                                                 src[:, n - 1:16 + TP - n], ALU.add))
                    chain.done(dve.tensor_tensor(dsts[:, :, 2 * n - 1 + 1:20], srcs[:, :, 2 * n - 1 + 1:20],
                                                 srcs[:, :, n:20 - n], ALU.add))
                    chain.settle()
                    src, srcs, n, k = dst, dsts, 2 * n, k + 1
                u, lo = u_ext[:, g, 16:16 + TP], PIECES[2][0]
                sums = src[:, 16:16 + TP]
                chain.done(dve.scalar_tensor_tensor(out=d_tail[:, g, 0:TAILP], in0=sums[:, lo:TP], scalar=1.0 / w,
                                                    in1=u[:, lo:TP], op0=ALU.mult, op1=ALU.subtract))
                chain.done(dve.scalar_tensor_tensor(out=d_tail[:, g, TAILP:TAILP + TS].rearrange("p (b j) -> p b j", j=DS),
                                                    in0=srcs[:, :, 16:20], scalar=1.0 / w, in1=es[:, g, :, 16:20],
                                                    op0=ALU.mult, op1=ALU.subtract))
                chain.done(dve.scalar_tensor_tensor(out=u[:, w - 1:lo], in0=sums[:, w - 1:lo], scalar=1.0 / w,
                                                    in1=u[:, w - 1:lo], op0=ALU.mult, op1=ALU.subtract))
                chain.link(dve.tensor_tensor(sums[:, 0:w - 1], sums[:, 0:w - 1], rcnt[:, 0:w - 1], ALU.mult))
                dve.tensor_tensor(u[:, 0:w - 1], sums[:, 0:w - 1], u[:, 0:w - 1], ALU.subtract).then_inc(s_d, 1)
                dve.wait_ge(s_d, g + 1)

            def pool_lo(g):
                for piece in range(3):
                    i = 3 * g + piece
                    lo, n = PIECES[piece]
                    dve.wait_ge(s_ph, i + 1)
                    dve.scalar_tensor_tensor(out=xl[:, g, lo:lo + n], in0=pool_ps(i)[:, 0:n],
                                             scalar=pscale[:, g:g + 1], in1=xh[:, g, lo:lo + n].bitcast(F32),
                                             op0=ALU.mult, op1=ALU.subtract).then_inc(s_pl, 1)

            for g in range(NG):
                diff(g)
                if g == 1:
                    split_lo(7)

            def spread_queries():
                dve.wait_ge(s_pad, 2)
                dve.wait_ge(s_ke, NQK)
                for h in range(H):
                    rows = slice(64 * (h % 2), 64 * (h % 2) + 64)
                    last = dve.tensor_copy(qz[rows, h // 2, :, DS * h:DS * h + DS],
                                           qT[rows, h // 2, TP:T].rearrange("p (b j) -> p b j", j=DS))
                    if h < H - 1:
                        chain.done(last)
                last.then_inc(s_qz, 1)

            def weigh(u):
                kind, w = units[u][0], width(u)
                lo = NK - w
                row, prod = sg[u % 2][0:height(u), :], pb[u % 2][0:height(u), :]
                dve.wait_ge(s_sg, u + 1)
                if kind == "full":
                    chain.link(dve.tensor_tensor(row[:, NK - P:NK], row[:, NK - P:NK], diag_mask[:, :], ALU.mult))
                elif kind == "tail":
                    chain.link(dve.tensor_tensor(row[:, NK - TAILP:NK], row[:, NK - TAILP:NK], tail_mask[:, :], ALU.mult))
                else:
                    n = ROWS[-1]
                    chain.link(dve.tensor_tensor(row[:, NK - n:NK], row[:, NK - n:NK], smp_mask[0:height(u), units[u][1], :],
                                                 ALU.mult))
                chain.link(dve.tensor_scalar(prod[:, lo:NK], row[:, lo:NK], -1.0, 1.0, ALU.mult, ALU.add))
                back = prod[:, lo:NK][:, ::-1]
                chain.link(dve.tensor_tensor_scan(back, back, back, 1.0, ALU.mult, ALU.bypass))
                if u >= 2:
                    dve.wait_ge(s_t, first_group(u - 2) + len(groups(u - 2)))
                dve.tensor_tensor(am[u % 2][0:height(u), lo:NK], row[:, lo:NK], prod[:, lo + 1:NK + 1], ALU.mult).then_inc(s_am, 1)
                dve.wait_ge(s_am, u + 1)

            def lo_o(u):
                i, ends = out_of(u)
                t = tile_of(i)
                if ends and t is not None:
                    r = P if t < LAST else TAILP
                    dve.wait_ge(s_oh, i + 1)
                    dve.tensor_tensor(xl[:, HP:KT, row0(t):row0(t) + r],
                                      o_ps(i).rearrange("p (c n) -> p c n", n=P)[:, :, 0:r],
                                      xh[:, HP:KT, row0(t):row0(t) + r].bitcast(F32), ALU.subtract).then_inc(s_ol, 1)
                if t is None:
                    dve.wait_ge(s_oh, i + 1)
                    dve.wait_ge(s_act, outs[i][1] + 1)
                    for half in range(2):
                        rows = slice(64 * half, 64 * half + 64)
                        last = dve.tensor_tensor(smp_out(xl, outs[i][1], rows), smp_in(i, half, rows),
                                                 smp_out(xh, outs[i][1], rows).bitcast(F32), ALU.subtract)
                        if half == 0:
                            chain.done(last)
                    last.then_inc(s_ol, 1)

            dve.wait_ge(s_pr, NS + NUS)
            for i in range(2):
                chain.link(dve.memset(pb[i][:, NK:NK + 1], 1.0))
            def split_out_lo(n):
                dve.wait_ge(s_whi, 8 + n + 1)
                if n >= 2:
                    dve.wait_ge(s_wo, NT * (n - 1))
                dve.tensor_tensor(w_lo[n % 2][:, :, :], w_raw[n % 2][:, :, :], w_hi[n % 2][:, :, :].bitcast(F32),
                                  ALU.subtract).then_inc(s_wlo, 1)

            for i in range(NU + 6):
                if i == 2:
                    for g in range(NG):
                        pool_lo(g)
                if i == H:
                    spread_queries()
                if i < NU:
                    weigh(i)
                if i == NU + 2:
                    split_out_lo(0)
                if 6 <= i:
                    lo_o(i - 6)

            def norm_scale(t):
                r = ROWS[t]
                c = slice(t % 2, t % 2 + 1)
                dve.wait_ge(s_ssq2, t + 1)
                dve.tensor_scalar(ss[0:r, c], ss[0:r, c], 1.0 / D, EPS, ALU.mult, ALU.add).then_inc(s_ms2, 1)
                dve.wait_ge(s_rms2, t + 1)
                chain.link(dve.reciprocal(rs[0:r, c], rs[0:r, c]))
                if t >= 2:
                    dve.wait_ge(s_n2T, t - 1)
                    dve.wait_ge(s_nst[t % 2], 16 * (t // 2))
                dve.scalar_tensor_tensor(out=xg[t % 2][0:r, :], in0=xmid[0:r, t, :], scalar=rs[0:r, c],
                                         in1=gffn[0:r, :], op0=ALU.mult, op1=ALU.mult).then_inc(s_n2, 1)

            def copy_logits(t):
                dve.wait_ge(s_lgp, t + 1)
                dve.tensor_copy(lg[0:ROWS[t], t, :], logit_ps(t)[0:ROWS[t], :]).then_inc(s_lg, 1)

            dve.wait_ge(s_wr, 48)
            dve.wait_ge(s_zr, 1)
            for s, (n, t) in enumerate(wsteps):
                if s in (2, NT + 2, 2 * NT):
                    split_out_lo({2: 1, NT + 2: 2, 2 * NT: 3}[s])
                r = ROWS[t]
                if n == 0:
                    dve.wait_ge(s_xr[t], 32)
                dve.wait_ge(s_wo, s + 1)
                dst = xmid[0:r, t, n * CG:n * CG + CG]
                dve.tensor_tensor(dst, out_ps(s)[0:r, :], dst, ALU.add).then_inc(s_xm, 1)
                if n == 3 and t >= 1:
                    norm_scale(t - 1)
                if n == 3 and t >= 4:
                    copy_logits(t - 4)
            norm_scale(LAST)
            for t in range(NT - 4, NT):
                copy_logits(t)
            dve.wait_ge(s_tbl, 1)
            dve.wait_ge(s_lg, NT)

            def wide(ap, n):
                return ap.rearrange("p (a x) -> p a x", x=1).to_broadcast([P, ap.shape[1], n])

            def over(ap, n):
                return ap.rearrange("p (x a) -> p x a", x=1).to_broadcast([P, n, ap.shape[1]])

            def first_best(out, best, values, steps_, n):
                chain.link(dve.reduce_max(best, values, axis=AXX))
                chain.link(dve.tensor_tensor(out, values, wide(best, n), ALU.is_equal))
                chain.link(dve.tensor_tensor(out, out, over(steps_[:, :], NT), ALU.mult))
                chain.link(dve.tensor_reduce(rsum[:, :], out, axis=AXX, op=ALU.min))
                chain.link(dve.tensor_tensor(out, over(steps_[:, :], NT), wide(rsum[:, :], n), ALU.is_equal))

            def weight_lo(j, b, half):
                h = e_raw[j].shape[1] // 2
                k = slice(h * half, h * half + h)
                dve.wait_ge(s_eh[j], 2 * b + half + 1)
                dve.tensor_tensor(e_lo[j][:, k, :], e_raw[j][:, k, :], e_hi[j][:, k, :].bitcast(F32),
                                  ALU.subtract).then_inc(s_el[j], 1)

            def weight_whole(j, b):
                for half in range(2):
                    weight_lo(j, b, half)

            first_best(goh[:, :, :], gmx[:, :], lg[:, :, 0:NGRP], io4, NGRP)
            dve.tensor_tensor(gex[:, :, :], lg[:, :, 0:NGRP], wide(gmx[:, :], NGRP), ALU.subtract).then_inc(s_gx, 1)
            for g in range(NGRP):
                part = lg[:, :, NGRP + EPG * g:NGRP + EPG * (g + 1)]
                chain.link(dve.tensor_tensor((le if g == 0 else tmp8)[:, :, :], part, wide(goh[:, :, g], EPG), ALU.mult))
                if g:
                    chain.link(dve.tensor_tensor(le[:, :, :], le[:, :, :], tmp8[:, :, :], ALU.add))
            first_best(oh[:, 0, :, :], mx[:, 0, :], le[:, :, :], io8, EPG)
            chain.link(dve.scalar_tensor_tensor(out=le[:, :, :], in0=oh[:, 0, :, :], scalar=-3.0e38, in1=le[:, :, :],
                                                op0=ALU.mult, op1=ALU.add))
            first_best(oh[:, 1, :, :], mx[:, 1, :], le[:, :, :], io8, EPG)
            dve.tensor_tensor(gt[:, 1, :], mx[:, 1, :], mx[:, 0, :], ALU.subtract).then_inc(s_gx, 1)
            chain.link(dve.tensor_scalar(valid[:, :], tok[:, :], 0.0, None, ALU.is_lt))
            chain.link(dve.tensor_tensor(goh[:, :, :], goh[:, :, :], wide(valid[:, :], NGRP), ALU.mult))
            for k in range(2):
                for g in range(NGRP):
                    chain.done(dve.tensor_tensor(ek[:, k, :, EPG * g:EPG * (g + 1)], oh[:, k, :, :], wide(goh[:, :, g], EPG),
                                                 ALU.mult))
            chain.settle()
            dve.tensor_tensor(eb[:, :, :], ek[:, 0, :, :], ek[:, 1, :, :], ALU.add).then_inc(s_eb, 1)
            dve.wait_ge(s_ge, 2)
            chain.link(dve.reduce_sum(gw[:, :], gex[:, :, :], axis=AXX))
            chain.link(dve.reciprocal(gw[:, :], gw[:, :]))
            chain.link(dve.tensor_scalar(gt[:, 0, :], gt[:, 1, :], 1.0, None, ALU.add))
            chain.link(dve.reciprocal(gt[:, 0, :], gt[:, 0, :]))
            chain.link(dve.tensor_tensor(gt[:, 0, :], gt[:, 0, :], gw[:, :], ALU.mult))
            chain.link(dve.tensor_tensor(gt[:, 1, :], gt[:, 1, :], gt[:, 0, :], ALU.mult))
            dve.wait_ge(s_rkp, 1)
            totals = bank[:, 7, 0:NT * NE].rearrange("p (t e) -> p t e", t=NT)
            chain.link(dve.memset(cum[:, 0, :], 0.0))
            for t in range(1, NT):
                chain.link(dve.tensor_tensor(cum[:, t, :], totals[:, t - 1, :], cum[:, t - 1, :], ALU.add))
            chain.link(dve.tensor_tensor(cnt[:, :], totals[:, LAST, :], cum[:, LAST, :], ALU.add))
            chain.link(dve.tensor_tensor(cum[:, :, :], bank[:, 6, 0:NT * NE].rearrange("p (t e) -> p t e", t=NT),
                                         cum[:, :, :], ALU.add))
            chain.link(dve.tensor_tensor(cmp_[:, :, :], wide(cnt[:, :], OVMAX), over(jt[:, :], NE), ALU.is_gt))
            chain.link(dve.reduce_sum(nov[:, :], cmp_[:, :, :], axis=AXX))
            chain.link(dve.tensor_tensor_scan(ovend[:, :], nov[:, :], nov[:, :], 0.0, ALU.add, ALU.bypass))
            chain.link(dve.tensor_tensor(ovst[:, :], ovend[:, :], nov[:, :], ALU.subtract))

            assert 2 * T < RANKS and NE == 32 and (OVB + 1) * NE * RANKS < 2 ** 24
            chain.link(dve.scalar_tensor_tensor(out=kcol[:, :], in0=ovst[:, :], scalar=float(NE), in1=io128[:, 0:NE],
                                                op0=ALU.mult, op1=ALU.add))
            chain.link(dve.tensor_scalar(kcol[:, :], kcol[:, :], float(RANKS), None, ALU.mult))
            chain.link(dve.tensor_tensor(cum[:, :, :], cum[:, :, :], over(kcol[:, :], NT), ALU.add))
            both = cum[:, :, :].rearrange("p (x t) e -> p x t e", x=1).to_broadcast([P, 2, NT, NE])
            chain.link(dve.tensor_tensor(ek[:, :, :, :], ek[:, :, :, :], both, ALU.mult))
            chain.link(dve.reduce_sum(key[:, :, :], ek[:, :, :, :], axis=AXX))
            chain.link(dve.tensor_copy(keyi[:, :, :], key[:, :, :]))
            chain.done(dve.tensor_scalar(fieldi[:, 0, :, :], keyi[:, :, :], RANKS - 1, None, ALU.bitwise_and))
            chain.done(dve.tensor_scalar(fieldi[:, 1, :, :], keyi[:, :, :], RANK_BITS, NE - 1, ALU.logical_shift_right,
                                         ALU.bitwise_and))
            chain.done(dve.tensor_scalar(fieldi[:, 2, :, :], keyi[:, :, :], RANK_BITS + 5, None, ALU.logical_shift_right))
            chain.settle()
            chain.link(dve.tensor_copy(field[:, :, :, :], fieldi[:, :, :, :]))
            rk_, eid_, ovs_ = [field[:, i, :, :].rearrange("p k t -> p (k t)") for i in range(3)]
            bk_, rw_, cl_ = [x[:, :, :].rearrange("p k t -> p (k t)") for x in (bk, rw, cl)]
            part = cmp_[:, 0:2 * NT, :]
            chain.link(dve.tensor_tensor(part, wide(rk_, OVMAX), over(jt[:, :], 2 * NT), ALU.is_ge))
            chain.link(dve.reduce_sum(bk_, part, axis=AXX))
            chain.done(dve.scalar_tensor_tensor(out=rw_, in0=bk_, scalar=-float(CAP), in1=rk_, op0=ALU.mult, op1=ALU.add))
            chain.done(dve.tensor_tensor(cl_, ovs_, bk_, ALU.add))
            chain.settle()
            valid2 = valid[:, :].rearrange("p (x t) -> p x t", x=1).to_broadcast([P, 2, NT])
            chain.done(dve.scalar_tensor_tensor(out=rw[:, :, :], in0=rw[:, :, :], scalar=1.0, in1=valid2,
                                                op0=ALU.add, op1=ALU.mult))
            chain.done(dve.scalar_tensor_tensor(out=cl_, in0=cl_, scalar=float(NE - 1), in1=eid_, op0=ALU.add,
                                                op1=ALU.subtract))
            chain.done(dve.tensor_scalar(ovs_, bk_, 0.0, None, ALU.is_gt))
            chain.settle()
            chain.link(dve.tensor_tensor(cl_, cl_, ovs_, ALU.mult))
            chain.link(dve.tensor_tensor(cl_, cl_, eid_, ALU.add))
            for k in range(2):
                chain.done(dve.tensor_tensor(row_oh[:, :, k, :], over(io_one[:, 0:CAP], NT), wide(rw[:, k, :], CAP), ALU.is_equal))
                chain.link(dve.tensor_tensor(col_oh[:, :, k, 0:NCOL], over(io128[:, 0:NCOL], NT), wide(cl[:, k, :], NCOL),
                                             ALU.is_equal))
                chain.link(dve.tensor_tensor(col_oh[:, :, k, NCOL:2 * NCOL], col_oh[:, :, k, 0:NCOL], wide(gt[:, k, :], NCOL),
                                             ALU.mult))
                dve.tensor_tensor(col_oh[:, :, k, 0:NCOL], col_oh[:, :, k, 0:NCOL], wide(tok[:, :], NCOL),
                                  ALU.mult).then_inc(s_ohr, 1)
            weight_whole(2, 0)
            dve.wait_ge(s_tbp, 1)
            chain.link(dve.tensor_scalar(vld[:, :], bank[0:CAP, 5, 0:NCOL], 0.0, None, ALU.is_lt))
            chain.link(dve.tensor_scalar(tabf[:, :], bank[0:CAP, 5, 0:NCOL], prow[0:CAP, :], None, ALU.add))
            chain.link(dve.scalar_tensor_tensor(out=tabf[:, :], in0=vld[:, :], scalar=nprow[0:CAP, :], in1=tabf[:, :],
                                                op0=ALU.mult, op1=ALU.add))
            chain.link(dve.tensor_copy(gtab[:, :], bank[0:CAP, 5, NCOL:2 * NCOL]))
            chain.link(dve.tensor_copy(tab[:, :], tabf[:, :]))
            for b in range(2):
                dve.tensor_copy(gidx[b][:, :], tab[:, b:b + 1]).then_inc(s_ix, 1)
            def name_gather(b, i):
                dve.wait_ge(s_gl[i], 16 * (b // 2) if type(b) is int else 8 * (b - i))
                dve.tensor_copy(gidx[i][:, :], tab[:, bass.ds(b, 1)]).then_inc(s_ix, 1)

            def name_scatter(b, i):
                if not (type(b) is int and b < 2):
                    dve.wait_ge(s_sc, 16 * b - 16)
                    dve.wait_ge(s_ya, b - 1)
                dve.tensor_copy(sidx[i][:, :], tab[:, bass.ds(b, 1)]).then_inc(s_sx2, 1)
                dve.tensor_copy(gcol[i][:, :], gtab[:, bass.ds(b, 1)]).then_inc(s_sx, 1)

            def block_lo(b, i):
                dve.wait_ge(s_xe, b + 1)
                dve.tensor_tensor(xel[i][:, :, :], xT_ps[:, :, 0:CAP], xeh[i][:, :, :].bitcast(F32),
                                  ALU.subtract).then_inc(s_xc, 1)

            def hidden(b):
                dve.wait_ge(s_up, b + 1)
                dve.wait_ge(s_si, b + 1)
                since(dve, s_hT, b)
                dve.tensor_tensor(hid[:, :], up_ps, sgl[:, :], ALU.mult).then_inc(s_h, 1)

            def hidden_lo(b):
                dve.wait_ge(s_hh, b + 1)
                dve.tensor_tensor(hT_lo[:, :, :], hT_ps, hT_hi[:, :, :].bitcast(F32), ALU.subtract).then_inc(s_hl, 1)

            def right_half(b, i):
                dve.wait_ge(s_dp, 2 * b + 2)
                dve.wait_ge(s_sx, b + 1)
                dve.tensor_scalar(yo[i][:, 512:D], bank[0:CAP, 7, :], gcol[i][:, 0:1], None, ALU.mult).then_inc(s_yd, 1)

            def first_dve():
                name_gather(2, 0)
                block_lo(0, 0)
                block_lo(1, 1)
                chain.link(dve.tensor_copy(ovm[0:1, OVB:OVB + 1], ovend[0:1, NE - 1:NE]))
                ends_ = ovend[0:1, :].rearrange("p (x e) -> p x e", x=1).to_broadcast([1, OVB, NE])
                blocks_ = io128[0:1, 0:OVB].rearrange("p (o x) -> p o x", x=1).to_broadcast([1, OVB, NE])
                chain.link(dve.tensor_tensor(past[:, :, :], ends_, blocks_, ALU.is_le))
                chain.link(dve.reduce_sum(ovm[0:1, 0:OVB], past[:, :, :], axis=AXX))
                chain.link(dve.tensor_scalar(ovm[0:1, 0:OVB], ovm[0:1, 0:OVB], float(NE - 1), None, ALU.min))
                dve.tensor_copy(ovmi[0:1, 0:OVB + 1], ovm[0:1, 0:OVB + 1]).then_inc(s_tab, 1)
                weight_whole(0, 1)

            def block_dve(i, b):
                hidden(b)
                hidden_lo(b)
                name_gather(b + 3, 1 - i)
                name_scatter(b, i)
                weight_whole(1, b + 1)
                if not (type(b) is int and b == NE - 2):
                    weight_whole(0, b + 2)
                right_half(b, i)
                block_lo(b + 2, i)
                weight_whole(2, b + 1)

            def last_dve(b):
                if b == NE - 2:
                    block_dve(0, b)
                else:
                    hidden(b)
                    hidden_lo(b)
                    name_gather(b + 3, 0)
                    name_scatter(b, 1)
                    right_half(b, 1)
                    block_lo(b + 2, 1)

            def further_dve(i, b):
                for j in range(3):
                    weight_whole(j, b)
                hidden(b)
                hidden_lo(b)
                name_gather(b + 3, 1 - i)
                name_scatter(b, i)
                right_half(b, i)
                block_lo(b + 2, i)

            blocks(dve, first_dve, block_dve, last_dve, further_dve)

        @block.tensor
        def _(pe):
            def transpose_x(t):
                r = ROWS[t]
                pe.wait_ge(s_xs, t + 1)
                if t == 0:
                    pe.wait_ge(s_ident, 1)
                else:
                    pe.wait_ge(s_xh, t)
                    pe.wait_ge(s_xl, t)
                for k in range(KT):
                    last = pe.transpose(xT_ps[:, k, 0:r], xt[t % 3][0:r, k * P:(k + 1) * P], ident[0:r, 0:r])
                last.then_inc(s_xT, 1)

            def freed(q):
                if q < NQK:
                    pe.wait_ge(s_kn, q + 1)
                elif q < NQK + NUS:
                    pe.wait_ge(s_uc, u_copies(q - NQK))
                else:
                    pe.wait_ge(s_v, q - NUS - NQK + 1)

            def project(s):
                kind, half, t = steps[s]
                r, n = ROWS[t], order.index((kind, half))
                if kind == "k":
                    pe.wait_ge(s_xl, t + 1)
                if t == 0:
                    pe.wait_ge(s_whi, n + 1)
                    pe.wait_ge(s_wlo, n + 1)
                if s >= 4:
                    freed(turn(s) - 4)
                for k in range(KT):
                    for j, (a, b) in enumerate(((xh, w_hi), (xh, w_lo), (xl, w_hi))):
                        last = pe.matmul(proj_ps(s)[0:r, :], a[:, k, row0(t):row0(t) + r], b[n % 2][:, k, :],
                                         start=(k == 0 and j == 0), stop=(k == KT - 1 and j == 2))
                last.then_inc(s_pr, 1)

            def transpose_heads(s):
                r = ROWS[steps[s][2]]
                pe.wait_ge(s_kn, s + 1)
                if s >= 2:
                    pe.wait_ge(s_ke, s - 1)
                for c in range(2):
                    last = pe.transpose(head_ps(s)[:, c, 0:r], kn[s % NKN][0:r, c * P:(c + 1) * P], ident[0:r, 0:r])
                last.then_inc(s_kt, 1)

            transpose_x(0)
            transpose_x(1)
            for s in range(NQK + 3):
                if s < NQK:
                    project(s)
                    if s >= 1 and steps[s - 1][0:2] == ("k", 0) and steps[s - 1][2] + 2 < NT:
                        transpose_x(steps[s - 1][2] + 2)
                if 3 <= s < NQK + 3:
                    transpose_heads(s - 3)

            def transpose_history():
                pe.wait_ge(s_hld, 16)
                pe.wait_ge(s_ke, NQK)
                n = DB * HIST
                for g in range(NG):
                    last = pe.transpose(bank[:, 6, g * n:(g + 1) * n], hist[0:n, g * P:(g + 1) * P], ident[0:n, 0:n])
                last.then_inc(s_ht, 1)

            for i, (g, piece) in enumerate(usteps):
                s, n = NQK + i, 4 + g // 2
                if i == 2:
                    transpose_history()
                lo, cols = UPIECES[piece]
                if i == 0 or i == NUS // 2:
                    pe.wait_ge(s_whi, n + 1)
                    pe.wait_ge(s_wlo, n + 1)
                freed(s - 4)
                c = (g % 2) * P
                for k in range(KT):
                    for j, (a, b) in enumerate(((w_hi, xh), (w_hi, xl), (w_lo, xh))):
                        last = pe.matmul(wide_ps(s)[:, 0:cols], a[n % 2][:, k, c:c + P], b[:, k, lo:lo + cols],
                                         start=(k == 0 and j == 0), stop=(k == KT - 1 and j == 2))
                last.then_inc(s_pr, 1)
            pe.wait_ge(s_uc, u_copies(NUS - 1))
            for g in range(NG):
                pe.transpose(bank[0:TAILP, 6, g * P:(g + 1) * P], u_ext[:, g, TP:16 + TP], ident[:, :])
            for g in range(NG):
                last = pe.transpose(bank[0:TS, 7, g * P:(g + 1) * P], us_cols[:, g, :], ident[:, :])
            last.then_inc(s_ut, 1)
            for s in range(NQK, NS):
                project(s)
            def pooling_products():
                pe.wait_ge(s_cst2, 16 * NCONST)
                for i, (g, piece) in enumerate(usteps):
                    lo, cols = PIECES[piece]
                    pe.wait_ge(s_d, g + 1)
                    if i >= 4:
                        pe.wait_ge(s_pl, i - 3)
                    d = u_ext[:, g, 16 + lo:16 + lo + cols] if piece < 2 else d_tail[:, g, :]
                    pe.matmul(pool_ps(i)[:, 0:cols], wp_sb[:, g, :], d, start=True, stop=True).then_inc(s_pm, 1)
                pe.wait_ge(s_pl, NUS)

            def scores(u):
                kind, w = units[u][0], width(u)
                if u == 1:
                    pe.wait_ge(s_v, NS - NQK)
                    pe.wait_ge(s_ur, 2)
                if u >= 2:
                    pe.wait_ge(s_sg, u if kind == "tail" else u - 1)
                z = z_ps(u)
                if kind == "full":
                    _, t, h = units[u]
                    rows = slice(64 * (h % 2), 64 * (h % 2) + 64)
                    for lo in range(0, w, 512):
                        n = min(512, w - lo)
                        last = pe.matmul(z[:, lo:lo + n], qT[rows, h // 2, row0(t):row0(t) + P],
                                         kT[rows, h // 2, lo:lo + n], start=True, stop=True)
                elif kind == "tail":
                    for j in range(4):
                        h = 4 * units[u][1] + j
                        rows = slice(64 * (h % 2), 64 * (h % 2) + 64)
                        for lo in range(0, w, 512):
                            n = min(512, w - lo)
                            last = pe.matmul(z[32 * j:32 * j + 32, lo:lo + n],
                                             qT[rows, h // 2, row0(LAST):row0(LAST) + TAIL_Q],
                                             kT[rows, h // 2, lo:lo + n], start=True, stop=True)
                else:
                    g = units[u][1]
                    if g == 0:
                        pe.wait_ge(s_qz, 1)
                    for j in range(SQ):
                        b = SQ * g + j
                        pe.wait_ge(s_kld[b % 2], 16 * NPG * (b // 2 + 1))

                        def past_scores(hp):
                            pe.wait_ge(s_te, key_group(b, hp) + 1)
                            pe.matmul(z[32 * j:32 * j + 32, 0:PAST], qz[:, hp, b, :], kTs[:, hp, :],
                                      start=(hp == 0), stop=(hp == HP - 1)).then_inc(s_kTs, 1)

                        for hp in range(HP):
                            past_keys(b, hp)
                            if hp >= 2:
                                past_scores(hp - 2)
                        for hp in range(HP - 2, HP):
                            past_scores(hp)
                    for hp in range(HP):
                        last = pe.matmul(z[0:32 * SQ, PAST:NKS], qz[:, hp, SQ * g:SQ * g + SQ, :].rearrange("p b e -> p (b e)"),
                                         kT[:, hp, row0(LAST):T], start=(hp == 0), stop=(hp == HP - 1))
                last.then_inc(s_z, 1)

            def past_keys(b, hp):
                n = key_group(b, hp)
                pe.wait_ge(s_te, n - 1)
                for j in range(NPG):
                    last = pe.transpose(t_ps(n)[:, j, :], pgk[b % 2][:, j, hp * P:(hp + 1) * P], ident[:, :])
                last.then_inc(s_t, 1)

            def transpose_weights(u):
                pe.wait_ge(s_am, u + 1)
                lo, rows = NK - width(u), height(u)
                for j, group in enumerate(groups(u)):
                    n = first_group(u) + j
                    if n >= 2:
                        pe.wait_ge(s_te, n - 1)
                    for k, (c, keys) in enumerate(group):
                        last = pe.transpose(t_ps(n)[0:keys, k, 0:rows], am[u % 2][0:rows, lo + P * c:lo + P * c + keys],
                                            ident[0:rows, 0:rows])
                    last.then_inc(s_t, 1)

            def sum_values(u):
                kind = units[u][0]
                i, _ = out_of(u)
                pe.wait_ge(s_te, first_group(u) + len(groups(u)))
                if freed_by[outs[i]] is not None and (kind == "smp" or units[u][-1] == 0):
                    pe.wait_ge(s_ol, outs.index(freed_by[outs[i]]) + 1)
                ch = chunks(u)
                if kind == "full":
                    h = units[u][2]
                    for c, keys in ch:
                        last = pe.matmul(o_ps(i)[:, h * HD:(h + 1) * HD], aT[u % 2][0:keys, c, :],
                                         vv[0:keys, c, h * HD:(h + 1) * HD], start=(c == 0), stop=(c == ch[-1][0]))
                    last.then_inc(s_av, 1)
                elif kind == "tail":
                    cols = slice(4 * HD * units[u][1], 4 * HD * (units[u][1] + 1))
                    for c, keys in ch:
                        last = pe.matmul(o_ps(i)[:, cols], aT[u % 2][0:keys, c, :], vv[0:keys, c, cols],
                                         start=(c == 0), stop=(c == ch[-1][0]))
                    last.then_inc(s_av, 1)
                else:
                    g = units[u][1]
                    c, keys = ch[-1]
                    pe.matmul(o_ps(i)[0:32 * SQ, :], aT[u % 2][0:keys, c, 0:32 * SQ], vv[0:keys, LAST, :],
                              start=True, stop=False)
                    for j in range(SQ):
                        b = SQ * g + j
                        pe.wait_ge(s_vld[b % 2], 16 * NPG * (b // 2 + 1))
                        for c in range(NPG):
                            last = pe.matmul(o_ps(i)[32 * j:32 * j + 32, :], aT[u % 2][:, c, 32 * j:32 * j + 32],
                                             pgv[b % 2][:, c, :], start=False, stop=(c == NPG - 1))
                        last.then_inc(s_av, 1)

            def transpose_o(u):
                i, ends = out_of(u)
                if ends:
                    r, step = out_rows(i), P if tile_of(i) is not None else P - 2 * DS
                    pe.wait_ge(s_os, i + 1)
                    for c in range(HP):
                        last = pe.transpose(o_ps(i)[:, c * step:c * step + r], o_sb[0:r, c * P:(c + 1) * P],
                                            ident[0:r, 0:r])
                    last.then_inc(s_oT, 1)

            def out_product(s):
                n, t = wsteps[s]
                r = ROWS[t]
                if s == 0:
                    pe.wait_ge(s_sg, NU)
                    pe.wait_ge(s_ol, NOUT - 1)
                elif s == LAST:
                    pe.wait_ge(s_ol, NOUT)
                if wsteps.index((n, 0)) == s:
                    pe.wait_ge(s_whi, 8 + n + 1)
                    pe.wait_ge(s_wlo, 8 + n + 1)
                if s >= 4:
                    pe.wait_ge(s_xm, s - 3)
                for k in range(KT):
                    for j, (a, b) in enumerate(((xh, w_hi), (xh, w_lo), (xl, w_hi))):
                        last = pe.matmul(out_ps(s)[0:r, :], a[:, k, row0(t):row0(t) + r], b[n % 2][:, k, :],
                                         start=(k == 0 and j == 0), stop=(k == KT - 1 and j == 2))
                last.then_inc(s_wo, 1)

            for i in range(NU + 5):
                if i == 2:
                    pooling_products()
                if i < NU:
                    scores(i)
                if 2 <= i < NU + 2:
                    transpose_weights(i - 2)
                if 5 <= i < NU + 5:
                    transpose_o(i - 5)
                if 3 <= i < NU + 3:
                    sum_values(i - 3)
                if i == NU + 3:
                    for s in range(2):
                        out_product(s)

            pe.wait_ge(s_wr, 48)

            def logits(t):
                r = ROWS[t]
                pe.wait_ge(s_n2c, t + 1)
                if t >= 2:
                    pe.wait_ge(s_lg, t - 1)
                for k in range(KT):
                    last = pe.matmul(logit_ps(t)[0:r, :], nT[t % 2][:, k, 0:r], w_r[:, k, :],
                                     start=(k == 0), stop=(k == KT - 1))
                last.then_inc(s_lgp, 1)

            def transpose_norm(t):
                r = ROWS[t]
                pe.wait_ge(s_n2, t + 1)
                if t >= 1:
                    pe.wait_ge(s_n2c, t)
                for k in range(KT):
                    last = pe.transpose(norm_ps(t)[:, k, 0:r], xg[t % 2][0:r, k * P:(k + 1) * P], ident[0:r, 0:r])
                last.then_inc(s_n2T, 1)

            def follow(t):
                if 0 <= t - 2 < NT:
                    transpose_norm(t - 2)
                if 0 <= t - 3 < NT:
                    logits(t - 3)

            for s in range(2, len(wsteps)):
                out_product(s)
                if wsteps[s][0] == 3:
                    follow(wsteps[s][1])
            for t in range(NT, NT + 3):
                follow(t)
            pe.wait_ge(s_eb, 1)
            marks = eb[:, :, :].rearrange("p t e -> p (t e)")
            pe.matmul(bank[:, 6, 0:NT * NE], before[:, :], marks, start=True, stop=True)
            pe.matmul(bank[:, 7, 0:NT * NE], ones[:, :], marks, start=True, stop=True).then_inc(s_rkp, 1)
            for k in range(2):
                pe.wait_ge(s_ohr, k + 1)
                for t in range(NT):
                    last = pe.matmul(bank[0:CAP, 5, 0:2 * NCOL], row_oh[:, t, k, :], col_oh[:, t, k, :],
                                     start=(t == 0 and k == 0), stop=(t == LAST and k == 1))
            last.then_inc(s_tbp, 1)

            def transpose_block(b, i, loaded):
                pe.wait_ge(s_gl[i], loaded)
                if not (type(b) is int and b == 0):
                    pe.wait_ge(s_xc, b)
                for k in range(KT):
                    last = pe.transpose(xT_ps[:, k, 0:CAP], xg[i][0:CAP, k * P:(k + 1) * P], ident[0:CAP, 0:CAP])
                last.then_inc(s_xt, 1)

            def turns(b, i):
                return 16 * (b // 2 + 1) if type(b) is int else 8 * (b - i) + 16

            def hidden_product(b, i, j, ks):
                ps, done = ((gate_ps(i), s_gp), (up_ps, s_up))[j]
                if ks[0] == 0:
                    pe.wait_ge(s_xc, b + 1)
                    pe.wait_ge(s_el[j], 2 * b + 2)
                    since(pe, *((s_si, b - 1), (s_h, b))[j])
                for k in ks:
                    for n, (x, w) in enumerate(((xeh, e_hi), (xeh, e_lo), (xel, e_hi))):
                        last = pe.matmul(ps, x[i][:, k, :], w[j][:, k, :], start=(k == 0 and n == 0),
                                         stop=(k == KT - 1 and n == 2))
                if ks[-1] == KT - 1:
                    last.then_inc(done, 1)

            def transpose_hidden(b):
                pe.wait_ge(s_h, b + 1)
                since(pe, s_hl, b)
                for ft in range(FT):
                    last = pe.transpose(hT_ps[:, ft, :], hid[:, ft * P:(ft + 1) * P], ident[0:CAP, 0:CAP])
                last.then_inc(s_hT, 1)

            def down_product(b):
                pe.wait_ge(s_hl, b + 1)
                pe.wait_ge(s_el[2], 2 * b + 2)
                for half, (m, done) in enumerate(((6, s_ya), (7, s_yd))):
                    since(pe, done, b)
                    for ft in range(FT):
                        for n, (x, w) in enumerate(((hT_hi, e_hi), (hT_hi, e_lo), (hT_lo, e_hi))):
                            last = pe.matmul(bank[0:CAP, m, :], x[:, ft, :], w[2][:, ft, 512 * half:512 * half + 512],
                                             start=(ft == 0 and n == 0), stop=(ft == FT - 1 and n == 2))
                    last.then_inc(s_dp, 1)

            def first_pe():
                for b in range(2):
                    transpose_block(b, b, 16)
                for j in range(2):
                    hidden_product(0, 0, j, range(KT))

            def block_pe(i, b):
                hidden_product(b + 1, 1 - i, 0, range(3))
                transpose_hidden(b)
                hidden_product(b + 1, 1 - i, 0, range(3, KT))
                down_product(b)
                transpose_block(b + 2, i, turns(b, i) + 16)
                hidden_product(b + 1, 1 - i, 1, range(KT))

            def last_pe(b):
                if b == NE - 2:
                    block_pe(0, b)
                else:
                    transpose_hidden(b)
                    down_product(b)
                    transpose_block(b + 2, 1, turns(b, 1) + 16)

            def further_pe(i, b):
                for j in range(2):
                    hidden_product(b, i, j, range(KT))
                transpose_hidden(b)
                down_product(b)
                transpose_block(b + 2, i, turns(b, i) + 16)

            blocks(pe, first_pe, block_pe, last_pe, further_pe)


_OUTS = {"y_all": (NY, D), "k_all": (T, AW), "v_all": (T, AW), "pool_p": (HIST, PW), "pool_s": (DB, HIST, PW)}
_LAYERED = ("cache_k", "cache_v", "state_pool", "w_in", "w_pool", "w_out", "w_group", "w_expert", "w_gate", "w_up",
            "w_down")


def kernel(**inputs):
    import numpy as np
    import concourse.bacc as bacc
    from concourse.bass_utils import run_bass_kernel_spmd

    nc = bacc.Bacc("TRN2", target_bir_lowering=False, num_devices=1)
    arrays, args = {}, {}
    for name, value in inputs.items():
        a = np.ascontiguousarray(value)
        arrays[f"in_{name}"] = a
        ap = nc.dram_tensor(f"in_{name}", a.shape, mybir.dt.from_np(a.dtype), kind="ExternalInput").ap()
        args[name] = ap[0] if name in _LAYERED else ap
    for name, shape in _OUTS.items():
        args[name] = nc.dram_tensor(f"out_{name}", shape, F32, kind="ExternalOutput").ap()
    hybrid_step(nc, **args)
    r = run_bass_kernel_spmd(nc, [arrays], core_ids=[0]).results[0]
    y, k, v = r["out_y_all"], r["out_k_all"], r["out_v_all"]
    return (y[META:TP].reshape(1, SEQ, D), y[TP:T].reshape(DB, DS, D),
            k[:TP].reshape(1, 1, TP, H, HD), v[:TP].reshape(1, 1, TP, H, HD), r["out_pool_p"].reshape(1, 1, HIST, PW),
            k[TP:].reshape(1, DB, DS, H, HD), v[TP:].reshape(1, DB, DS, H, HD),
            r["out_pool_s"].reshape(1, DB, HIST, PW))
```
